# Optimizing a Trainium2 kernel written in Bass

```python
import jax
import jax.numpy as jnp
from jax import lax
import numpy as np

D_MODEL = 1024
BATCH = 1
SEQ = 512
DEPTH = 1
DEC_BATCH = 8
DEC_SEQ = 4
PAST_LEN = 2048
PAGE_SIZE = 128

A_HEADS = 8
A_HEAD_DIM = 64
A_WIDTH = A_HEADS * A_HEAD_DIM
A_DECAY_LORA = 64
A_ICLR_LORA = 64
A_GATE_LORA = 128
A_PROJ = 3 * A_WIDTH + A_DECAY_LORA + A_ICLR_LORA + A_GATE_LORA
A_LNX_EPS = 64e-5

B_GROUPS = ((128, 1), (512, 4), (2048, 16))
B_HEADS_PER_GROUP = 4
B_HEAD_DIM = 64
B_HEADS = B_HEADS_PER_GROUP * len(B_GROUPS)
B_WIDTH = B_HEADS * B_HEAD_DIM
B_PROJ = 3 * B_WIDTH
B_OUT = B_HEADS_PER_GROUP * B_HEAD_DIM
ROPE_THETA = 500000.0
ROPE_DIM = B_HEAD_DIM // 4

N_BRANCH = 2
IN_PROJ = A_PROJ + B_PROJ + N_BRANCH * D_MODEL

N_MEM = 256
MEM_HEADS = 4
MEM_HEAD_DIM = 128
MEM_WIDTH = MEM_HEADS * MEM_HEAD_DIM

N_GROUPS = 4
EXPERTS_PER_GROUP = 8
N_EXPERTS = N_GROUPS * EXPERTS_PER_GROUP
TOP_K = 2
EXPERT_FF = 512
MOE_BLOCK = 128

RMS_EPS = 1e-6

kernel_name = 'hybrid_rwkv7_dilated_swa_hmoe_step'

def rmsnorm(x, g):
    xf = x.astype(jnp.float32)
    xf = xf * lax.rsqrt(jnp.mean(xf * xf, axis=-1, keepdims=True) + RMS_EPS)
    return (xf * g.astype(jnp.float32)).astype(x.dtype)

def rope_partial(x, pos):
    half = ROPE_DIM // 2
    inv_freq = ROPE_THETA ** (-jnp.arange(half, dtype=jnp.float32) * 2.0 / ROPE_DIM)
    ang = pos.astype(jnp.float32)[:, None] * inv_freq[None, :]
    cos = jnp.cos(ang)[None, :, None, :]
    sin = jnp.sin(ang)[None, :, None, :]
    xr = x[..., :ROPE_DIM].astype(jnp.float32)
    x1, x2 = xr[..., :half], xr[..., half:]
    rot = jnp.concatenate([x1 * cos - x2 * sin, x2 * cos + x1 * sin], axis=-1)
    return jnp.concatenate([rot.astype(x.dtype), x[..., ROPE_DIM:]], axis=-1)

def rwkv7_mix(u, shift0, s0, mu, w0, w2, a0, a2, g2, k_k, k_a, r_k, lnx_g, lnx_b):
    f32 = jnp.float32
    bsz, t_len, _ = u.shape
    u_prev = jnp.concatenate([shift0[:, None, :].astype(u.dtype), u[:, :-1]], axis=1)
    um = u + (u_prev - u) * mu
    o1, o2, o3 = A_WIDTH, 2 * A_WIDTH, 3 * A_WIDTH
    o4 = o3 + A_DECAY_LORA
    o5 = o4 + A_ICLR_LORA
    r, k, v = um[..., :o1], um[..., o1:o2], um[..., o2:o3]
    xw, xa, xg = um[..., o3:o4], um[..., o4:o5], um[..., o5:]
    w = -jax.nn.softplus(-(w0 + jnp.tanh(xw) @ w2)) - 0.5
    decay = jnp.exp(-jnp.exp(w.astype(f32)))
    a = jax.nn.sigmoid(a0 + xa @ a2)
    g = jax.nn.sigmoid(xg) @ g2

    def heads(t):
        return t.astype(f32).reshape(bsz, t_len, A_HEADS, A_HEAD_DIM)

    kk = heads(k * k_k)
    kk = kk / jnp.maximum(jnp.sqrt(jnp.sum(kk * kk, axis=-1, keepdims=True)), 1e-12)
    k = k * (1 + (a - 1) * k_a)
    r_h, k_h, v_h, a_h, d_h = heads(r), heads(k), heads(v), heads(a), heads(decay)
    b_h = kk * a_h

    def step(state, inp):
        r_t, d_t, k_t, v_t, kk_t, b_t = inp
        sa = jnp.einsum('bhvk,bhk->bhv', state, -kk_t)
        state = state * d_t[:, :, None, :] + sa[..., None] * b_t[:, :, None, :] + v_t[..., None] * k_t[:, :, None, :]
        return state, jnp.einsum('bhvk,bhk->bhv', state, r_t)

    xs = tuple(jnp.swapaxes(t, 0, 1) for t in (r_h, d_h, k_h, v_h, kk, b_h))
    s_fin, ys = lax.scan(step, s0.astype(f32), xs)
    y = jnp.swapaxes(ys, 0, 1)
    mean = jnp.mean(y, axis=-1, keepdims=True)
    var = jnp.mean(jnp.square(y - mean), axis=-1, keepdims=True)
    y = (y - mean) * lax.rsqrt(var + A_LNX_EPS)
    y = y.reshape(bsz, t_len, A_WIDTH) * lnx_g.astype(f32) + lnx_b.astype(f32)
    bonus = jnp.sum(r_h * k_h * r_k.astype(f32), axis=-1, keepdims=True) * v_h
    out = (y + bonus.reshape(bsz, t_len, A_WIDTH)) * g.astype(f32)
    return out.astype(u.dtype), s_fin, u[:, -1]

def masked_softmax_stats(s, valid):
    s = jnp.where(valid, s, -jnp.inf)
    m = jnp.max(s, axis=-1, keepdims=True)
    p = jnp.exp(s - m)
    den = jnp.sum(p, axis=-1, keepdims=True)
    return p / den, (m + jnp.log(den))[..., 0]

def dilated_group_prompt(q, k, v, window, dilation):
    bsz, s_len, nh, dh = q.shape
    nk = window // dilation
    n_cls = s_len // dilation
    nb = -(-n_cls // nk)
    pad = nb * nk - n_cls

    def to_blocks(t):
        t = t.reshape(bsz, n_cls, dilation, nh, dh).transpose(0, 2, 1, 3, 4)
        t = jnp.pad(t, ((0, 0), (0, 0), (0, pad), (0, 0), (0, 0)))
        return t.reshape(bsz, dilation, nb, nk, nh, dh).astype(jnp.float32)

    def band(t):
        prev = jnp.pad(t[:, :, :-1], ((0, 0), (0, 0), (1, 0), (0, 0), (0, 0), (0, 0)))
        return jnp.concatenate([prev, t], axis=3)

    qb = to_blocks(q)
    kb = band(to_blocks(k))
    vb = band(to_blocks(v))
    s = jnp.einsum('brnqhd,brnkhd->brnhqk', qb, kb) * (dh ** -0.5)
    qi = jnp.arange(nk)[:, None] + nk
    ki = jnp.arange(2 * nk)[None, :]
    dist = qi - ki
    first = (jnp.arange(nb) == 0)[:, None, None]
    valid = (dist >= 0) & (dist <= nk) & ~(first & (ki < nk))
    p, lse = masked_softmax_stats(s, valid[:, None])
    o = jnp.einsum('brnhqk,brnkhd->brnqhd', p, vb)
    o = o.reshape(bsz, dilation, nb * nk, nh, dh)[:, :, :n_cls].transpose(0, 2, 1, 3, 4).reshape(bsz, s_len, nh, dh)
    lse = jnp.swapaxes(lse, 3, 4).reshape(bsz, dilation, nb * nk, nh)[:, :, :n_cls]
    lse = lse.transpose(0, 2, 1, 3).reshape(bsz, s_len, nh)
    return o, lse

def dilated_group_sample(q, k_new, v_new, buf, window, dilation):
    t_len = q.shape[1]
    buf_len = buf.shape[2]
    nk = window // dilation
    k_all = jnp.concatenate([buf[:, 0].astype(k_new.dtype), k_new], axis=1)
    v_all = jnp.concatenate([buf[:, 1].astype(v_new.dtype), v_new], axis=1)
    idx = buf_len + jnp.arange(t_len)[:, None] - dilation * jnp.arange(nk + 1)[None, :]
    valid = idx >= 0
    idx = jnp.maximum(idx, 0)
    kg = jnp.take(k_all, idx, axis=1).astype(jnp.float32)
    vg = jnp.take(v_all, idx, axis=1).astype(jnp.float32)
    s = jnp.einsum('bthd,btjhd->bhtj', q.astype(jnp.float32), kg) * (q.shape[-1] ** -0.5)
    p, lse = masked_softmax_stats(s, valid)
    o = jnp.einsum('bhtj,btjhd->bthd', p, vg)
    new_buf = jnp.stack([k_all[:, t_len:], v_all[:, t_len:]], axis=1)
    return o, jnp.swapaxes(lse, 1, 2), new_buf

def mixing_sublayer(x, pos, s0, shift0, swa_bufs, p):
    bsz, t_len, _ = x.shape
    xn = rmsnorm(x, p['norm_mix_g'])
    u = xn @ p['w_in']
    u_a = u[..., :A_PROJ]
    u_b = u[..., A_PROJ:A_PROJ + B_PROJ].reshape(bsz, t_len, 3, B_HEADS, B_HEAD_DIM)
    gates = jax.nn.sigmoid(u[..., A_PROJ + B_PROJ:] + p['b_gate']).reshape(bsz, t_len, N_BRANCH, D_MODEL)
    y_a, s_fin, shift_new = rwkv7_mix(u_a, shift0, s0, p['rwkv_mu'], p['rwkv_w0'], p['rwkv_w2'], p['rwkv_a0'],
                                      p['rwkv_a2'], p['rwkv_g2'], p['rwkv_k_k'], p['rwkv_k_a'], p['rwkv_r_k'],
                                      p['rwkv_lnx_g'], p['rwkv_lnx_b'])
    q = rope_partial(u_b[:, :, 0], pos)
    k = rope_partial(u_b[:, :, 1], pos)
    v = u_b[:, :, 2]
    outs, lses, bufs = [], [], []
    for gi, (window, dilation) in enumerate(B_GROUPS):
        hs = slice(gi * B_HEADS_PER_GROUP, (gi + 1) * B_HEADS_PER_GROUP)
        if swa_bufs is None:
            o, lse = dilated_group_prompt(q[:, :, hs], k[:, :, hs], v[:, :, hs], window, dilation)
            keep = min(window, t_len)
            buf = jnp.stack([k[:, t_len - keep:, hs], v[:, t_len - keep:, hs]], axis=1)
        else:
            o, lse, buf = dilated_group_sample(q[:, :, hs], k[:, :, hs], v[:, :, hs], swa_bufs[gi], window, dilation)
        outs.append(o)
        lses.append(lse)
        bufs.append(buf)
    w_grp = jax.nn.softmax(jnp.stack(lses, axis=0), axis=0)
    y_b = jnp.einsum('gbth,gbthd->bthd', w_grp, jnp.stack(outs, axis=0)).astype(x.dtype).reshape(bsz, t_len, B_OUT)
    merged = gates[:, :, 0] * (y_a @ p['w_branch_a']) + gates[:, :, 1] * (y_b @ p['w_branch_b'])
    return x + merged @ p['w_out'], s_fin, shift_new, bufs

def memory_kv(mem, g, w_mem_kv):
    bsz = mem.shape[0]
    kv = rmsnorm(mem, g) @ w_mem_kv
    return kv.reshape(bsz, N_MEM, 2, MEM_HEADS, MEM_HEAD_DIM).transpose(0, 2, 1, 3, 4)

def memory_sublayer(x, mem_kv, p):
    bsz, t_len, _ = x.shape
    q = (rmsnorm(x, p['norm_mem_g']) @ p['w_mem_q']).reshape(bsz, t_len, MEM_HEADS, MEM_HEAD_DIM)
    s = jnp.einsum('bthd,bmhd->bhtm', q.astype(jnp.float32), mem_kv[:, 0].astype(jnp.float32)) * (MEM_HEAD_DIM ** -0.5)
    o = jnp.einsum('bhtm,bmhd->bthd', jax.nn.softmax(s, axis=-1), mem_kv[:, 1].astype(jnp.float32))
    return x + o.astype(x.dtype).reshape(bsz, t_len, MEM_WIDTH) @ p['w_mem_out']

def expert_dispatch(xt, expert_id, expert_w, w_gate, w_up, w_down):
    n_tok, dm = xt.shape
    n_rows = n_tok * TOP_K
    n_blocks = (n_rows + N_EXPERTS * (MOE_BLOCK - 1) + MOE_BLOCK - 1) // MOE_BLOCK
    flat_e = expert_id.reshape(-1)
    flat_tok = jnp.repeat(jnp.arange(n_tok, dtype=jnp.int32), TOP_K)
    flat_w = expert_w.reshape(-1).astype(jnp.float32)
    order = jnp.argsort(flat_e)
    sorted_e = flat_e[order]
    counts = jnp.bincount(flat_e, length=N_EXPERTS)
    padded = (counts + MOE_BLOCK - 1) // MOE_BLOCK * MOE_BLOCK
    pad_end = jnp.cumsum(padded)
    pad_start = pad_end - padded
    start = jnp.cumsum(counts) - counts
    dest = pad_start[sorted_e] + jnp.arange(n_rows) - start[sorted_e]
    row_tok = jnp.full((n_blocks * MOE_BLOCK,), n_tok, jnp.int32).at[dest].set(flat_tok[order])
    row_w = jnp.zeros((n_blocks * MOE_BLOCK,), jnp.float32).at[dest].set(flat_w[order])
    block_e = jnp.minimum(jnp.searchsorted(pad_end, jnp.arange(n_blocks) * MOE_BLOCK, side='right'), N_EXPERTS - 1)
    x_pad = jnp.concatenate([xt, jnp.zeros((1, dm), xt.dtype)], axis=0)

    def block_fn(args):
        tok, e = args
        xb = x_pad[tok]
        h = jax.nn.silu(xb @ w_gate[e]) * (xb @ w_up[e])
        return (h @ w_down[e]).astype(jnp.float32)

    yb = lax.map(block_fn, (row_tok.reshape(n_blocks, MOE_BLOCK), block_e))
    y = jnp.zeros((n_tok + 1, dm), jnp.float32).at[row_tok].add(yb.reshape(-1, dm) * row_w[:, None])
    return y[:n_tok].astype(xt.dtype)

def hier_moe_sublayer(x, p):
    bsz, t_len, dm = x.shape
    xn = rmsnorm(x, p['norm_ffn_g']).reshape(bsz * t_len, dm)
    logit_g = (xn @ p['w_router_group'] + p['b_router_group']).astype(jnp.float32)
    grp = jnp.argmax(logit_g, axis=-1)
    w_grp = jnp.take_along_axis(jax.nn.softmax(logit_g, axis=-1), grp[:, None], axis=-1)
    logit_e = (xn @ p['w_router_expert'] + p['b_router_expert']).astype(jnp.float32)
    logit_e = logit_e.reshape(-1, N_GROUPS, EXPERTS_PER_GROUP)
    logit_e = jnp.take_along_axis(logit_e, grp[:, None, None], axis=1)[:, 0]
    top_v, top_i = lax.top_k(logit_e, TOP_K)
    gate = jax.nn.softmax(top_v, axis=-1) * w_grp
    eid = grp[:, None] * EXPERTS_PER_GROUP + top_i
    y = expert_dispatch(xn, eid, gate, p['w_exp_gate'], p['w_exp_up'], p['w_exp_down'])
    return x + y.reshape(bsz, t_len, dm)

def decoder_layer(x, pos, s0, shift0, swa_bufs, mem_kv, p):
    x, s_fin, shift_new, bufs = mixing_sublayer(x, pos, s0, shift0, swa_bufs, p)
    x = memory_sublayer(x, mem_kv, p)
    x = hier_moe_sublayer(x, p)
    return x, s_fin, shift_new, bufs

def setup_inputs(seed: int = 0) -> dict:
    key = jax.random.key(seed)
    ks = iter(jax.random.split(key, 64))
    f32 = jnp.float32

    def nrm(shape, scale=1.0):
        return jax.random.normal(next(ks), shape, f32) * scale

    def gain(n):
        return 1.0 + nrm((n,), 0.05)

    swa = [nrm((DEC_BATCH, 2, min(w, PAST_LEN), B_HEADS_PER_GROUP, B_HEAD_DIM)) for w, _ in B_GROUPS]
    return {
        'x_prompt': nrm((BATCH, SEQ, D_MODEL)),
        'x_sample': nrm((DEC_BATCH, DEC_SEQ, D_MODEL)),
        'state_rwkv': nrm((DEC_BATCH, A_HEADS, A_HEAD_DIM, A_HEAD_DIM), 0.5),
        'state_shift': nrm((DEC_BATCH, A_PROJ)),
        'cache_swa_w128': swa[0],
        'cache_swa_w512': swa[1],
        'cache_swa_w2048': swa[2],
        'cache_mem_kv': nrm((DEC_BATCH, 2, N_MEM, MEM_HEADS, MEM_HEAD_DIM)),
        'mem_prompt': nrm((BATCH, N_MEM, D_MODEL)),
        'norm_mix_g': gain(D_MODEL),
        'w_in': nrm((D_MODEL, IN_PROJ), D_MODEL ** -0.5),
        'b_gate': nrm((N_BRANCH * D_MODEL,), 0.02),
        'rwkv_mu': jax.random.uniform(next(ks), (A_PROJ,), f32),
        'rwkv_w0': jax.random.uniform(next(ks), (A_WIDTH,), f32, -6.0, -1.0),
        'rwkv_w2': nrm((A_DECAY_LORA, A_WIDTH), 0.1),
        'rwkv_a0': nrm((A_WIDTH,), 0.1),
        'rwkv_a2': nrm((A_ICLR_LORA, A_WIDTH), 0.1),
        'rwkv_g2': nrm((A_GATE_LORA, A_WIDTH), A_GATE_LORA ** -0.5),
        'rwkv_k_k': 0.85 + nrm((A_WIDTH,), 0.05),
        'rwkv_k_a': 1.0 + nrm((A_WIDTH,), 0.05),
        'rwkv_r_k': nrm((A_HEADS, A_HEAD_DIM), 0.1),
        'rwkv_lnx_g': gain(A_WIDTH),
        'rwkv_lnx_b': nrm((A_WIDTH,), 0.02),
        'w_branch_a': nrm((A_WIDTH, D_MODEL), A_WIDTH ** -0.5),
        'w_branch_b': nrm((B_OUT, D_MODEL), B_OUT ** -0.5),
        'w_out': nrm((D_MODEL, D_MODEL), D_MODEL ** -0.5),
        'norm_mem_g': gain(D_MODEL),
        'norm_memkv_g': gain(D_MODEL),
        'w_mem_q': nrm((D_MODEL, MEM_WIDTH), D_MODEL ** -0.5),
        'w_mem_kv': nrm((D_MODEL, 2 * MEM_WIDTH), D_MODEL ** -0.5),
        'w_mem_out': nrm((MEM_WIDTH, D_MODEL), MEM_WIDTH ** -0.5),
        'norm_ffn_g': gain(D_MODEL),
        'w_router_group': nrm((D_MODEL, N_GROUPS), D_MODEL ** -0.5),
        'b_router_group': nrm((N_GROUPS,), 0.01),
        'w_router_expert': nrm((D_MODEL, N_EXPERTS), D_MODEL ** -0.5),
        'b_router_expert': nrm((N_EXPERTS,), 0.01),
        'w_exp_gate': nrm((N_EXPERTS, D_MODEL, EXPERT_FF), D_MODEL ** -0.5),
        'w_exp_up': nrm((N_EXPERTS, D_MODEL, EXPERT_FF), D_MODEL ** -0.5),
        'w_exp_down': nrm((N_EXPERTS, EXPERT_FF, D_MODEL), EXPERT_FF ** -0.5),
        'norm_final_g': gain(D_MODEL),
    }

def reference(x_prompt, x_sample, state_rwkv, state_shift, cache_swa_w128, cache_swa_w512, cache_swa_w2048,
              cache_mem_kv, mem_prompt, norm_mix_g, w_in, b_gate, rwkv_mu, rwkv_w0, rwkv_w2, rwkv_a0, rwkv_a2,
              rwkv_g2, rwkv_k_k, rwkv_k_a, rwkv_r_k, rwkv_lnx_g, rwkv_lnx_b, w_branch_a, w_branch_b, w_out,
              norm_mem_g, norm_memkv_g, w_mem_q, w_mem_kv, w_mem_out, norm_ffn_g, w_router_group, b_router_group,
              w_router_expert, b_router_expert, w_exp_gate, w_exp_up, w_exp_down, norm_final_g):
    p = {
        'norm_mix_g': norm_mix_g, 'w_in': w_in, 'b_gate': b_gate,
        'rwkv_mu': rwkv_mu, 'rwkv_w0': rwkv_w0, 'rwkv_w2': rwkv_w2, 'rwkv_a0': rwkv_a0, 'rwkv_a2': rwkv_a2,
        'rwkv_g2': rwkv_g2, 'rwkv_k_k': rwkv_k_k, 'rwkv_k_a': rwkv_k_a, 'rwkv_r_k': rwkv_r_k,
        'rwkv_lnx_g': rwkv_lnx_g, 'rwkv_lnx_b': rwkv_lnx_b,
        'w_branch_a': w_branch_a, 'w_branch_b': w_branch_b, 'w_out': w_out,
        'norm_mem_g': norm_mem_g, 'w_mem_q': w_mem_q, 'w_mem_out': w_mem_out,
        'norm_ffn_g': norm_ffn_g, 'w_router_group': w_router_group, 'b_router_group': b_router_group,
        'w_router_expert': w_router_expert, 'b_router_expert': b_router_expert,
        'w_exp_gate': w_exp_gate, 'w_exp_up': w_exp_up, 'w_exp_down': w_exp_down,
    }
    bsz, s_len, _ = x_prompt.shape
    mem_kv_prompt = memory_kv(mem_prompt, norm_memkv_g, w_mem_kv)
    s0 = jnp.zeros((bsz, A_HEADS, A_HEAD_DIM, A_HEAD_DIM), jnp.float32)
    shift0 = jnp.zeros((bsz, A_PROJ), x_prompt.dtype)
    h_p, p_rwkv, p_shift, p_bufs = decoder_layer(x_prompt, jnp.arange(s_len), s0, shift0, None, mem_kv_prompt, p)
    y_prompt = rmsnorm(h_p, norm_final_g)
    t_len = x_sample.shape[1]
    h_s, s_rwkv, s_shift, s_bufs = decoder_layer(x_sample, PAST_LEN + jnp.arange(t_len), state_rwkv, state_shift,
                                                 (cache_swa_w128, cache_swa_w512, cache_swa_w2048), cache_mem_kv, p)
    y_sample = rmsnorm(h_s, norm_final_g)
    return (y_prompt, y_sample, p_rwkv, p_shift, p_bufs[0], p_bufs[1], p_bufs[2], mem_kv_prompt,
            s_rwkv, s_shift, s_bufs[0], s_bufs[1], s_bufs[2])


_drawn_inputs = setup_inputs


def setup_inputs(seed=0):
    import zlib

    import numpy as np

    out = dict(_drawn_inputs(seed))
    spreads = {}
    factors = {'b_gate': 4.462, 'norm_mem_g': 2.749, 'rwkv_lnx_b': 2.765, 'b_router_expert': 4.262}
    for name, (base, spread) in spreads.items():
        noise = np.random.default_rng([zlib.crc32(name.encode()), seed]).standard_normal(out[name].shape)
        drawn = base * np.exp(spread * noise) if base else spread * noise
        out[name] = jnp.asarray(drawn.astype(out[name].dtype))
    for name, factor in factors.items():
        out[name] = (out[name] * factor).astype(out[name].dtype)
    return out
```

```python
from contextlib import ExitStack

import numpy as np
import concourse.bass as bass
from concourse import mybir

F32 = mybir.dt.float32
I32 = mybir.dt.int32
U32 = mybir.dt.uint32
ALU = mybir.AluOpType
ACT = mybir.ActivationFunctionType
AX = mybir.AxisListType.X

P = 128
D = 1024
KT = D // P
SEQ = 512
NB = 8
NS = 4
TS = NB * NS
T = SEQ + TS
TILES = [(i * P, P) for i in range(SEQ // P)] + [(SEQ, TS)]
NPT = SEQ // P
PAST = 2048
AH, AD = 8, 64
AW = AH * AD
APROJ = 3 * AW + 64 + 64 + 128
AJ = APROJ // P
GROUPS = ((128, 1), (512, 4), (2048, 16))
NG = len(GROUPS)
BW = 4 * NG * 64
BPROJ = 3 * BW
MEM = 256
MH, MD = 4, 128
MW = MH * MD
NE, NGR, EPG = 32, 4, 8
FF = 512
EPS = 1e-6
LNX_EPS = 64e-5
NEG = -1e30
BLK = P
ROWS = 2 * T
MAXBLK = -(-T // BLK)
ALLBLK = NE + ROWS // BLK
NTAB = ALLBLK + 1
LEVELS = (1, 2, 4, 8, 16, 32, 64)


def constants():
    q, k = np.arange(P)[:, None], np.arange(P)[None, :]
    out = {}

    def put(name, a):
        out[name] = np.ascontiguousarray(np.broadcast_to(a, (P, a.shape[-1])), dtype=np.float32)

    put("ident", (q == k) * 1.0)
    put("ones", np.ones((P, P)))
    put("blk", (q // AD == k // AD) * 1.0)
    put("strict", (q < k) * 1.0)
    put("incl", (q <= k) * 1.0)
    for m in LEVELS:
        put(f"low{m}", ((q // (2 * m) == k // (2 * m)) & ((k // m) % 2 == 1) & ((q // m) % 2 == 0)) * 1.0)
    put("low1t", ((q // 2 == k // 2) & (q % 2 == 1) & (k % 2 == 0)) * 1.0)
    put("off0", np.where(k >= q, 0, NEG))
    put("diag0", np.where(k <= q, 0, NEG))
    for g in (1, 2):
        dil = GROUPS[g][1]
        put(f"off{g}", np.where((q - k) % dil == 0, 0, NEG))
        put(f"diag{g}", np.where(((q - k) % dil == 0) & (k <= q), 0, NEG))
    tok = np.arange(P) % TS
    b, t = tok // NS, tok % NS
    nb, nt = np.arange(TS) // NS, np.arange(TS) % NS
    cached = [np.where(k >= t[:, None], 0, NEG), np.zeros((P, P)), np.zeros((P, P))]
    same = b[:, None] == nb[None, :]
    new = [np.where(same & (nt[None, :] <= t[:, None]), 0, NEG)] + [np.where(same & (nt[None, :] == t[:, None]), 0, NEG)] * 2
    put("samp", np.concatenate(cached + new, axis=1))
    put("reset", (np.arange(SEQ) % P != 0)[None, :] * 1.0)
    half = 8
    inv = (np.float32(500000.0) ** (-np.arange(half, dtype=np.float32) * np.float32(2.0) / np.float32(16))).astype(np.float32)
    rope = np.zeros((P, len(TILES), 2 * half), np.float32)
    for i, (t0, n) in enumerate(TILES):
        pos = np.arange(t0, t0 + n) if t0 < SEQ else PAST + np.arange(TS) % NS
        ang = pos.astype(np.float32)[:, None] * inv[None, :]
        rope[:n, i, :half], rope[:n, i, half:] = np.cos(ang), np.sin(ang)
    put("rope", rope.reshape(P, -1))
    put("iota", np.arange(NE)[None, :] * 1.0)
    put("grp", (np.arange(NE) // EPG)[None, :] * 1.0)
    put("eps", np.full((1, 1), EPS))
    put("count", np.arange(NTAB)[None, :] * 1.0)
    put("thr", (BLK * (1 + np.arange(MAXBLK - 1)))[None, :] * 1.0)
    return out


def const_layout():
    at, n = {}, 0
    for name, a in constants().items():
        at[name] = (n, a.shape[1])
        n += a.shape[1]
    return at, n


class Mail:

    def __init__(self, banks, filled, freed):
        self.banks, self.filled, self.freed = banks, filled, freed
        self.put = self.got = 0

    def claim(self, pe):
        if self.put >= len(self.banks):
            pe.wait_ge(self.freed, self.put - len(self.banks) + 1)
        self.put += 1
        return self.banks[(self.put - 1) % len(self.banks)]

    def take(self, eng):
        eng.wait_ge(self.filled, self.got + 1)
        self.got += 1
        return self.banks[(self.got - 1) % len(self.banks)]


class Line:

    def __init__(self, eng, step):
        self.eng, self.step, self.n = eng, step, {}

    def do(self, ins, sem=None):
        key = sem or self.step
        ins.then_inc(key, 1)
        self.n[key.name] = self.n.get(key.name, 0) + 1
        self.eng.wait_ge(key, self.n[key.name])

    def count(self, ins, sem):
        ins.then_inc(sem, 1)
        self.n[sem.name] = self.n.get(sem.name, 0) + 1


def build(nc, a, o, cst):
    with ExitStack() as ctx:
        def sem(name):
            return ctx.enter_context(nc.semaphore(name))

        CL, NC = const_layout()
        cols = (nc.sbuf_usable_end - nc.sbuf_base) // 4 // 16 * 16 - 16
        arena = ctx.enter_context(nc.sbuf_tensor("arena", [P, cols], F32))
        top = [0]

        def at(n):
            top[0] += n
            return top[0] - n

        def view(off, *shape):
            n = int(np.prod(shape))
            v = arena[:, off:off + n]
            if len(shape) == 2:
                v = v.rearrange("p (a b) -> p a b", b=shape[1])
            if len(shape) == 3:
                v = v.rearrange("p (a b c) -> p a b c", b=shape[1], c=shape[2])
            return v

        con = view(at(NC), NC)
        x_res = view(at(5 * D), 5, D)
        x_t = view(at(KT * T), KT, T)
        prm = view(at(64), 64)
        gains = view(at(4 * KT), 4, KT)
        omka = view(at(4), 4)
        lora = view(at(2 * AW), 2, AW)
        wr = view(at(KT * 36), KT, 36)
        yb_t = view(at(2 * T), 2, T)
        stat = view(at(64), 64)
        ring_at = at(2 * 4096)
        ring = [view(ring_at + 4096 * s, KT, 512) for s in range(2)]
        AR = top[0]

        def C(name):
            n, w = CL[name]
            return con[:, n:n + w]

        ident = C("ident")
        MU, W0, A0, KK_, KA, RK, LG, LB, BG = 0, 14, 18, 22, 26, 30, 34, 38, 42
        NPRM = 58

        qkv = view(AR, 5, BPROJ)
        qk_t = view(AR + 5 * BPROJ, 12, T)
        rt = [view(AR + 5 * BPROJ + 12 * T + 192 * n, 24, 8) for n in range(4)]
        s0 = AR + 5 * BPROJ + 12 * T + 768
        s_sb = [view(s0 + 1280 * n, 1280) for n in range(2)]
        p_t = [view(s0 + 2560 + 1280 * n, 10, P) for n in range(2)]
        kvb = [view(s0 + 5120 + 1024 * n, 4, 256) for n in range(3)]
        row_b = view(s0 + 5120 + 3072, P)
        assert s0 + 5120 + 3072 + P <= cols, (s0, cols)
        xs_tmp = [view(s0 + 1024 * n, D) for n in range(2)]
        kt_s = [view(s0 + 1280 + 1024 * n, 8, P) for n in range(2)]
        qblk = view(s0 + 3400, NG * 2, 64)
        st_sb = view(s0 + 3800, NG, P)
        stn_sb = view(s0 + 4200, NG, P)
        ps_sb = view(s0, 480)
        pts = view(s0 + 512, NG, P)
        ptn = view(s0 + 896, NG, P)

        U = AR
        u_p, u_s = view(U, AJ, SEQ), view(U + 7168, AJ, TS)
        UM = AR + 7616
        um_p, um_s = view(UM, AJ, SEQ), view(UM + 7168, AJ, TS)
        SL = UM + 7616
        a_p, kk_p, sg_p, c_p, g_p, bon_p = (view(SL + 2048 * n, 4, SEQ) for n in range(6))
        SM = SL + 6 * 2048
        tmp_p, tm_b, tm_k = (view(U + 2048 * n, 4, SEQ) for n in range(3))
        tm_v = sg_p
        mat_l, mat_t = view(SL + 3 * 2048, 8, P), view(SL + 3 * 2048 + 1024, 8, P)
        mat_tt, mat_lm, mat_w = (view(UM + 4096 + 1024 * n, 8, P) for n in range(3))
        mat_rb, mat_rk, mat_ak = view(U, 8, P), view(U + 1024, 8, P), view(U + 6144, 8, P)
        w_sb, uu_sb = view(SM, 8, 64), view(SM + 512, 8, 64)
        st0, st0m = view(SM + 1024, 4, 64), view(SM + 1280, 4, 64)
        pmid, pend = view(SM + 1536, 4, 4), view(SM + 1552, 4, 4)
        assert SM + 1568 <= cols, (SM, cols)
        R0 = ring_at
        a_s, kk_s, dec_s, g_s, bon_s, tmp_s = (view(R0 + 128 * n, 4, TS) for n in range(6))
        y_s = view(SM, 4, TS)
        rec = view(R0 + 1024, 5, NS * 64)
        rec_v, rec_y, rec_sa = (view(R0 + 2304 + 128 * n, NS, 32) for n in range(3))
        tok_s = view(R0 + 4096, 6, AW)
        rec_s, rec_t = view(R0 + 4096, 32, 64), view(R0 + 6144, 32, 64)
        y_tok = view(R0 + 2752, AW)

        wa, wb = view(U, 4, D), view(U + 4096, 2, D)
        m_t = view(UM, KT, T)
        sg_a, sg_b, mg = (view(SL + 3 * 2048 + 560 * n, T) for n in range(3))
        Z = AR
        mem_x = view(Z, 2, D)
        mem_t = view(Z + 2048, KT, MEM)
        mkv = view(Z + 4096, 2, 2 * MW)
        mk_t = view(Z + 6144, MH, MEM)
        q_t = view(Z + 7168, MH, T)
        o_t = view(Z + 9344, MH, T)
        ms_sb = [view(Z + 11520 + 256 * n, 256) for n in range(2)]
        mp_t = [view(Z + 12032 + 256 * n, 2, P) for n in range(2)]
        mks = [view(Z + 12544 + 1024 * n, 2, MW) for n in range(2)]
        mvs = [view(Z + 14592 + 1024 * n, 2, MW) for n in range(2)]
        mkt_s = [view(Z + 16640 + 1024 * n, 8, P) for n in range(2)]
        mst = view(Z + 18688, 2, P)
        xs2 = [view(Z + 19000 + 1024 * n, D) for n in range(2)]
        wg = [view(ring_at, KT, FF), view(Z, KT, FF)]
        wu = [view(ring_at + 4096, KT, FF), view(Z + 4096, KT, FF)]
        wd = [view(Z + 8192, 4, D), view(Z + 12288, 4, D)]
        E0 = Z + 16384
        xs3 = view(E0, 5, D)
        x_e = view(E0, KT, BLK)
        h_sg, h_b, h_t = view(E0 + 1024, FF), view(E0 + 1536, FF), view(E0 + 2048, 4, BLK)
        xb = view(E0 + 5120, D)
        y_b = view(E0 + 6144, D)
        hot = view(E0 + 7168, 5, 2 * NE)
        slot_f = view(E0 + 7488, 10)
        slot_i = view(E0 + 7498, 10).bitcast(U32)
        gate = view(E0 + 7508, 5, 2)
        lg = view(E0 + 7520, 36)
        rbias = view(E0 + 7556, 36)
        rs = view(E0 + 7592, 200)
        tab_i = view(E0 + 7792, 2 * NE + NTAB + 1).bitcast(I32)
        cnt3 = view(E0 + 7920, NE, MAXBLK - 1)
        row3 = view(E0 + 8080, NTAB, NE)
        yg = [view(Z + D * n, D) for n in range(2 * len(TILES))]
        gfin = view(Z + 10 * D, D)
        assert E0 + 8080 + NTAB * NE <= cols, (E0, cols)
        shift_rows = view(SL + 3 * 2048, APROJ)
        last_s, last_p = view(UM, APROJ), view(UM + APROJ, APROJ)
        fin_s = view(UM + 6144, AW)
        OUT_CACHES = sum(2 * (min(w, SEQ) // P) for w, _ in GROUPS) + 2 * NB * NG

        def tab_of(part, e):
            return tab_i[0:1, bass.ds(part + e, 1)]

        srec_d = nc.dram_tensor("scratch_sample_vectors", [6, TS, AW], F32).ap()
        yrec_d = nc.dram_tensor("scratch_sample_y", [TS, AW], F32).ap()
        xs_d = nc.dram_tensor("scratch_rows_by_expert", [ROWS + BLK, D], F32).ap()
        ys_d = nc.dram_tensor("scratch_expert_rows", [ROWS + BLK, D], F32).ap()

        banks = [ctx.enter_context(nc.psum_tensor(f"bank{n}", [P, 512], F32))[:, :] for n in range(8)]
        v_mail = (banks[0:4], sem("v_filled"), sem("v_freed"))
        a_mail = (banks[4:7], sem("a_filled"), sem("a_freed"))
        aux = banks[7]

        N = {n: sem(n) for n in (
            "pe_step", "v_step", "act_step", "pool_step",
            "con_in", "x_in", "prm_in", "small_in", "prm_rows",
            "ring_used", "ring_spare", "qkv_raw", "rope_done", "xt_done",
            "p_neg", "p_exp", "p_ready", "pv_full", "pv_taken", "yb_done",
            "kv_used", "st_full", "qblk_ready", "snew", "s_soft", "sneg", "sexp",
            "um_done", "lora_in", "sga", "prep_sq", "prep_e", "exp_done", "prep_done", "stm_done",
            "lm_ready", "mats", "w_ready", "u_ready", "state_ready", "tm_done",
            "srec_out", "srec_out2", "srec_in", "rec_done", "yrec_out", "yrec_in", "ysq", "ya_done",
            "br_free", "br_in", "sig_done", "merged", "x1_done",
            "mem_in", "memx", "mkv_done", "mkv_out", "mq_done", "m_neg", "m_exp", "m_ready", "mo_done",
            "mkv_used", "mst_ready", "x2_done", "hot_done", "route_done", "xs3_done", "scattered", "pad_in", "pad_out",
            "e_area", "exp_used", "xb_in", "xb_used", "h_sig", "h_done", "yb_out", "y_ready", "yg_in", "yg_used",
            "y_final", "out", "copies", "shift_out", "tab_ready", "ssq", "state_in", "state_out", "gfin_in", "rb_in", "xe_ready",
            "shift_in", "u_raw", "y_raw", "gate_used", "route_a", "route_e", "silu_done", "x3_done", "y_taken", "y_out",
            "shift_ready", "fin_ready", "g_full", "u_full", "ht_full", "ht_done", "y_taken_a", "y_taken_v", "rms", "sq_ready", "sq_done", "seen")}
        ring_in = [sem(f"ring_in{s}") for s in range(2)]
        kv_in = [sem(f"kv_in{s}") for s in range(3)]
        mks_in = [sem(f"mks_in{s}") for s in range(2)]
        mvs_in = [sem(f"mvs_in{s}") for s in range(2)]
        w_in_sem = [sem(f"expert_weights_in{s}") for s in range(2)]
        yg_in = [sem(f"yg_in{s}") for s in range(2)]
        wexp_in = [sem(f"wexp_in{s}") for s in range(2)]

        w_in = a["w_in"].rearrange("(p kt) c -> p kt c", kt=KT)
        w_out = a["w_out"].rearrange("(kt p) c -> p kt c", p=P)
        GATE = APROJ + BPROJ
        chunks = []
        for c in range(0, BPROJ, 512):
            w = min(512, BPROJ - c)
            chunks.append([(slice(0, w), w_in[:, :, APROJ + c:APROJ + c + w])])
        NA = len(chunks)
        for c in range(0, APROJ, 512):
            w = min(512, APROJ - c)
            chunks.append([(slice(0, w), w_in[:, :, c:c + w])])
        NR = len(chunks)
        for q in range(4):
            chunks.append([(slice(0, 256), w_in[:, :, GATE + 256 * q:GATE + 256 * q + 256]),
                           (slice(256, 512), w_in[:, :, GATE + D + 256 * q:GATE + D + 256 * q + 256])])
        NGT = len(chunks)
        for c in range(2):
            chunks.append([(slice(0, 512), w_out[:, :, 512 * c:512 * c + 512])])
        NO = len(chunks)
        mkv_w = a["w_mem_kv"].rearrange("(p kt) c -> p kt c", kt=KT)
        for c in range(2):
            chunks.append([(slice(0, 512), mkv_w[:, :, 512 * c:512 * c + 512])])
        NM = len(chunks)
        chunks.append([(slice(0, 512), a["w_mem_q"].rearrange("(p kt) c -> p kt c", kt=KT))])
        chunks.append([(None, a["w_mem_out"].rearrange("(h p) d -> p h d", p=P))])
        loaded = []
        tot = [0, 0]
        for n, ch in enumerate(chunks):
            tot[n % 2] += 16 * len(ch)
            loaded.append(tot[n % 2])

        caches = (a["cache_swa_w128"], a["cache_swa_w512"], a["cache_swa_w2048"])
        units = [(g, b) for g in range(NG) for b in range(NB)]
        wide = [1, NS, NS]
        att = [(i, h) for i in range(NPT) for h in range(4)]

        def key_blocks(i):
            return [(0, j) for j in range(max(0, i - 1), i + 1)] + [(g, j) for g in (1, 2) for j in range(i + 1)]

        FIRST, COUNT, ROW, TOTAL = 0, NE, 2 * NE, 2 * NE + NTAB
        g_ps, u_ps, x_ps, h_ps, d_ps = banks[0], banks[1], banks[2:4], banks[4], banks[5:7]
        mem_units = [(i, h) for i in range(NPT) for h in range(MH)]
        block = ctx.enter_context(nc.Block())

        @block.sync
        def _(sp):
            sp.dma_start(con, cst[:, :]).then_inc(N["con_in"], 16)
            for i, (t0, n) in enumerate(TILES):
                src = a["x_prompt"][0, t0:t0 + n, :] if t0 < SEQ else a["x_sample"].rearrange("b t d -> (b t) d")
                sp.dma_start(x_res[0:n, i, :], src).then_inc(N["x_in"], 16)
            for n, g in enumerate(("norm_mix_g", "norm_mem_g", "norm_memkv_g", "norm_ffn_g")):
                sp.dma_start(gains[:, n, :], a[g].rearrange("(p k) -> p k", k=KT)).then_inc(N["prm_in"], 16)
            for name, r in (("rwkv_mu", MU), ("rwkv_w0", W0), ("rwkv_a0", A0), ("rwkv_k_k", KK_), ("rwkv_k_a", KA),
                            ("rwkv_r_k", RK), ("rwkv_lnx_g", LG), ("rwkv_lnx_b", LB), ("b_gate", BG)):
                v = a[name] if name != "rwkv_r_k" else a[name].rearrange("h d -> (h d)")
                k = v.shape[0] // P
                sp.dma_start(row_b[r:r + k, :], v.rearrange("(j p) -> j p", p=P)).then_inc(N["prm_in"], 16)

            def load_chunk(n):
                if n >= 2:
                    sp.wait_ge(N["ring_used"], n - 1)
                if n == NR:
                    sp.wait_ge(N["ring_spare"], 1)
                for cols_, src in chunks[n]:
                    dst = view(ring_at + 4096 * (n % 2), 4, D) if cols_ is None else ring[n % 2][:, :, cols_]
                    sp.dma_start(dst, src).then_inc(ring_in[n % 2], 16)

            for n in range(2):
                load_chunk(n)
            sp.dma_start(lora[0:64, 0, :], a["rwkv_w2"][:, :]).then_inc(N["small_in"], 16)
            sp.dma_start(lora[64:128, 0, :], a["rwkv_a2"][:, :]).then_inc(N["small_in"], 16)
            sp.dma_start(lora[:, 1, :], a["rwkv_g2"][:, :]).then_inc(N["small_in"], 16)
            sp.dma_start(wr[:, :, 0:4], a["w_router_group"].rearrange("(p k) e -> p k e", k=KT)).then_inc(N["small_in"], 16)
            sp.dma_start(wr[:, :, 4:36], a["w_router_expert"].rearrange("(p k) e -> p k e", k=KT)).then_inc(N["small_in"], 16)
            for n in range(2, NA):
                load_chunk(n)
            sp.wait_ge(N["rope_done"], len(TILES))
            for g, (window, _) in enumerate(GROUPS):
                keep = min(window, SEQ)
                dst = o[f"p_cache{g}"]
                for i in range(NPT - keep // P, NPT):
                    r0 = i * P - (SEQ - keep)
                    for kv in range(2):
                        src = qkv[:, i, BW * (1 + kv) + 256 * g:BW * (1 + kv) + 256 * g + 256]
                        sp.dma_start(dst[0, kv, r0:r0 + P].rearrange("t h d -> t (h d)"), src).then_inc(N["out"], 16)
                for b in range(NB):
                    for kv in range(2):
                        src = qkv[b * NS:(b + 1) * NS, 4, BW * (1 + kv) + 256 * g:BW * (1 + kv) + 256 * g + 256]
                        sp.dma_start(o[f"s_cache{g}"][b, kv, window - NS:window].rearrange("t h d -> t (h d)"), src)\
                          .then_inc(N["out"], 16)
            for kv in range(2):
                for m, (g, b) in enumerate(units):
                    z = kv * len(units) + m
                    if z >= 3:
                        sp.wait_ge(N["kv_used"], z - 2)
                    src = caches[g][b, kv].rearrange("(i r) h d -> i r (h d)", r=GROUPS[g][1])[:, 0:wide[g], :]
                    sp.dma_start(kvb[z % 3][:, 0:wide[g], :], src).then_inc(kv_in[z % 3], 16)
            sp.wait_ge(N["yb_done"], 1)
            sp.dma_start(shift_rows[0:NB, :], a["state_shift"][:, :]).then_inc(N["shift_in"], 16)
            for n in range(NA, NR):
                load_chunk(n)
            sp.wait_ge(N["stm_done"], 1)
            sp.dma_start(srec_d.rearrange("v t c -> t v c"), tok_s[0:TS]).then_inc(N["srec_out"], 16)
            sp.wait_ge(N["srec_out"], 16)
            for hf in range(2):
                for b in range(NB):
                    rows = slice(hf * 64 + b * AH, hf * 64 + (b + 1) * AH)
                    for n in range(5):
                        src = srec_d[n, b * NS:(b + 1) * NS, :].rearrange("t (h k) -> h t k", h=AH)
                        sp.dma_start(rec[rows, n, :].rearrange("p (t k) -> p t k", t=NS), src).then_inc(N["srec_in"], 16)
                    src = srec_d[5, b * NS:(b + 1) * NS, :].rearrange("t (h f k) -> h f t k", h=AH, f=2)[:, hf]
                    sp.dma_start(rec_v[rows], src).then_inc(N["srec_in"], 16)
                src = a["state_rwkv"].rearrange("b h (f v) k -> (b h) f (v k)", f=2)[:, hf]
                sp.dma_start(rec_s[hf * 64:(hf + 1) * 64].rearrange("p v k -> p (v k)"), src).then_inc(N["srec_in"], 16)
            sp.wait_ge(N["ya_done"], 1)
            sp.dma_start(wa, a["w_branch_a"].rearrange("(j p) d -> p j d", p=P)).then_inc(N["br_in"], 16)
            sp.dma_start(wb, a["w_branch_b"].rearrange("(j p) d -> p j d", p=P)).then_inc(N["br_in"], 16)
            for n in range(NR, NO):
                load_chunk(n)
            sp.wait_ge(N["x1_done"], 1)
            sp.wait_ge(N["state_out"], 48)
            sp.dma_start(mem_x, a["mem_prompt"][0].rearrange("(i p) d -> p i d", p=P)).then_inc(N["mem_in"], 16)
            for n in range(NO, len(chunks)):
                load_chunk(n)
            for b in range(NB):
                if b >= 2:
                    sp.wait_ge(N["mkv_used"], b - 1)
                sp.dma_start(mks[b % 2], a["cache_mem_kv"][b, 0].rearrange("(i p) h d -> p i (h d)", p=P)).then_inc(mks_in[b % 2], 16)
            for b in range(NB):
                if b >= 2:
                    sp.wait_ge(N["mkv_used"], NB + b - 1)
                sp.dma_start(mvs[b % 2], a["cache_mem_kv"][b, 1].rearrange("(i p) h d -> p i (h d)", p=P)).then_inc(mvs_in[b % 2], 16)
            sp.wait_ge(N["e_area"], 1)
            sp.wait_ge(N["mkv_out"], 32)
            eg = a["w_exp_gate"].rearrange("e (p k) f -> e p k f", k=KT)
            eu = a["w_exp_up"].rearrange("e (p k) f -> e p k f", k=KT)
            ed = a["w_exp_down"].rearrange("e (c p) d -> e p c d", p=P)

            def load_expert(e, s, started):
                part = 0
                for w, src, k in ((wg, eg, KT), (wu, eu, KT), (wd, ed, 4)):
                    src = src[e] if isinstance(e, int) else src[bass.ds(e, 1)][0]
                    for h in range(2):
                        q = part % 2
                        if started or part >= 2:
                            sp.wait_ge(w_in_sem[q], 48 * e + 16 * (part // 2))
                        if not isinstance(e, int):
                            sp.sem_inc(N["seen"], 1)
                        ks = slice(h * k // 2, (h + 1) * k // 2)
                        sp.dma_start(w[s][:, ks, :], src[:, ks, :]).then_inc(w_in_sem[q], 16)
                        part += 1

            for s in range(2):
                load_expert(s, s, s > 0)
            with sp.Fori(1, NE // 2) as j:
                for s in range(2):
                    sp.wait_ge(N["exp_used"], 2 * j + s - 1)
                    sp.sem_inc(N["seen"], 1)
                    load_expert(2 * j + s, s, True)
            sp.wait_ge(N["out"], 16 * OUT_CACHES)

        @block.tensor
        def _(pe):
            line = Line(pe, N["pe_step"])
            vm, am = Mail(*v_mail), Mail(*a_mail)
            mm = pe.matmul

            def turn_rows(src, n, s, k):
                for half in range(2):
                    bank = vm.claim(pe)
                    for q in range(4):
                        last = pe.transpose(bank[:, q * P:q * P + n], src[0:n, 4 * half + q:D:KT], ident[0:n, 0:n])
                    last.then_inc(vm.filled, 1)

            def chunk_ready(n):
                pe.wait_ge(ring_in[n % 2], loaded[n])

            def chunk_used(mail):
                pe.wait_ge(mail.filled, mail.put)
                pe.sem_inc(N["ring_used"], 1)

            pe.wait_ge(N["con_in"], 16)
            pe.wait_ge(N["prm_in"], 16 * 13)
            bank = vm.claim(pe)
            pe.transpose(bank[:, 0:NPRM], row_b[0:NPRM, :], ident[0:NPRM, 0:NPRM]).then_inc(vm.filled, 1)
            for i, (t0, n) in enumerate(TILES):
                pe.wait_ge(N["xs3_done"], i + 1)
                turn_rows(xs_tmp[i % 2], n, None, i)
            pe.wait_ge(N["xt_done"], len(TILES))
            for n in range(NA):
                chunk_ready(n)
                w = chunks[n][0][0].stop
                for i, (t0, m) in enumerate(TILES):
                    bank = am.claim(pe)
                    for kt in range(KT):
                        last = mm(bank[0:m, 0:w], x_t[:, kt, t0:t0 + m], ring[n % 2][:, kt, 0:w], start=kt == 0, stop=kt == KT - 1)
                    last.then_inc(am.filled, 1)
                chunk_used(am)
            for i, (t0, m) in enumerate(TILES):
                pe.wait_ge(N["rope_done"], i + 1)
                for half in range(3):
                    bank = vm.claim(pe)
                    for q in range(4):
                        j = 4 * half + q
                        last = pe.transpose(bank[:, q * P:q * P + m], qkv[0:m, i, j * P:(j + 1) * P], ident[0:m, 0:m])
                    last.then_inc(vm.filled, 1)
            pe.wait_ge(vm.freed, vm.put)
            def scores(u):
                i, h = att[u]
                lo = 64 * (h % 2)
                for g in range(NG):
                    js = [j for gg, j in key_blocks(i) if gg == g]
                    bank = vm.claim(pe)
                    mm(bank[:, 0:P * len(js)], qk_t[lo:lo + 64, 2 * g + h // 2, i * P:(i + 1) * P],
                       qk_t[lo:lo + 64, 6 + 2 * g + h // 2, js[0] * P:(js[-1] + 1) * P], start=True, stop=True).then_inc(vm.filled, 1)

            def weigh(u):
                i, h = att[u]
                kb = key_blocks(i)
                pe.wait_ge(N["p_ready"], u + 1)
                for c in range(0, len(kb), 4):
                    bank = am.claim(pe)
                    for q in range(c, min(c + 4, len(kb))):
                        last = pe.transpose(bank[:, (q - c) * P:(q - c + 1) * P], s_sb[u % 2][:, q * P:(q + 1) * P], ident)
                    last.then_inc(am.filled, 1)
                pe.wait_ge(am.freed, am.put)
                if u >= 1:
                    pe.wait_ge(N["pv_taken"], u)
                lo = 64 * (h % 2)
                for q, (g, j) in enumerate(kb):
                    c = 2 * BW + 256 * g + 64 * h
                    last = mm(aux[lo:lo + 64, 0:P], qkv[:, j, c:c + 64], p_t[u % 2][:, q, :], start=q == 0, stop=q == len(kb) - 1)
                last.then_inc(N["pv_full"], 1)

            for u in range(len(att) + 1):
                if u < len(att):
                    scores(u)
                if u >= 1:
                    weigh(u - 1)
            pe.wait_ge(N["qblk_ready"], 1)
            pe.wait_ge(N["pv_taken"], len(att))

            def turn_keys(m):
                g, b = units[m]
                pe.wait_ge(kv_in[m % 3], 16 * (m // 3 + 1))
                for c in range(0, 2 * wide[g], 4):
                    bank = am.claim(pe)
                    for q in range(c, min(c + 4, 2 * wide[g])):
                        last = pe.transpose(bank[:, (q - c) * P:(q - c + 1) * P], kvb[m % 3][:, q // 2, (q % 2) * P:(q % 2 + 1) * P], ident)
                    last.then_inc(am.filled, 1)
                return am.put

            def cached_scores(m, got):
                g, b = units[m]
                pe.wait_ge(am.freed, got)
                for t in range(wide[g]):
                    for hp in range(2):
                        q = qblk[:, 2 * g + hp, :].rearrange("p (h t) -> p h t", t=TS)
                        dst = aux[:, P * g + 64 * hp:P * g + 64 * hp + 64].rearrange("p (h t) -> p h t", t=TS)
                        ts = slice(b * NS, (b + 1) * NS) if wide[g] == 1 else slice(b * NS + t, b * NS + t + 1)
                        last = mm(dst[:, :, ts], kt_s[m % 2][:, 2 * t + hp, :], q[:, :, ts], start=True, stop=True)
                last.then_inc(N["kv_used"], 1)

            got = turn_keys(0)
            for m in range(len(units)):
                nxt = turn_keys(m + 1) if m + 1 < len(units) else None
                cached_scores(m, got)
                got = nxt
            bank = vm.claim(pe)
            for g in range(NG):
                for hp in range(2):
                    last = mm(bank[0:TS, P * g + 64 * hp:P * g + 64 * hp + 64], qk_t[:, 6 + 2 * g + hp, SEQ:T],
                              qblk[:, 2 * g + hp, :], start=True, stop=True)
            last.then_inc(vm.filled, 1)
            pe.wait_ge(N["snew"], 1)
            bank = vm.claim(pe)
            for g in range(NG):
                pe.transpose(bank[:, g * P:(g + 1) * P], st_sb[:, g, :], ident)
                last = pe.transpose(bank[:, NG * P + g * TS:NG * P + (g + 1) * TS], stn_sb[0:TS, g, :], ident[0:TS, 0:TS])
            last.then_inc(vm.filled, 1)
            pe.wait_ge(N["s_soft"], 1)
            bank = vm.claim(pe)
            for g in range(NG):
                last = pe.transpose(bank[:, g * P:(g + 1) * P], ps_sb[:, g * P:(g + 1) * P], ident)
            last.then_inc(vm.filled, 1)
            bank = vm.claim(pe)
            for g in range(NG):
                last = pe.transpose(bank[0:TS, g * P:(g + 1) * P], ps_sb[:, NG * P + g * TS:NG * P + (g + 1) * TS], ident)
            last.then_inc(vm.filled, 1)
            pe.wait_ge(vm.freed, vm.put)
            for g in range(NG):
                for hp in range(2):
                    c = 2 * BW + 256 * g + P * hp
                    mm(aux[:, 64 * hp:64 * hp + 64], qkv[0:TS, 4, c:c + P], ptn[0:TS, g, 64 * hp:64 * hp + 64],
                       start=g == 0 and hp == 0, stop=False, skip_group_check=True)
            for m, (g, b) in enumerate(units):
                z = len(units) + m
                pe.wait_ge(kv_in[z % 3], 16 * (z // 3 + 1))
                for t in range(wide[g]):
                    for hp in range(2):
                        pr = pts[:, g, 64 * hp:64 * hp + 64].rearrange("p (h t) -> p h t", t=TS)
                        dst = aux[:, 64 * hp:64 * hp + 64].rearrange("p (h t) -> p h t", t=TS)
                        ts = slice(b * NS, (b + 1) * NS) if wide[g] == 1 else slice(b * NS + t, b * NS + t + 1)
                        last = mm(dst[:, :, ts], kvb[z % 3][:, t, hp * P:(hp + 1) * P], pr[:, :, ts], start=False,
                                  stop=m == len(units) - 1, skip_group_check=True)
                last.then_inc(N["kv_used"], 1)
            for c in range(NA, NR):
                chunk_ready(c)
                w = chunks[c][0][0].stop
                small = vm.claim(pe)
                for q in range(w // P):
                    bank = am.claim(pe)
                    for kt in range(KT):
                        last = mm(bank, ring[c % 2][:, kt, q * P:(q + 1) * P], x_t[:, kt, 0:SEQ], start=kt == 0, stop=kt == KT - 1)
                    last.then_inc(am.filled, 1)
                    for kt in range(KT):
                        last = mm(small[:, q * TS:(q + 1) * TS], ring[c % 2][:, kt, q * P:(q + 1) * P], x_t[:, kt, SEQ:T],
                                  start=kt == 0, stop=kt == KT - 1)
                last.then_inc(vm.filled, 1)
                chunk_used(vm)
            pe.wait_ge(N["um_done"], 1)
            for c in range(0, AJ, 4):
                bank = vm.claim(pe)
                for j in range(c, min(c + 4, AJ)):
                    last = pe.transpose(bank[0:NB, (j - c) * P:(j - c + 1) * P], u_s[:, j, NS - 1:TS:NS], ident)
                last.then_inc(vm.filled, 1)
                bank = vm.claim(pe)
                for j in range(c, min(c + 4, AJ)):
                    last = pe.transpose(bank[0:1, (j - c) * P:(j - c + 1) * P], u_p[:, j, SEQ - 1:SEQ], ident)
                last.then_inc(vm.filled, 1)
            pe.wait_ge(N["shift_in"], 16)
            for c in range(0, AJ, 4):
                bank = vm.claim(pe)
                for j in range(c, min(c + 4, AJ)):
                    last = pe.transpose(bank[:, (j - c) * NB:(j - c + 1) * NB],
                                        shift_rows[0:NB, j * P:(j + 1) * P],
                                        ident[0:NB, 0:NB])
                last.then_inc(vm.filled, 1)
            for part, (um, sq) in enumerate(((um_s, tmp_s), (um_p, tmp_p))):
                n = TS if part == 0 else SEQ
                pe.wait_ge(N["lora_in"], part + 1)
                for j in range(4):
                    for lhs, rhs in ((lora[0:64, 0], um[0:64, 12]), (lora[64:128, 0], um[64:128, 12]), (lora[:, 1], um[:, 13])):
                        bank = am.claim(pe)
                        mm(bank[:, 0:n], lhs[:, j * P:(j + 1) * P], rhs, start=True, stop=True).then_inc(am.filled, 1)
                for what in range(2):
                    pe.wait_ge(N["prep_sq"], 2 * part + what + 1)
                    for j in range(4):
                        bank = vm.claim(pe)
                        mm(bank[:, 0:n], C("blk"), sq[:, j, 0:n], start=True, stop=True).then_inc(vm.filled, 1)
                if part == 0:
                    pe.wait_ge(N["tm_done"], 1)
                    for src in (um_s[:, 0:4], um_s[:, 4:8], kk_s, a_s, dec_s, um_s[:, 8:12]):
                        bank = vm.claim(pe)
                        for j in range(4):
                            last = pe.transpose(bank[0:TS, j * P:(j + 1) * P], src[:, j, :], ident)
                        last.then_inc(vm.filled, 1)
            pe.wait_ge(N["prep_done"], 1)
            for src in (a_p, um_p[:, 4:8], um_p[:, 8:12]):
                for i in range(NPT):
                    bank = vm.claim(pe)
                    for j in range(4):
                        last = pe.transpose(bank[:, j * P:(j + 1) * P], src[:, j, i * P:(i + 1) * P], ident)
                    last.then_inc(vm.filled, 1)
            pe.wait_ge(vm.freed, vm.put)

            def heads(par):
                return [(j, 2 * j + par) for j in range(4)]

            r_p, k_p = um_p[:, 0:4], um_p[:, 4:8]
            for i in range(NPT):
                tk = slice(i * P, (i + 1) * P)
                if i >= 1:
                    pe.wait_ge(N["state_ready"], i)
                for lhs, rhs in ((a_p, kk_p), (kk_p, a_p), (k_p, kk_p), (a_p, r_p), (k_p, r_p)):
                    two = [vm.claim(pe), vm.claim(pe)]
                    for par in range(2):
                        lo = 64 * par
                        for j, h in heads(par):
                            last = mm(two[par][:, j * P:(j + 1) * P], lhs[lo:lo + 64, j, tk], rhs[lo:lo + 64, j, tk], start=True, stop=True)
                        last.then_inc(vm.filled, 1)
                for lv, m in enumerate(LEVELS[1:]):
                    final = m == LEVELS[-1]
                    pe.wait_ge(N["lm_ready"], 6 * i + lv + 1)
                    pe.wait_ge(vm.freed, vm.put)
                    for par in range(2):
                        bank = vm.claim(pe)
                        for j in range(4):
                            last = mm(bank[:, j * P:(j + 1) * P], mat_lm[:, 4 * par + j, :], mat_t[:, 4 * par + j, :], start=True, stop=True)
                        last.then_inc(vm.filled, 1)
                    base = vm.put
                    for par in range(2):
                        pe.wait_ge(vm.freed, base - 1 + par)
                        for tt in ((0, 1) if not final else (1,)):
                            bank = vm.claim(pe)
                            for j in range(4):
                                z = 4 * par + j
                                lhs, rhs = (mat_w, mat_tt) if tt else (mat_tt, mat_w)
                                last = mm(bank[:, j * P:(j + 1) * P], lhs[:, z, :], rhs[:, z, :], start=True, stop=True)
                            last.then_inc(vm.filled, 1)
                pe.wait_ge(vm.freed, vm.put)
                two = [vm.claim(pe), vm.claim(pe)]
                for par in range(2):
                    lo = 64 * par
                    for j, h in heads(par):
                        dst = two[par][:, j * 64:j * 64 + 64]
                        mm(dst, kk_p[lo:lo + 64, j, tk], st0m[lo:lo + 64, j, :], start=True, stop=False)
                        last = mm(dst, mat_ak[:, 4 * par + j, :], tm_v[:, i, h * 64:h * 64 + 64], start=False, stop=True)
                    last.then_inc(vm.filled, 1)
                pe.wait_ge(vm.freed, vm.put)
                bank = vm.claim(pe)
                for z in range(8):
                    last = mm(bank[:, z * 64:z * 64 + 64], mat_tt[:, z, :], w_sb[:, z, :], start=True, stop=True)
                last.then_inc(vm.filled, 1)
                pe.wait_ge(vm.freed, vm.put)
                bank = vm.claim(pe)
                for par in range(2):
                    lo = 64 * par
                    for j, h in heads(par):
                        dst = bank[lo:lo + 64, j * 64:j * 64 + 64]
                        mm(dst, tm_b[:, i, h * 64:h * 64 + 64], uu_sb[:, 4 * par + j, :], start=True, stop=False)
                        last = mm(dst, tm_k[:, i, h * 64:h * 64 + 64], tm_v[:, i, h * 64:h * 64 + 64], start=False, stop=True)
                last.then_inc(vm.filled, 1)
                two = [am.claim(pe), am.claim(pe)]
                for par in range(2):
                    lo = 64 * par
                    for j, h in heads(par):
                        dst = two[par][lo:lo + 64, j * P:(j + 1) * P]
                        z = 4 * par + j
                        mm(dst, st0m[lo:lo + 64, j, :], r_p[lo:lo + 64, j, tk], start=True, stop=False)
                        mm(dst, uu_sb[:, z, :], mat_rb[:, z, :], start=False, stop=False)
                        last = mm(dst, tm_v[:, i, h * 64:h * 64 + 64], mat_rk[:, z, :], start=False, stop=True)
                    last.then_inc(am.filled, 1)
                pe.wait_ge(am.filled, am.put)
                pe.sem_inc(N["mats"], 1)
            pe.wait_ge(N["state_ready"], NPT)
            bank = vm.claim(pe)
            for j in range(4):
                last = pe.transpose(bank[0:64, j * P:(j + 1) * P], st0[:, j, :], ident)
            last.then_inc(vm.filled, 1)
            pe.wait_ge(N["yrec_in"], 16)
            bank = vm.claim(pe)
            for j in range(4):
                last = pe.transpose(bank[:, j * TS:(j + 1) * TS], y_tok[0:TS, j * P:(j + 1) * P], ident[0:TS, 0:TS])
            last.then_inc(vm.filled, 1)
            for part in range(2):
                n = TS if part == 0 else SEQ
                y = y_s if part == 0 else a_p
                sq = tmp_s if part == 0 else tmp_p
                for what, src in enumerate((y, sq)):
                    pe.wait_ge(N["ysq"], 2 * part + what + 1)
                    for j in range(4):
                        bank = vm.claim(pe)
                        mm(bank[:, 0:n], C("blk"), src[:, j, 0:n], start=True, stop=True).then_inc(vm.filled, 1)
            pe.wait_ge(N["ya_done"], 1)
            pe.wait_ge(N["br_in"], 32)
            for c in range(NR, NGT):
                chunk_ready(c)
                for jj in range(2):
                    j = 2 * (c - NR) + jj
                    for part, (t0, n) in enumerate(((0, SEQ), (SEQ, TS))):
                        for off in (0, 256):
                            bank = am.claim(pe)
                            for kt in range(KT):
                                last = mm(bank[:, 0:n], ring[c % 2][:, kt, off + jj * P:off + (jj + 1) * P], x_t[:, kt, t0:t0 + n],
                                          start=kt == 0, stop=kt == KT - 1)
                            last.then_inc(am.filled, 1)
                        ya = a_p if part == 0 else y_s
                        bank = vm.claim(pe)
                        for q in range(4):
                            last = mm(bank[:, 0:n], wa[:, q, j * P:(j + 1) * P], ya[:, q, 0:n], start=q == 0, stop=q == 3)
                        last.then_inc(vm.filled, 1)
                        bank = vm.claim(pe)
                        for q in range(2):
                            last = mm(bank[:, 0:n], wb[:, q, j * P:(j + 1) * P], yb_t[:, q, t0:t0 + n], start=q == 0, stop=q == 1)
                        last.then_inc(vm.filled, 1)
                chunk_used(vm)
            pe.wait_ge(N["merged"], 1)

            def out_rows(first, nk, lhs, last_sem):
                for i, (t0, m) in enumerate(TILES):
                    for c in range(2):
                        bank = vm.claim(pe)
                        for k in range(nk):
                            last = mm(bank[0:m, :], lhs[:, k, t0:t0 + m], first(c, k), start=k == 0, stop=k == nk - 1)
                        last.then_inc(vm.filled, 1)

            chunk_ready(NGT)
            chunk_ready(NGT + 1)
            out_rows(lambda c, k: ring[(NGT + c) % 2][:, k, :], KT, m_t, None)
            chunk_used(vm)
            chunk_used(vm)
            for i in range(2):
                pe.wait_ge(N["memx"], i + 1)
                turn_rows(xs2[i % 2], P, None, i)
            pe.wait_ge(vm.freed, vm.put)
            for c in range(2):
                chunk_ready(NO + c)
                for i in range(2):
                    bank = vm.claim(pe)
                    for kt in range(KT):
                        last = mm(bank, mem_t[:, kt, i * P:(i + 1) * P], ring[(NO + c) % 2][:, kt, :], start=kt == 0, stop=kt == KT - 1)
                    last.then_inc(vm.filled, 1)
                chunk_used(vm)
            pe.wait_ge(vm.freed, vm.put)
            for i in range(2):
                bank = vm.claim(pe)
                for h in range(MH):
                    last = pe.transpose(bank[:, h * P:(h + 1) * P], mkv[:, i, h * P:(h + 1) * P], ident)
                last.then_inc(vm.filled, 1)
            for i, (t0, n) in enumerate(TILES):
                pe.wait_ge(N["memx"], 2 + i + 1)
                turn_rows(xs2[i % 2], n, None, i)
            pe.wait_ge(vm.freed, vm.put)
            chunk_ready(NM)
            for h in range(MH):
                for t0, n in ((0, SEQ), (SEQ, TS)):
                    bank = vm.claim(pe)
                    for kt in range(KT):
                        last = mm(bank[:, 0:n], ring[NM % 2][:, kt, h * P:(h + 1) * P], x_t[:, kt, t0:t0 + n], start=kt == 0, stop=kt == KT - 1)
                    last.then_inc(vm.filled, 1)
            chunk_used(vm)
            pe.wait_ge(vm.freed, vm.put)

            def mem_scores(u):
                i, h = mem_units[u]
                bank = vm.claim(pe)
                mm(bank[:, 0:MEM], q_t[:, h, i * P:(i + 1) * P], mk_t[:, h, :], start=True, stop=True).then_inc(vm.filled, 1)

            def mem_weigh(u):
                i, h = mem_units[u]
                pe.wait_ge(N["m_ready"], u + 1)
                bank = am.claim(pe)
                for c in range(2):
                    last = pe.transpose(bank[:, c * P:(c + 1) * P], ms_sb[u % 2][:, c * P:(c + 1) * P], ident)
                last.then_inc(am.filled, 1)
                pe.wait_ge(am.freed, am.put)
                bank = am.claim(pe)
                for c in range(2):
                    last = mm(bank[:, 0:P], mkv[:, c, MW + h * P:MW + (h + 1) * P], mp_t[u % 2][:, c, :], start=c == 0, stop=c == 1)
                last.then_inc(am.filled, 1)

            for u in range(len(mem_units) + 1):
                if u < len(mem_units):
                    mem_scores(u)
                if u >= 1:
                    mem_weigh(u - 1)
            def turn_mem(b):
                pe.wait_ge(mks_in[b % 2], 16 * (b // 2 + 1))
                for c in range(2):
                    bank = am.claim(pe)
                    for h in range(MH):
                        last = pe.transpose(bank[:, h * P:(h + 1) * P], mks[b % 2][:, c, h * P:(h + 1) * P], ident)
                    last.then_inc(am.filled, 1)
                return am.put

            got = turn_mem(0)
            for b in range(NB):
                nxt = turn_mem(b + 1) if b + 1 < NB else None
                pe.wait_ge(am.freed, got)
                for c in range(2):
                    for h in range(MH):
                        last = mm(aux[:, c * P + h * TS + b * NS:c * P + h * TS + (b + 1) * NS], mkt_s[b % 2][:, 4 * c + h, :],
                                  q_t[:, h, SEQ + b * NS:SEQ + (b + 1) * NS], start=True, stop=True)
                last.then_inc(N["mkv_used"], 1)
                got = nxt
            pe.wait_ge(N["mst_ready"], 1)
            bank = vm.claim(pe)
            for c in range(2):
                last = pe.transpose(bank[:, c * P:(c + 1) * P], mst[:, c, :], ident)
            last.then_inc(vm.filled, 1)
            pe.wait_ge(N["m_ready"], len(mem_units) + 1)
            bank = am.claim(pe)
            for c in range(2):
                last = pe.transpose(bank[:, c * P:(c + 1) * P], ms_sb[0][:, c * P:(c + 1) * P], ident)
            last.then_inc(am.filled, 1)
            pe.wait_ge(am.freed, am.put)
            for b in range(NB):
                pe.wait_ge(mvs_in[b % 2], 16 * (b // 2 + 1))
                for h in range(MH):
                    for c in range(2):
                        cs = h * TS + b * NS
                        last = mm(aux[:, cs:cs + NS], mvs[b % 2][:, c, h * P:(h + 1) * P], mp_t[0][:, c, cs:cs + NS],
                                  start=c == 0, stop=c == 1)
                last.then_inc(N["mkv_used"], 1)
            pe.wait_ge(N["mo_done"], 1)
            pe.wait_ge(am.freed, am.put)
            chunk_ready(NM + 1)
            wmo = view(ring_at + 4096 * ((NM + 1) % 2), 4, D)
            out_rows(lambda c, k: wmo[:, k, c * 512:(c + 1) * 512], MH, o_t, None)
            chunk_used(vm)
            pe.wait_ge(N["x2_done"], 1)
            pe.sem_inc(N["e_area"], 1)
            for i, (t0, n) in enumerate(TILES):
                pe.wait_ge(N["xs3_done"], len(TILES) + i + 1)
                turn_rows(xs3[:, i, :], n, None, i)
                pe.wait_ge(vm.freed, vm.put)
                bank = vm.claim(pe)
                for kt in range(KT):
                    last = mm(bank[0:n, 0:36], x_t[:, kt, t0:t0 + n], wr[:, kt, :], start=kt == 0, stop=kt == KT - 1)
                last.then_inc(vm.filled, 1)
            pe.wait_ge(N["hot_done"], 1)
            bank = vm.claim(pe)
            for j, (t0, m) in enumerate(TILES):
                last = mm(bank[:, 0:2 * NE], C("ones")[0:m, :], hot[0:m, j, :], start=j == 0, stop=j == len(TILES) - 1)
            last.then_inc(vm.filled, 1)
            for i, (t0, n) in enumerate(TILES):
                bank = vm.claim(pe)
                for j in range(i + 1):
                    m = TILES[j][1]
                    lhs = C("ones")[0:m, 0:n] if j < i else C("strict")[0:m, 0:n]
                    last = mm(bank[0:n, 0:2 * NE], lhs, hot[0:m, j, :], start=j == 0, stop=j == i)
                last.then_inc(vm.filled, 1)
            pe.wait_ge(N["tab_ready"], 1)
            def turn_block():
                for kt in range(KT):
                    last = pe.transpose(x_ps[kt // 4][:, kt % 4 * BLK:(kt % 4 + 1) * BLK], xb[:, kt:D:KT], ident)
                last.then_inc(N["xb_used"], 1)

            pe.wait_ge(N["xb_in"], 16)
            turn_block()
            with pe.Fori(0, NE // 2) as jj:
                for s in range(2):
                    first = pe.value_load(tab_of(FIRST, 2 * jj + s), min_val=0, max_val=ALLBLK)
                    blocks = pe.value_load(tab_of(COUNT, 2 * jj + s), min_val=1, max_val=MAXBLK)
                    for q in range(2):
                        pe.wait_ge(w_in_sem[q], 48 * (2 * jj + s + 1))
                    pe.sem_inc(N["seen"], 1)
                    with pe.Fori(0, blocks) as m:
                        n = pe.snap(first + m)
                        pe.wait_ge(N["xe_ready"], n + 1)
                        for dst, w, full in ((g_ps, wg[s], N["g_full"]), (u_ps, wu[s], N["u_full"])):
                            for kt in range(KT):
                                last = mm(dst, x_e[:, kt, :], w[:, kt, :], start=kt == 0, stop=kt == KT - 1)
                            last.then_inc(full, 1)
                        pe.wait_ge(N["xb_in"], 16 * n + 32)
                        pe.sem_inc(N["seen"], 1)
                        turn_block()
                        pe.wait_ge(N["h_done"], n + 1)
                        pe.sem_inc(N["seen"], 1)
                        for k in range(4):
                            last = pe.transpose(h_ps[:, k * BLK:(k + 1) * BLK], h_b[:, k * P:(k + 1) * P], ident)
                        last.then_inc(N["ht_full"], 1)
                        pe.wait_ge(N["ht_done"], n + 1)
                        for c in range(2):
                            for k in range(4):
                                last = mm(d_ps[c], h_t[:, k, :], wd[s][:, k, c * 512:(c + 1) * 512], start=k == 0, stop=k == 3)
                            last.then_inc(N["y_ready"], 1)
                    pe.wait_ge(N["y_ready"], 2 * (first + blocks))
                    pe.sem_inc(N["exp_used"], 1)

        @block.scalar
        def _(act):
            line = Line(act, N["act_step"])
            am = Mail(*a_mail)

            def f(out, in_, func, sem=None, **kw):
                line.do(nc.scalar.activation(out, in_, func, **kw), sem)

            def rms(rows, junk):
                for col, (src, n) in enumerate(rows):
                    f(junk[0:n], src, ACT.Square, accum_out=stat[0:n, col:col + 1])
                full = sum(n == P for _, n in rows)
                f(stat[:, 0:full], stat[:, 0:full], ACT.Sqrt, scale=1.0 / D, bias=C("eps"))
                if full < len(rows):
                    n = rows[-1][1]
                    f(stat[0:n, full:full + 1], stat[0:n, full:full + 1], ACT.Sqrt, scale=1.0 / D, bias=C("eps")[0:n])
                act.sem_inc(N["rms"], 1)

            stream = [(x_res[0:n, i, :], n) for i, (t0, n) in enumerate(TILES)]

            act.wait_ge(N["x_in"], 16 * len(TILES))
            act.wait_ge(N["con_in"], 16)
            rms(stream, view(s0 + 2560, D))
            for c in range(NA):
                w = chunks[c][0][0].stop
                for i, (t0, n) in enumerate(TILES):
                    bank = am.take(act)
                    f(qkv[0:n, i, 512 * c:512 * c + w], bank[0:n, 0:w], ACT.Copy, am.freed)
            act.sem_inc(N["qkv_raw"], 1)

            def exp_unit(u):
                i, h = att[u]
                n = P * len(key_blocks(i))
                c = 8 + 4 * (u % 2)
                act.wait_ge(N["p_neg"], u + 1)
                f(s_sb[u % 2][:, 0:n], s_sb[u % 2][:, 0:n], ACT.Exp, N["p_exp"], bias=stat[:, c + 1:c + 2], scale=0.125,
                  accum_out=stat[:, c + 2:c + 3])

            def take_unit(u):
                i, h = att[u]
                kb = key_blocks(i)
                for c in range(0, len(kb), 4):
                    k = min(4, len(kb) - c)
                    bank = am.take(act)
                    f(p_t[u % 2][:, c:c + k, :], bank[:, 0:k * P].rearrange("p (a b) -> p a b", b=P), ACT.Copy, am.freed)
                act.wait_ge(N["pv_full"], u + 1)
                lo = 64 * (h % 2)
                f(yb_t[lo:lo + 64, h // 2, i * P:(i + 1) * P], aux[lo:lo + 64, 0:P], ACT.Copy, N["pv_taken"])

            for u in range(len(att) + 1):
                if u < len(att):
                    exp_unit(u)
                if u >= 1:
                    take_unit(u - 1)
            for m, (g, b) in enumerate(units):
                for c in range(0, 2 * wide[g], 4):
                    k = min(4, 2 * wide[g] - c)
                    bank = am.take(act)
                    f(kt_s[m % 2][:, c:c + k, :], bank[:, 0:k * P].rearrange("p (a b) -> p a b", b=P), ACT.Copy, am.freed)
            act.wait_ge(N["sneg"], 1)
            f(ps_sb, ps_sb, ACT.Exp, N["sexp"], bias=stat[:, 17:18], scale=0.125, accum_out=stat[:, 18:19])
            act.wait_ge(N["yb_done"], 1)
            act.wait_ge(N["out"], 16 * OUT_CACHES)
            for c in range(NA, NR):
                for q in range(chunks[c][0][0].stop // P):
                    bank = am.take(act)
                    f(u_p[:, 4 * (c - NA) + q, :], bank, ACT.Copy, am.freed)
            act.sem_inc(N["u_raw"], 1)
            for part, um in enumerate((um_s, um_p)):
                n = TS if part == 0 else SEQ
                act.wait_ge(N["um_done"], part + 2)
                f(um[0:64, 12, :], um[0:64, 12, :], ACT.Tanh)
                f(um[:, 13, :], um[:, 13, :], ACT.Sigmoid, N["lora_in"])
                sg, aa, gg = (dec_s, a_s, g_s) if part == 0 else (sg_p, a_p, g_p)
                for j in range(4):
                    f(sg[:, j, 0:n], am.take(act)[:, 0:n], ACT.Sigmoid, am.freed, bias=prm[:, W0 + j:W0 + j + 1])
                    f(aa[:, j, 0:n], am.take(act)[:, 0:n], ACT.Sigmoid, am.freed, bias=prm[:, A0 + j:A0 + j + 1])
                    f(gg[:, j, 0:n], am.take(act)[:, 0:n], ACT.Copy, am.freed)
                act.sem_inc(N["sga"], 1)
                act.wait_ge(N["sq_ready"], part + 1)
                tmp = tmp_s if part == 0 else tmp_p
                f(tmp, tmp, ACT.Sqrt, N["sq_done"])
                act.wait_ge(N["prep_e"], part + 1)
                if part == 0:
                    f(dec_s, dec_s, ACT.Exp, scale=-float(np.exp(np.float32(-0.5))))
                else:
                    f(sg_p, sg_p, ACT.Exp)
                    f(tmp_p, c_p, ACT.Exp)
                    f(c_p, c_p, ACT.Exp, scale=-1.0)
                    f(pmid, pmid, ACT.Exp)
                act.sem_inc(N["exp_done"], 1)
            for i in range(NPT):
                for par in range(2):
                    lo = 64 * par
                    bank = am.take(act)
                    f(a_p[lo:lo + 64, :, i * P:(i + 1) * P], bank[lo:lo + 64, :].rearrange("p (a b) -> p a b", b=P), ACT.Copy, am.freed)
            act.sem_inc(N["y_raw"], 1)
            for part in range(2):
                act.wait_ge(N["sq_ready"], 2 + part + 1)
                tmp = tmp_s if part == 0 else tmp_p
                f(tmp, tmp, ACT.Sqrt, N["sq_done"])
            z = 0
            for j in range(KT):
                for t0, n in ((0, SEQ), (SEQ, TS)):
                    if z >= 2:
                        act.wait_ge(N["gate_used"], z - 1)
                    f(sg_a[:, t0:t0 + n], am.take(act)[:, 0:n], ACT.Sigmoid, am.freed, bias=prm[:, BG + j:BG + j + 1])
                    f(sg_b[:, t0:t0 + n], am.take(act)[:, 0:n], ACT.Sigmoid, am.freed, bias=prm[:, BG + 8 + j:BG + 9 + j])
                    act.sem_inc(N["sig_done"], 1)
                    z += 1
            act.wait_ge(N["x1_done"], 1)
            act.wait_ge(N["mem_in"], 16)
            rms([(mem_x[:, i, :], P) for i in range(2)] + stream, view(Z + 21060, D))
            MS = float(MD) ** -0.5
            nu = len(mem_units)
            for u in range(nu + 1):
                if u < nu:
                    c = 20 + 4 * (u % 2)
                    act.wait_ge(N["m_neg"], u + 1)
                    f(ms_sb[u % 2], ms_sb[u % 2], ACT.Exp, N["m_exp"], bias=stat[:, c + 1:c + 2], scale=MS, accum_out=stat[:, c + 2:c + 3])
                if u >= 1:
                    i, h = mem_units[u - 1]
                    f(mp_t[(u - 1) % 2], am.take(act)[:, 0:MEM].rearrange("p (a b) -> p a b", b=P), ACT.Copy, am.freed)
                    f(o_t[:, h, i * P:(i + 1) * P], am.take(act)[:, 0:P], ACT.Copy, am.freed)
            for b in range(NB):
                for c in range(2):
                    f(mkt_s[b % 2][:, 4 * c:4 * c + 4, :], am.take(act)[:, :].rearrange("p (a b) -> p a b", b=P), ACT.Copy, am.freed)
            act.wait_ge(N["m_neg"], nu + 1)
            f(ms_sb[0], ms_sb[0], ACT.Exp, N["m_exp"], bias=stat[:, 21:22], scale=MS, accum_out=stat[:, 22:23])
            f(mp_t[0], am.take(act)[:, 0:MEM].rearrange("p (a b) -> p a b", b=P), ACT.Copy, am.freed)
            act.wait_ge(N["x2_done"], 1)
            rms(stream, y_b)
            for i, (t0, n) in enumerate(TILES):
                act.wait_ge(N["route_a"], i + 1)
                f(rs[0:n, 160:164], lg[0:n, 0:4], ACT.Exp, bias=rs[0:n, 24:25], accum_out=rs[0:n, 25:26])
                f(rs[0:n, 27:28], rs[0:n, 26:27], ACT.Exp)
                act.sem_inc(N["route_e"], 1)
            act.wait_ge(N["tab_ready"], 1)
            total = act.value_load(tab_i[0:1, TOTAL:TOTAL + 1], min_val=NE, max_val=ALLBLK)
            with act.Fori(0, total) as n:
                act.wait_ge(N["g_full"], n + 1)
                nc.scalar.activation(h_sg, g_ps, ACT.Silu).then_inc(N["silu_done"], 1)
                act.wait_ge(N["ht_full"], n + 1)
                nc.scalar.activation(h_t, h_ps.rearrange("p (a b) -> p a b", b=BLK), ACT.Copy).then_inc(N["ht_done"], 1)
                act.wait_ge(N["yb_out"], 16 * n + 16)
                act.wait_ge(N["y_ready"], 2 * n + 1)
                nc.scalar.activation(y_b[:, 0:512], d_ps[0], ACT.Copy).then_inc(N["y_taken_a"], 1)
            act.wait_ge(N["x3_done"], len(TILES))
            rms(stream, view(E0 + 3072, D))

        @block.vector
        def _(dve):
            line = Line(dve, N["v_step"])
            vm = Mail(*v_mail)
            V = nc.vector

            def tt(out, x, y, op, sem=None):
                line.do(V.tensor_tensor(out, x, y, op), sem)

            def ts(out, x, s1, s2, op0, op1=None, sem=None):
                line.do(V.tensor_scalar(out, x, s1, s2, op0) if op1 is None else V.tensor_scalar(out, x, s1, s2, op0, op1), sem)

            def stt(out, x, s, y, op0, op1, sem=None):
                line.do(V.scalar_tensor_tensor(out=out, in0=x, scalar=s, in1=y, op0=op0, op1=op1), sem)

            def cp(out, x, sem=None):
                line.do(V.tensor_copy(out, x), sem)

            def tell(s):
                dve.sem_inc(s, 1)

            def q4(bank, w=P):
                return bank[:, 0:4 * w].rearrange("p (a b) -> p a b", b=w)

            def last_dim(x, n):
                return x.unsqueeze(len(x.shape)).to_broadcast(list(x.shape) + [n])

            def mid(x, n):
                return x.unsqueeze(1).to_broadcast([x.shape[0], n, x.shape[1]])

            def rstd(n, col):
                line.do(V.reciprocal(stat[0:n, col:col + 1], stat[0:n, col:col + 1]))

            def rsqrt(x, part):
                tell(N["sq_ready"])
                dve.wait_ge(N["sq_done"], part)
                line.do(V.reciprocal(x, x))

            def turned(dst, t0, n, gain):
                for half in range(2):
                    bank = vm.take(dve)
                    tt(dst[:, 4 * half:4 * half + 4, t0:t0 + n], q4(bank)[:, :, 0:n],
                       last_dim(gains[:, gain, 4 * half:4 * half + 4], n), ALU.mult, vm.freed)

            cp(prm[:, 0:NPRM], vm.take(dve)[:, 0:NPRM], vm.freed)
            ts(omka, prm[:, KA:KA + 4], -1.0, 1.0, ALU.mult, ALU.add)
            for i in range(len(TILES) + 1):
                if i < len(TILES):
                    n = TILES[i][1]
                    dve.wait_ge(N["rms"], 1)
                    rstd(n, i)
                    ts(xs_tmp[i % 2][0:n], x_res[0:n, i, :], stat[0:n, i:i + 1], None, ALU.mult)
                    tell(N["xs3_done"])
                if i >= 1:
                    turned(x_t, *TILES[i - 1], 0)
                    tell(N["xt_done"])
            dve.wait_ge(N["qkv_raw"], 1)
            for i in range(len(TILES) + 1):
                if i < len(TILES):
                    n = TILES[i][1]
                    qk = qkv[0:n, i, 0:2 * BW].rearrange("p (h d) -> p h d", d=64)
                    x1, x2 = qk[:, :, 0:8], qk[:, :, 8:16]
                    co = mid(C("rope")[0:n, 16 * i:16 * i + 8], 24)
                    si = mid(C("rope")[0:n, 16 * i + 8:16 * i + 16], 24)
                    tt(rt[0][0:n], x1, co, ALU.mult)
                    tt(rt[1][0:n], x2, si, ALU.mult)
                    tt(rt[2][0:n], x2, co, ALU.mult)
                    tt(rt[3][0:n], x1, si, ALU.mult)
                    tt(x1, rt[0][0:n], rt[1][0:n], ALU.subtract)
                    tt(x2, rt[2][0:n], rt[3][0:n], ALU.add)
                    tell(N["rope_done"])
                if i >= 1:
                    t0, n = TILES[i - 1]
                    for half in range(3):
                        cp(qk_t[:, 4 * half:4 * half + 4, t0:t0 + n], q4(vm.take(dve))[:, :, 0:n], vm.freed)

            def mask_unit(u):
                i, h = att[u]
                kb = key_blocks(i)
                s = s_sb[u % 2]
                at_ = 0
                for g in range(NG):
                    k = len([1 for gg, _ in kb if gg == g])
                    bank = vm.take(dve)
                    if k > 1:
                        tt(s[:, at_:at_ + (k - 1) * P].rearrange("p (a b) -> p a b", b=P),
                           bank[:, 0:(k - 1) * P].rearrange("p (a b) -> p a b", b=P), mid(C(f"off{g}"), k - 1), ALU.add)
                    tt(s[:, at_ + (k - 1) * P:at_ + k * P], bank[:, (k - 1) * P:k * P], C(f"diag{g}"), ALU.add, vm.freed)
                    at_ += k * P
                c = 8 + 4 * (u % 2)
                line.do(V.reduce_max(stat[:, c:c + 1], s[:, 0:at_], AX))
                ts(stat[:, c + 1:c + 2], stat[:, c:c + 1], -0.125, None, ALU.mult, sem=N["p_neg"])

            def scale_unit(u):
                i, h = att[u]
                n = P * len(key_blocks(i))
                c = 8 + 4 * (u % 2)
                dve.wait_ge(N["p_exp"], u + 1)
                line.do(V.reciprocal(stat[:, c + 3:c + 4], stat[:, c + 2:c + 3]))
                ts(s_sb[u % 2][:, 0:n], s_sb[u % 2][:, 0:n], stat[:, c + 3:c + 4], None, ALU.mult, sem=N["p_ready"])

            for u in range(len(att) + 1):
                if u < len(att):
                    mask_unit(u)
                if u >= 1:
                    scale_unit(u - 1)
            dve.wait_ge(N["pv_taken"], len(att))
            line.do(V.memset(qblk, 0.0))
            for hh in range(2):
                lo = 64 * hh
                cp(qblk[lo:lo + 64, :, TS * hh:TS * hh + TS], qk_t[lo:lo + 64, 0:6, SEQ:T])
            tell(N["qblk_ready"])
            dve.wait_ge(N["kv_used"], len(units))
            cp(st_sb, aux[:, 0:NG * P].rearrange("p (a b) -> p a b", b=P))
            cp(stn_sb[0:TS], vm.take(dve)[0:TS, 0:NG * P].rearrange("p (a b) -> p a b", b=P), vm.freed)
            tell(N["snew"])
            tt(ps_sb, vm.take(dve)[:, 0:480], C("samp"), ALU.add, vm.freed)
            line.do(V.reduce_max(stat[:, 16:17], ps_sb, AX))
            ts(stat[:, 17:18], stat[:, 16:17], -0.125, None, ALU.mult, sem=N["sneg"])
            dve.wait_ge(N["sexp"], 1)
            line.do(V.reciprocal(stat[:, 19:20], stat[:, 18:19]))
            ts(ps_sb, ps_sb, stat[:, 19:20], None, ALU.mult, sem=N["s_soft"])
            cp(pts, vm.take(dve)[:, 0:NG * P].rearrange("p (a b) -> p a b", b=P), vm.freed)
            cp(ptn[0:TS], vm.take(dve)[0:TS, 0:NG * P].rearrange("p (a b) -> p a b", b=P), vm.freed)
            dve.wait_ge(N["kv_used"], 2 * len(units))
            for hh in range(2):
                lo = 64 * hh
                cp(yb_t[lo:lo + 64, :, SEQ:T], aux[lo:lo + 64, 0:P].rearrange("p (a b c) -> p a b c", b=2, c=TS)[:, :, hh, :])
            tell(N["yb_done"])
            for c in range(NA, NR):
                k = chunks[c][0][0].stop // P
                if c == NA:
                    dve.wait_ge(N["out"], 16 * OUT_CACHES)
                cp(u_s[:, 4 * (c - NA):4 * (c - NA) + k, :], vm.take(dve)[:, 0:k * TS].rearrange("p (a b) -> p a b", b=TS), vm.freed)
            dve.wait_ge(N["u_raw"], 1)
            tell(N["um_done"])
            for c in range(0, AJ, 4):
                w = P * min(4, AJ - c)
                cp(last_s[0:NB, c * P:c * P + w], vm.take(dve)[0:NB, 0:w], vm.freed)
                cp(last_p[0:1, c * P:c * P + w], vm.take(dve)[0:1, 0:w], vm.freed)
            tell(N["shift_ready"])
            us4 = u_s.rearrange("p j (b t) -> p j b t", t=NS)
            ums4 = um_s.rearrange("p j (b t) -> p j b t", t=NS)
            for c in range(0, AJ, 4):
                k = min(4, AJ - c)
                tt(ums4[:, c:c + k, :, 0], vm.take(dve)[:, 0:k * NB].rearrange("p (a b) -> p a b", b=NB), us4[:, c:c + k, :, 0],
                   ALU.subtract, vm.freed)
            for j in range(AJ):
                tt(ums4[:, j, :, 1:NS], us4[:, j, :, 0:NS - 1], us4[:, j, :, 1:NS], ALU.subtract)
                stt(um_s[:, j, :], um_s[:, j, :], prm[:, MU + j:MU + j + 1], u_s[:, j, :], ALU.mult, ALU.add)
            tell(N["um_done"])
            dve.wait_ge(N["shift_out"], 32)
            ts(um_p[:, :, 0:1], u_p[:, :, 0:1], -1.0, None, ALU.mult)
            tt(um_p[:, :, 1:SEQ], u_p[:, :, 0:SEQ - 1], u_p[:, :, 1:SEQ], ALU.subtract)
            for j in range(AJ):
                stt(um_p[:, j, :], um_p[:, j, :], prm[:, MU + j:MU + j + 1], u_p[:, j, :], ALU.mult, ALU.add)
            tell(N["um_done"])

            for part in range(2):
                n = TS if part == 0 else SEQ
                um, aa, kk, tmp, bon = (um_s, a_s, kk_s, tmp_s, bon_s) if part == 0 else (um_p, a_p, kk_p, tmp_p, bon_p)
                r, k, v = um[:, 0:4], um[:, 4:8], um[:, 8:12]
                tt(kk, k, last_dim(prm[:, KK_:KK_ + 4], n), ALU.mult)
                tt(tmp, kk, kk, ALU.mult, N["prep_sq"])
                for j in range(4):
                    ts(tmp[:, j], vm.take(dve)[:, 0:n], 1e-24, None, ALU.max, sem=vm.freed)
                rsqrt(tmp, part + 1)
                tt(kk, kk, tmp, ALU.mult)
                dve.wait_ge(N["sga"], part + 1)
                for j in range(4):
                    ts(tmp[:, j], aa[:, j], prm[:, KA + j:KA + j + 1], omka[:, j:j + 1], ALU.mult, ALU.add)
                tt(k, k, tmp, ALU.mult)
                tt(aa, aa, kk, ALU.mult)
                tt(tmp, r, k, ALU.mult)
                tt(tmp, tmp, last_dim(prm[:, RK:RK + 4], n), ALU.mult, N["prep_sq"])
                for j in range(4):
                    tt(bon[:, j], vm.take(dve)[:, 0:n], v[:, j], ALU.mult, vm.freed)
                if part == 0:
                    tell(N["prep_e"])
                    dve.wait_ge(N["exp_done"], 1)
                    tell(N["tm_done"])
                    for z in range(6):
                        cp(tok_s[0:TS, z, :], vm.take(dve)[0:TS, :], vm.freed)
                    tell(N["stm_done"])
            ts(sg_p, sg_p, -float(np.exp(np.float32(-0.5))), None, ALU.mult)
            for j in range(4):
                line.do(V.tensor_tensor_scan(c_p[:, j], C("reset"), sg_p[:, j], 0.0, ALU.mult, ALU.add))
            c16 = c_p.rearrange("p j (i t) -> p (j i) t", t=P)
            pm16 = pmid.rearrange("p a b -> p (a b)")
            cp(pm16, c16[:, :, P // 2 - 1])
            tt(c16, c16, last_dim(pm16, P), ALU.subtract)
            tt(sg_p, c_p, sg_p, ALU.subtract)
            tell(N["prep_e"])
            dve.wait_ge(N["exp_done"], 2)
            r, k = um_p[:, 0:4], um_p[:, 4:8]
            tt(r, r, tmp_p, ALU.mult)
            cp(pend.rearrange("p a b -> p (a b)"), tmp_p.rearrange("p j (i t) -> p (j i) t", t=P)[:, :, P - 1])
            stt(kk_p.rearrange("p a b -> p (a b)"), kk_p.rearrange("p a b -> p (a b)"), -1.0, sg_p.rearrange("p a b -> p (a b)"), ALU.mult, ALU.mult)
            tt(k, k, c_p, ALU.mult)
            tt(a_p, a_p, c_p, ALU.mult)
            tell(N["prep_done"])
            for dst in (tm_b, tm_k, tm_v):
                for i in range(NPT):
                    cp(dst[:, i, :], vm.take(dve)[:, :], vm.freed)
            line.do(V.memset(st0, 0.0))
            line.do(V.memset(st0m, 0.0))
            for i in range(NPT):
                for dst, mask, plus in ((mat_l, None, None), (mat_t, "low1t", 1), (mat_ak, "strict", 0), (mat_rb, "incl", 0), (mat_rk, "incl", 0)):
                    for par in range(2):
                        bank = vm.take(dve)
                        d4 = dst[:, 4 * par:4 * par + 4, :]
                        if mask is None:
                            cp(d4, q4(bank), vm.freed)
                        else:
                            tt(d4, q4(bank), mid(C(mask), 4), ALU.mult, vm.freed)
                            if plus:
                                tt(d4, d4, mid(ident, 4), ALU.add)
                tt(mat_tt, mat_l, mid(C("low1"), 8), ALU.mult)
                tt(mat_tt, mat_tt, mid(ident, 8), ALU.add)
                tt(mat_lm, mat_l, mid(C("low2"), 8), ALU.mult, N["lm_ready"])
                for lv, m in enumerate(LEVELS[1:]):
                    final = m == LEVELS[-1]
                    for par in range(2):
                        cp(mat_w[:, 4 * par:4 * par + 4, :], q4(vm.take(dve)), vm.freed)
                    if not final:
                        tt(mat_lm, mat_l, mid(C(f"low{2 * m}"), 8), ALU.mult, N["lm_ready"])
                    for par in range(2):
                        for dst in ((mat_t, mat_tt) if not final else (mat_tt,)):
                            d4 = dst[:, 4 * par:4 * par + 4, :]
                            tt(d4, d4, q4(vm.take(dve)), ALU.add, vm.freed)
                for par in range(2):
                    cp(w_sb[:, 4 * par:4 * par + 4, :], q4(vm.take(dve), 64), vm.freed)
                cp(uu_sb, vm.take(dve)[:, :].rearrange("p (a b) -> p a b", b=64), vm.freed)
                tt(st0, st0m, q4(vm.take(dve), 64), ALU.add, vm.freed)
                tt(st0, st0, last_dim(pend[:, :, i], 64), ALU.mult)
                dve.wait_ge(N["mats"], i + 1)
                if i + 1 < NPT:
                    tt(st0m, st0, last_dim(pmid[:, :, i + 1], 64), ALU.mult)
                tell(N["state_ready"])
            cp(fin_s[0:64], vm.take(dve)[0:64, :], vm.freed)
            tell(N["fin_ready"])
            cp(y_s, vm.take(dve)[:, 0:4 * TS].rearrange("p (a b) -> p a b", b=TS), vm.freed)
            dve.wait_ge(N["y_raw"], 1)
            for part in range(2):
                n = TS if part == 0 else SEQ
                y, tmp, bon, gg = (y_s, tmp_s, bon_s, g_s) if part == 0 else (a_p, tmp_p, bon_p, g_p)
                tell(N["ysq"])
                for j in range(4):
                    stt(y[:, j], vm.take(dve)[:, 0:n], -1.0 / AD, y[:, j], ALU.mult, ALU.add, vm.freed)
                tt(tmp, y, y, ALU.mult)
                tell(N["ysq"])
                for j in range(4):
                    ts(tmp[:, j], vm.take(dve)[:, 0:n], 1.0 / AD, LNX_EPS, ALU.mult, ALU.add, sem=vm.freed)
                rsqrt(tmp, part + 3)
                tt(y, y, tmp, ALU.mult)
                for j in range(4):
                    ts(y[:, j], y[:, j], prm[:, LG + j:LG + j + 1], prm[:, LB + j:LB + j + 1], ALU.mult, ALU.add)
                tt(y, y, bon, ALU.add)
                tt(y, y, gg, ALU.mult)
            tell(N["ya_done"])
            z = 0
            for j in range(KT):
                for t0, n in ((0, SEQ), (SEQ, TS)):
                    dve.wait_ge(N["sig_done"], z + 1)
                    tt(mg[:, 0:n], vm.take(dve)[:, 0:n], sg_a[:, t0:t0 + n], ALU.mult, vm.freed)
                    tt(m_t[:, j, t0:t0 + n], vm.take(dve)[:, 0:n], sg_b[:, t0:t0 + n], ALU.mult, vm.freed)
                    tt(m_t[:, j, t0:t0 + n], m_t[:, j, t0:t0 + n], mg[:, 0:n], ALU.add, N["gate_used"])
                    z += 1
            tell(N["merged"])

            def add_rows():
                for i, (t0, m) in enumerate(TILES):
                    for c in range(2):
                        x = x_res[0:m, i, c * 512:(c + 1) * 512]
                        tt(x, x, vm.take(dve)[0:m, :], ALU.add, vm.freed)

            add_rows()
            tell(N["x1_done"])
            def norm_turn(srcs, col0, gain, dst):
                for i in range(len(srcs) + 1):
                    if i < len(srcs):
                        x, t0, n = srcs[i]
                        dve.wait_ge(N["rms"], 2)
                        rstd(n, col0 + i)
                        ts(xs2[i % 2][0:n], x, stat[0:n, col0 + i:col0 + i + 1], None, ALU.mult)
                        tell(N["memx"])
                    if i >= 1:
                        turned(dst, srcs[i - 1][1], srcs[i - 1][2], gain)

            norm_turn([(mem_x[:, i, :], i * P, P) for i in range(2)], 0, 2, mem_t)
            for c in range(2):
                for i in range(2):
                    cp(mkv[:, i, c * 512:(c + 1) * 512], vm.take(dve)[:, :], vm.freed)
            tell(N["mkv_done"])
            for i in range(2):
                cp(mk_t[:, :, i * P:(i + 1) * P], q4(vm.take(dve)), vm.freed)
            norm_turn([(x_res[0:n, i, :], t0, n) for i, (t0, n) in enumerate(TILES)], 2, 1, x_t)
            for h in range(MH):
                for t0, n in ((0, SEQ), (SEQ, TS)):
                    cp(q_t[:, h, t0:t0 + n], vm.take(dve)[:, 0:n], vm.freed)
            MS = float(MD) ** -0.5
            nu = len(mem_units)

            def mem_mask(u):
                c = 20 + 4 * (u % 2)
                cp(ms_sb[u % 2], vm.take(dve)[:, 0:MEM], vm.freed)
                line.do(V.reduce_max(stat[:, c:c + 1], ms_sb[u % 2], AX))
                ts(stat[:, c + 1:c + 2], stat[:, c:c + 1], -MS, None, ALU.mult, sem=N["m_neg"])

            def mem_scale(u):
                c = 20 + 4 * (u % 2)
                dve.wait_ge(N["m_exp"], u + 1)
                line.do(V.reciprocal(stat[:, c + 3:c + 4], stat[:, c + 2:c + 3]))
                ts(ms_sb[u % 2], ms_sb[u % 2], stat[:, c + 3:c + 4], None, ALU.mult, sem=N["m_ready"])

            for u in range(nu + 1):
                if u < nu:
                    mem_mask(u)
                if u >= 1:
                    mem_scale(u - 1)
            dve.wait_ge(N["mkv_used"], NB)
            cp(mst, aux[:, 0:2 * P].rearrange("p (a b) -> p a b", b=P), N["mst_ready"])
            mem_mask(nu)
            mem_scale(nu)
            dve.wait_ge(N["mkv_used"], 2 * NB)
            cp(o_t[:, :, SEQ:T], aux[:, 0:MH * TS].rearrange("p (a b) -> p a b", b=TS), N["mo_done"])
            add_rows()
            tell(N["x2_done"])
            for i, (t0, n) in enumerate(TILES):
                dve.wait_ge(N["rms"], 3)
                rstd(n, i)
                if i == 0:
                    dve.wait_ge(N["mkv_out"], 32)
                ts(xs3[0:n, i, :], x_res[0:n, i, :], stat[0:n, i:i + 1], None, ALU.mult)
                tell(N["xs3_done"])
            ru = rs.bitcast(U32)
            dve.wait_ge(N["rb_in"], 32)
            for i, (t0, n) in enumerate(TILES):
                turned(x_t, t0, n, 3)
                z = slice(0, n)
                tt(lg[z], vm.take(dve)[z, 0:36], rbias[z], ALU.add, vm.freed)
                line.do(V.memset(rs[z, 0:8], 2 * NEG))
                cp(rs[z, 0:4], lg[z, 0:4])
                line.do(V.max(rs[z, 8:16], rs[z, 0:8]))
                line.do(V.max_index(ru[z, 16:24], rs[z, 8:16], rs[z, 0:8]))
                cp(rs[z, 30:31], ru[z, 16:17])
                ts(rs[z, 24:25], rs[z, 8:9], -1.0, None, ALU.mult)
                ts(rs[z, 32:64], C("grp")[z], rs[z, 30:31], None, ALU.is_equal)
                ts(rs[z, 64:96], rs[z, 32:64], -NEG, NEG, ALU.mult, ALU.add)
                tt(rs[z, 96:128], lg[z, 4:36], rs[z, 32:64], ALU.mult)
                tt(rs[z, 96:128], rs[z, 96:128], rs[z, 64:96], ALU.add)
                line.do(V.max(rs[z, 128:136], rs[z, 96:128]))
                line.do(V.max_index(ru[z, 136:144], rs[z, 128:136], rs[z, 96:128]))
                cp(rs[z, 144:146], ru[z, 136:138])
                for k in range(2):
                    ts(hot[z, i, NE * k:NE * k + NE], C("iota")[z], rs[z, 144 + k:145 + k], None, ALU.is_equal)
                tt(rs[z, 26:27], rs[z, 129:130], rs[z, 128:129], ALU.subtract)
                tell(N["route_a"])
                dve.wait_ge(N["route_e"], i + 1)
                ts(rs[z, 28:29], rs[z, 27:28], 1.0, None, ALU.add)
                tt(rs[z, 28:29], rs[z, 28:29], rs[z, 25:26], ALU.mult)
                line.do(V.reciprocal(gate[z, i, 0:1], rs[z, 28:29]))
                tt(gate[z, i, 1:2], gate[z, i, 0:1], rs[z, 27:28], ALU.mult)
            tell(N["hot_done"])
            bank = vm.take(dve)
            cnt, base, nblk = rs[:, 0:32], rs[:, 32:64], rs[:, 64:96]
            cp(cnt, bank[:, 0:NE])
            tt(cnt, cnt, bank[:, NE:2 * NE], ALU.add, vm.freed)
            one = C("ones")[:, 0:NE]
            line.do(V.tensor_tensor_scan(base, one, cnt, 0.0, ALU.mult, ALU.add))
            tt(base, base, cnt, ALU.subtract)
            tt(cnt3, last_dim(cnt, MAXBLK - 1), mid(C("thr"), NE), ALU.is_gt)
            line.do(V.reduce_sum(nblk, cnt3, AX))
            ts(nblk, nblk, 1.0, None, ALU.add)
            first_ = rs[:, 96:128]
            line.do(V.tensor_tensor_scan(first_, one, nblk, 0.0, ALU.mult, ALU.add))
            cp(tab_i[:, TOTAL:TOTAL + 1], first_[:, NE - 1:NE])
            tt(first_, first_, nblk, ALU.subtract)
            cp(tab_i[:, FIRST:FIRST + NE], first_)
            cp(tab_i[:, COUNT:COUNT + NE], nblk)
            tt(row3, mid(first_, NTAB), last_dim(C("count"), NE), ALU.is_gt)
            stt(nblk, first_, -float(BLK), base, ALU.mult, ALU.add)
            stt(row3, row3, 1e6, mid(nblk, NTAB), ALU.mult, ALU.add)
            line.do(V.tensor_reduce(rs[:, 128:128 + NTAB], row3, AX, ALU.min))
            stt(rs[:, 128:128 + NTAB], C("count"), float(BLK), rs[:, 128:128 + NTAB], ALU.mult, ALU.add)
            ts(tab_i[:, ROW:ROW + NTAB], rs[:, 128:128 + NTAB], float(ROWS), None, ALU.min)
            tell(N["tab_ready"])
            for i, (t0, n) in enumerate(TILES):
                z = slice(0, n)
                bank = vm.take(dve)
                tt(rs[z, 128:160], bank[z, 0:NE], base[z], ALU.add)
                tt(rs[z, 128:160], rs[z, 128:160], bank[z, NE:2 * NE], ALU.add, vm.freed)
                for k in range(2):
                    tt(rs[z, 160:192], rs[z, 128:160], hot[z, i, NE * k:NE * k + NE], ALU.mult)
                    line.do(V.reduce_sum(slot_f[z, 2 * i + k:2 * i + k + 1], rs[z, 160:192], AX))
                cp(slot_i[z, 2 * i:2 * i + 2], slot_f[z, 2 * i:2 * i + 2])
            tell(N["route_done"])
            def take_block():
                for half in range(2):
                    k = slice(4 * half, 4 * half + 4)
                    last = V.tensor_tensor(x_e[:, k, :], x_ps[half].rearrange("p (a b) -> p a b", b=BLK), last_dim(gains[:, 3, k], BLK), ALU.mult)
                last.then_inc(N["xe_ready"], 1)

            dve.wait_ge(N["scattered"], 16 * 2 * len(TILES))
            dve.wait_ge(N["xb_used"], 1)
            take_block()
            total = dve.value_load(tab_i[0:1, TOTAL:TOTAL + 1], min_val=NE, max_val=ALLBLK)
            with dve.Fori(0, total) as n:
                dve.wait_ge(N["silu_done"], n + 1)
                dve.wait_ge(N["u_full"], n + 1)
                V.tensor_tensor(h_b, h_sg, u_ps, ALU.mult).then_inc(N["h_done"], 1)
                dve.wait_ge(N["xb_used"], n + 2)
                take_block()
                dve.wait_ge(N["yb_out"], 16 * n + 16)
                dve.wait_ge(N["y_ready"], 2 * n + 2)
                V.tensor_copy(y_b[:, 512:1024], d_ps[1]).then_inc(N["y_taken_v"], 1)
            for i, (t0, n) in enumerate(TILES):
                for k in range(2):
                    dve.wait_ge(N["yg_in"], 16 * 2 * len(TILES))
                    stt(x_res[0:n, i, :], yg[2 * i + k][0:n], gate[0:n, i, k:k + 1], x_res[0:n, i, :], ALU.mult, ALU.add, N["yg_used"])
                tell(N["x3_done"])
            dve.wait_ge(N["gfin_in"], 16)
            for i, (t0, n) in enumerate(TILES):
                dve.wait_ge(N["rms"], 4)
                rstd(n, i)
                stt(x_res[0:n, i, :], x_res[0:n, i, :], stat[0:n, i:i + 1], gfin[0:n], ALU.mult, ALU.mult)
                tell(N["y_final"])

        @block.gpsimd
        def _(pool):
            line = Line(pool, N["pool_step"])
            G = nc.gpsimd

            def tt(out, x, y, op):
                line.do(G.tensor_tensor(out, x, y, op))

            for g, (window, _) in enumerate(GROUPS):
                for b in range(NB):
                    src = caches[g][b, :, NS:window].rearrange("k (r q) h d -> k r (q h d)", q=NS)
                    dst = o[f"s_cache{g}"][b, :, 0:window - NS].rearrange("k (r q) h d -> k r (q h d)", q=NS)
                    pool.dma_start(dst, src).then_inc(N["copies"], 16)
            pool.wait_ge(N["shift_ready"], 1)
            pool.dma_start(o["s_shift"][:, :], last_s[0:NB, :]).then_inc(N["shift_out"], 16)
            pool.dma_start(o["p_shift"][:, :], last_p[0:1, :]).then_inc(N["shift_out"], 16)
            pool.wait_ge(N["srec_in"], 16 * 2 * (6 * NB + 1))
            line.do(G.memset(rec_sa[:, 0, :], 0.0))
            for t in range(NS):
                def vec(n):
                    return rec[:, n, t * 64:(t + 1) * 64].unsqueeze(1).to_broadcast([P, 32, 64])

                def val(x):
                    return x.unsqueeze(2).to_broadcast([P, 32, 64])

                def row_sums(dst, src):
                    w = 32
                    while w >= 1:
                        last = dst.unsqueeze(2) if w == 1 else src[:, :, 0:w]
                        tt(last, src[:, :, 0:w], src[:, :, w:2 * w], ALU.add)
                        w //= 2

                tt(rec_t, rec_s, vec(2), ALU.mult)
                row_sums(rec_sa[:, 0, :], rec_t)
                tt(rec_s, rec_s, vec(4), ALU.mult)
                tt(rec_t, val(rec_sa[:, 0, :]), vec(3), ALU.mult)
                tt(rec_s, rec_s, rec_t, ALU.subtract)
                tt(rec_t, val(rec_v[:, t, :]), vec(1), ALU.mult)
                tt(rec_s, rec_s, rec_t, ALU.add)
                tt(rec_t, rec_s, vec(0), ALU.mult)
                row_sums(rec_y[:, t, :], rec_t)
            for hf in range(2):
                rows = slice(hf * 64, (hf + 1) * 64)
                dst = o["s_rwkv"].rearrange("b h (f v) k -> (b h) f (v k)", f=2)[:, hf]
                pool.dma_start(dst, rec_s[rows].rearrange("p v k -> p (v k)")).then_inc(N["state_out"], 16)
                for b in range(NB):
                    r8 = slice(hf * 64 + b * AH, hf * 64 + (b + 1) * AH)
                    dst = yrec_d[b * NS:(b + 1) * NS, :].rearrange("t (h f k) -> h f t k", h=AH, f=2)[:, hf]
                    pool.dma_start(dst, rec_y[r8]).then_inc(N["yrec_out"], 16)
            pool.wait_ge(N["yrec_out"], 16 * 2 * NB)
            pool.dma_start(y_tok[0:TS, :], yrec_d[:, :]).then_inc(N["yrec_in"], 16)
            pool.wait_ge(N["state_out"], 32)
            pool.wait_ge(N["ya_done"], 1)
            pool.sem_inc(N["ring_spare"], 1)
            pool.wait_ge(N["fin_ready"], 1)
            pool.dma_start(o["p_rwkv"][0].rearrange("h v k -> v h k"), fin_s[0:64].rearrange("p (h k) -> p h k", k=64))\
                .then_inc(N["state_out"], 16)
            pool.wait_ge(N["mkv_done"], 1)
            for i in range(2):
                pool.dma_start(o["p_mem"][0, :, i * P:(i + 1) * P].rearrange("k p h d -> p k (h d)"),
                               mkv[:, i, :].rearrange("p (k c) -> p k c", k=2)).then_inc(N["mkv_out"], 16)
            pool.wait_ge(N["x2_done"], 1)
            line.do(G.memset(xb, 0.0))
            pool.dma_start(xs_d[ROWS:ROWS + BLK, :], xb).then_inc(N["pad_out"], 16)
            pool.dma_start(ys_d[ROWS:ROWS + BLK, :], xb).then_inc(N["yb_out"], 16)
            pool.dma_start(rbias[:, 0:4], a["b_router_group"].partition_broadcast(P)).then_inc(N["rb_in"], 16)
            pool.dma_start(rbias[:, 4:36], a["b_router_expert"].partition_broadcast(P)).then_inc(N["rb_in"], 16)
            pool.wait_ge(N["route_done"], 1)
            for i, (t0, n) in enumerate(TILES):
                for k in range(2):
                    pool.indirect_dma_start(out=xs_d[0:ROWS, :], out_offset=bass.IndirectOffsetOnAxis(ap=slot_i[0:n, 2 * i + k:2 * i + k + 1], axis=0),
                                            in_=xs3[0:n, i, :], in_offset=None, bounds_check=ROWS - 1).then_inc(N["scattered"], 16)
            pool.wait_ge(N["scattered"], 16 * 2 * len(TILES))
            pool.wait_ge(N["pad_out"], 16)
            pool.wait_ge(N["yb_out"], 16)
            row0 = pool.value_load(tab_of(ROW, 0), min_val=0, max_val=ROWS)
            pool.dma_start(xb, xs_d[bass.ds(row0, BLK), :]).then_inc(N["xb_in"], 16)
            total = pool.value_load(tab_i[0:1, TOTAL:TOTAL + 1], min_val=NE, max_val=ALLBLK)
            with pool.Fori(0, total) as n:
                row = pool.value_load(tab_of(ROW, n), min_val=0, max_val=ROWS)
                ahead = pool.value_load(tab_of(ROW, n + 1), min_val=0, max_val=ROWS)
                pool.wait_ge(N["xb_used"], n + 1)
                pool.sem_inc(N["seen"], 1)
                pool.dma_start(xb, xs_d[bass.ds(ahead, BLK), :]).then_inc(N["xb_in"], 16)
                pool.wait_ge(N["y_taken_a"], n + 1)
                pool.wait_ge(N["y_taken_v"], n + 1)
                pool.wait_ge(N["yb_out"], 16 * n + 16)
                pool.sem_inc(N["seen"], 1)
                pool.dma_start(ys_d[bass.ds(row, BLK), :], y_b).then_inc(N["yb_out"], 16)
            pool.wait_ge(N["yb_out"], 16 * total + 16)
            pool.sem_inc(N["seen"], 1)
            pool.wait_ge(N["exp_used"], NE)
            pool.dma_start(gfin, a["norm_final_g"].partition_broadcast(P)).then_inc(N["gfin_in"], 16)
            for i, (t0, n) in enumerate(TILES):
                for k in range(2):
                    pool.indirect_dma_start(out=yg[2 * i + k][0:n], out_offset=None, in_=ys_d[0:ROWS, :],
                                            in_offset=bass.IndirectOffsetOnAxis(ap=slot_i[0:n, 2 * i + k:2 * i + k + 1], axis=0),
                                            bounds_check=ROWS - 1).then_inc(N["yg_in"], 16)
            for i, (t0, n) in enumerate(TILES):
                pool.wait_ge(N["y_final"], i + 1)
                dst = o["y_prompt"][0, t0:t0 + n, :] if t0 < SEQ else o["y_sample"].rearrange("b t d -> (b t) d")
                pool.dma_start(dst, x_res[0:n, i, :]).then_inc(N["y_out"], 16)
            pool.wait_ge(N["y_out"], 16 * len(TILES))
            pool.wait_ge(N["copies"], 16 * NG * NB)
            pool.wait_ge(N["shift_out"], 32)
            pool.wait_ge(N["state_out"], 48)
            pool.wait_ge(N["mkv_out"], 32)


_INS = ['x_prompt', 'x_sample', 'state_rwkv', 'state_shift', 'cache_swa_w128', 'cache_swa_w512', 'cache_swa_w2048',
        'cache_mem_kv', 'mem_prompt', 'norm_mix_g', 'w_in', 'b_gate', 'rwkv_mu', 'rwkv_w0', 'rwkv_w2', 'rwkv_a0', 'rwkv_a2',
        'rwkv_g2', 'rwkv_k_k', 'rwkv_k_a', 'rwkv_r_k', 'rwkv_lnx_g', 'rwkv_lnx_b', 'w_branch_a', 'w_branch_b', 'w_out',
        'norm_mem_g', 'norm_memkv_g', 'w_mem_q', 'w_mem_kv', 'w_mem_out', 'norm_ffn_g', 'w_router_group', 'b_router_group',
        'w_router_expert', 'b_router_expert', 'w_exp_gate', 'w_exp_up', 'w_exp_down', 'norm_final_g']
_OUTS = [('y_prompt', (1, SEQ, D)), ('y_sample', (NB, NS, D)), ('p_rwkv', (1, AH, AD, AD)), ('p_shift', (1, APROJ)),
         ('p_cache0', (1, 2, 128, 4, 64)), ('p_cache1', (1, 2, 512, 4, 64)), ('p_cache2', (1, 2, 512, 4, 64)),
         ('p_mem', (1, 2, MEM, MH, MD)), ('s_rwkv', (NB, AH, AD, AD)), ('s_shift', (NB, APROJ)),
         ('s_cache0', (NB, 2, 128, 4, 64)), ('s_cache1', (NB, 2, 512, 4, 64)), ('s_cache2', (NB, 2, 2048, 4, 64))]


def kernel(**inputs):
    import concourse.bacc as _bacc
    from concourse.bass_utils import run_bass_kernel_spmd as _run

    nc = _bacc.Bacc("TRN2", target_bir_lowering=False, num_devices=1)
    arrays, ins, outs = {}, {}, {}
    for name in _INS:
        x = np.ascontiguousarray(inputs[name])
        arrays[f"in_{name}"] = x
        ins[name] = nc.dram_tensor(f"in_{name}", x.shape, mybir.dt.from_np(x.dtype), kind="ExternalInput").ap()
    table = np.concatenate(list(constants().values()), axis=1)
    arrays["constants"] = table
    cst = nc.dram_tensor("constants", table.shape, F32, kind="ExternalInput").ap()
    for name, shape in _OUTS:
        outs[name] = nc.dram_tensor(f"out_{name}", shape, F32, kind="ExternalOutput").ap()
    build(nc, ins, outs, cst)
    r = _run(nc, [arrays], core_ids=[0])
    return tuple(r.results[0][f"out_{name}"] for name, _ in _OUTS)
```

```python
from contextlib import ExitStack

import numpy as np
import concourse.bass as bass
from concourse import mybir

F32 = mybir.dt.float32
I32 = mybir.dt.int32
U32 = mybir.dt.uint32
ALU = mybir.AluOpType
ACT = mybir.ActivationFunctionType
AX = mybir.AxisListType.X

P = 128
D = 1024
KT = D // P
SEQ = 512
NB = 8
NS = 4
TS = NB * NS
T = SEQ + TS
TILES = [(i * P, P) for i in range(SEQ // P)] + [(SEQ, TS)]
HALVES = [(0, T // 2), (T // 2, T // 2)]
NPT = SEQ // P
PAST = 2048
AH, AD = 8, 64
AW = AH * AD
APROJ = 3 * AW + 64 + 64 + 128
AJ = APROJ // P
GROUPS = ((128, 1), (512, 4), (2048, 16))
NG = len(GROUPS)
BW = 4 * NG * 64
BPROJ = 3 * BW
MEM = 256
MH, MD = 4, 128
MW = MH * MD
NE, NGR, EPG = 32, 4, 8
FF = 512
EPS = 1e-6
LNX_EPS = 64e-5
NEG = -1e30
BLK = P
ROWS = 2 * T
MAXBLK = -(-T // BLK)
ALLBLK = NE + ROWS // BLK
NTAB = ALLBLK + 1
LEVELS = (1, 2, 4, 8, 16, 32, 64)


def constants():
    q, k = np.arange(P)[:, None], np.arange(P)[None, :]
    out = {}

    def put(name, a):
        out[name] = np.ascontiguousarray(np.broadcast_to(a, (P, a.shape[-1])), dtype=np.float32)

    put("ident", (q == k) * 1.0)
    put("ones", np.ones((P, P)))
    put("blk", (q // AD == k // AD) * 1.0)
    put("strict", (q < k) * 1.0)
    put("incl", (q <= k) * 1.0)
    for m in LEVELS:
        put(f"low{m}", ((q // (2 * m) == k // (2 * m)) & ((k // m) % 2 == 1) & ((q // m) % 2 == 0)) * 1.0)
    put("low1t", ((q // 2 == k // 2) & (q % 2 == 1) & (k % 2 == 0)) * 1.0)
    put("off0", np.where(k >= q, 0, NEG))
    put("diag0", np.where(k <= q, 0, NEG))
    for g in (1, 2):
        dil = GROUPS[g][1]
        put(f"off{g}", np.where((q - k) % dil == 0, 0, NEG))
        put(f"diag{g}", np.where(((q - k) % dil == 0) & (k <= q), 0, NEG))
    tok = np.arange(P) % TS
    b, t = tok // NS, tok % NS
    nb, nt = np.arange(TS) // NS, np.arange(TS) % NS
    cached = [np.where(k >= t[:, None], 0, NEG), np.zeros((P, P)), np.zeros((P, P))]
    same = b[:, None] == nb[None, :]
    new = [np.where(same & (nt[None, :] <= t[:, None]), 0, NEG)] + [np.where(same & (nt[None, :] == t[:, None]), 0, NEG)] * 2
    put("samp", np.concatenate(cached + new, axis=1))
    put("spread", (q % 32 == np.where(k < AD, 0, 31)) * 1.0)
    half = 8
    inv = (np.float32(500000.0) ** (-np.arange(half, dtype=np.float32) * np.float32(2.0) / np.float32(16))).astype(np.float32)
    rope = np.zeros((P, len(TILES), 2 * half), np.float32)
    for i, (t0, n) in enumerate(TILES):
        pos = np.arange(t0, t0 + n) if t0 < SEQ else PAST + np.arange(TS) % NS
        ang = pos.astype(np.float32)[:, None] * inv[None, :]
        rope[:n, i, :half], rope[:n, i, half:] = np.cos(ang), np.sin(ang)
    put("rope", rope.reshape(P, -1))
    put("iota", np.arange(NE)[None, :] * 1.0)
    put("grp", (np.arange(NE) // EPG)[None, :] * 1.0)
    put("eps", np.full((1, 1), EPS))
    put("count", np.arange(NTAB)[None, :] * 1.0)
    put("thr", (BLK * (1 + np.arange(MAXBLK - 1)))[None, :] * 1.0)
    return out


def const_layout():
    at, n = {}, 0
    for name, a in constants().items():
        at[name] = (n, a.shape[1])
        n += a.shape[1]
    return at, n


class Mail:

    def __init__(self, banks, filled, freed):
        self.banks, self.filled, self.freed = banks, filled, freed
        self.put = self.got = 0

    def claim(self, pe):
        if self.put >= len(self.banks):
            pe.wait_ge(self.freed, self.put - len(self.banks) + 1)
        self.put += 1
        return self.banks[(self.put - 1) % len(self.banks)]

    def take(self, eng):
        eng.wait_ge(self.filled, self.got + 1)
        self.got += 1
        return self.banks[(self.got - 1) % len(self.banks)]


class Line:

    def __init__(self, eng, step):
        self.eng, self.step, self.n = eng, step, {}

    def do(self, ins, sem=None):
        key = sem or self.step
        ins.then_inc(key, 1)
        self.n[key.name] = self.n.get(key.name, 0) + 1
        self.eng.wait_ge(key, self.n[key.name])

    def count(self, ins, sem):
        ins.then_inc(sem, 1)
        self.n[sem.name] = self.n.get(sem.name, 0) + 1


def build(nc, a, o, cst):
    with ExitStack() as ctx:
        def sem(name):
            return ctx.enter_context(nc.semaphore(name))

        CL, NC = const_layout()
        cols = (nc.sbuf_usable_end - nc.sbuf_base) // 4 // 16 * 16 - 16
        arena = ctx.enter_context(nc.sbuf_tensor("arena", [P, cols], F32))
        top = [0]

        def at(n):
            top[0] += n
            return top[0] - n

        def view(off, *shape):
            n = int(np.prod(shape))
            v = arena[:, off:off + n]
            if len(shape) == 2:
                v = v.rearrange("p (a b) -> p a b", b=shape[1])
            if len(shape) == 3:
                v = v.rearrange("p (a b c) -> p a b c", b=shape[1], c=shape[2])
            return v

        con = view(at(NC), NC)
        x_res = view(at(5 * D), 5, D)
        x_t = view(at(KT * T), KT, T)
        prm = view(at(64), 64)
        gains = view(at(4 * KT), 4, KT)
        omka = view(at(4), 4)
        lora = view(at(2 * AW), 2, AW)
        wr = view(at(KT * 36), KT, 36)
        yb_t = view(at(2 * T), 2, T)
        stat = view(at(64), 64)
        ring_at = at(2 * 4096)
        ring = [view(ring_at + 4096 * s, KT, 512) for s in range(2)]
        AR = top[0]

        def C(name):
            n, w = CL[name]
            return con[:, n:n + w]

        ident = C("ident")
        MU, W0, A0, KK_, KA, RK, LG, LB, BG = 0, 14, 18, 22, 26, 30, 34, 38, 42
        NPRM = 58

        qkv = view(AR, 5, BPROJ)
        qk_t = view(AR + 5 * BPROJ, 12, T)
        rt = [view(AR + 5 * BPROJ + 12 * T + 192 * n, 24, 8) for n in range(4)]
        s0 = AR + 5 * BPROJ + 12 * T + 768
        s_sb = [view(s0 + c, 1280) for c in (0, 1280, 8320)]
        p_t = [view(s0 + 2560 + 1280 * n, 10, P) for n in range(2)]
        kvb = [view(s0 + 5120 + 1024 * n, 4, 256) for n in range(3)]
        row_b = view(s0 + 5120 + 3072, P)
        assert s0 + 8320 + 1280 <= cols, (s0, cols)
        xs_tmp = [view(s0 + 1024 * n, D) for n in range(2)]
        kt_s = [view(s0 + 1280 + 1024 * n, 8, P) for n in range(2)]
        qblk = view(s0 + 3400, NG * 2, 64)
        st_sb = view(s0 + 3800, NG, P)
        stn_sb = view(s0 + 4200, NG, P)
        ps_sb = view(s0, 480)
        pts = view(s0 + 512, NG, P)
        ptn = view(s0 + 896, NG, P)

        U = AR
        u_p, u_s = view(U, AJ, SEQ), view(U + 7168, AJ, TS)
        UM = AR + 7616
        um_p, um_s = view(UM, AJ, SEQ), view(UM + 7168, AJ, TS)
        SL = UM + 7616
        a_p, kk_p, sg_p, c_p, g_p, bon_p = (view(SL + 2048 * n, 4, SEQ) for n in range(6))
        sq_p = bon_p
        SM = SL + 6 * 2048
        tmp_p, tm_b, tm_k = (view(U + 2048 * n, 4, SEQ) for n in range(3))
        tm_v = sg_p
        mat_l, mat_t = view(SL + 3 * 2048, 8, P), view(SL + 3 * 2048 + 1024, 8, P)
        mat_tt, mat_lm, mat_w = (view(UM + 4096 + 1024 * n, 8, P) for n in range(3))
        mat_rb, mat_rk, mat_ak = view(U, 8, P), view(U + 1024, 8, P), view(U + 6144, 8, P)
        w_sb, uu_sb = view(SM, 8, 64), view(SM + 512, 8, 64)
        st0, st0m = view(SM + 1024, 4, 64), view(SM + 1280, 4, 64)
        pmid, pend = view(SM + APROJ + 14, 4, 4), view(SM + APROJ + 30, 4, 4)
        assert SM + APROJ + 46 <= cols, (SM, cols)
        R0 = ring_at
        a_s, kk_s, dec_s, g_s, bon_s, tmp_s = (view(R0 + 128 * n, 4, TS) for n in range(6))
        inv = view(SM + 1024, SEQ)
        y_s = view(SM, 4, TS)
        rec = view(R0 + 1024, 5, NS * 64)
        rec_v, rec_y, rec_sa = (view(R0 + 2304 + 128 * n, NS, 32) for n in range(3))
        tok_s = view(R0 + 4096, 6, AW)
        rec_s, rec_t = view(R0 + 4096, 32, 64), view(R0 + 6144, 32, 64)
        y_tok = view(R0 + 2752, AW)

        wa, wb = view(U + 2048, 4, D), view(UM + KT * T + 256, 2, D)
        m_t = view(UM, KT, T)
        y_all = view(SL + 2048, 4, T)
        gate_sb = [view(SL + 2048 + (4 + 2 * n) * T, 2, T) for n in range(3)]
        mg = view(SL + 2048 + 10 * T, T)
        Z = AR
        mem_x = view(Z, 2, D)
        mem_t = view(Z + 2048, KT, MEM)
        mkv = view(Z + 4096, 2, 2 * MW)
        mk_t = view(Z + 6144, MH, MEM)
        q_t = view(Z + 7168, MH, T)
        o_t = view(Z + 9344, MH, T)
        ms_sb = [view(Z + c, 256) for c in (11520, 11776, 22100)]
        mp_t = [view(Z + 12032 + 256 * n, 2, P) for n in range(2)]
        mks = [view(Z + 12544 + 1024 * n, 2, MW) for n in range(2)]
        mvs = [view(Z + 14592 + 1024 * n, 2, MW) for n in range(2)]
        mkt_s = [view(Z + 16640 + 1024 * n, 8, P) for n in range(2)]
        mst = view(Z + 18688, 2, P)
        xs2 = [view(Z + 19000 + 1024 * n, D) for n in range(2)]
        wg = [view(ring_at, KT, FF), view(Z, KT, FF)]
        wu = [view(ring_at + 4096, KT, FF), view(Z + 4096, KT, FF)]
        wd = [view(Z + 8192, 4, D), view(Z + 12288, 4, D)]
        E0 = Z + 16384
        xs3 = view(E0, 5, D)
        x_e = view(E0, KT, BLK)
        h_sg, h_b, h_t = view(E0 + 1024, FF), view(E0 + 1536, FF), view(E0 + 2048, 4, BLK)
        xb = view(E0 + 5120, D)
        y_b = view(E0 + 6144, D)
        hot = view(E0 + 7168, 5, 2 * NE)
        slot_f = view(E0 + 7488, 10)
        slot_i = view(E0 + 7498, 10).bitcast(U32)
        gate = view(E0 + 7508, 5, 2)
        lg = view(E0 + 7520, 36)
        rbias = view(E0 + 7556, 36)
        rs = view(E0 + 7592, 200)
        tab_i = view(E0 + 7792, 2 * NE + NTAB + 1).bitcast(I32)
        cnt3 = view(E0 + 7920, NE, MAXBLK - 1)
        row3 = view(E0 + 8080, NTAB, NE)
        yg = [view(Z + D * n, D) for n in range(2 * len(TILES))]
        gfin = view(Z + 10 * D, D)
        assert E0 + 8080 + NTAB * NE <= cols, (E0, cols)
        shift_rows = view(SL + 3 * 2048, APROJ)
        last_s = view(SM, APROJ)
        last_p = view(SM, P)[64:64 + AJ]
        u_last = view(SM + APROJ, AJ)
        fin_s = view(SM + 512, AW)
        OUT_CACHES = sum(2 * (min(w, SEQ) // P) for w, _ in GROUPS) + 2 * NB * NG

        def tab_of(part, e):
            return tab_i[0:1, bass.ds(part + e, 1)]

        srec_d = nc.dram_tensor("scratch_sample_vectors", [6, TS, AW], F32).ap()
        yrec_d = nc.dram_tensor("scratch_sample_y", [TS, AW], F32).ap()
        xs_d = nc.dram_tensor("scratch_rows_by_expert", [ROWS + BLK, D], F32).ap()
        ys_d = nc.dram_tensor("scratch_expert_rows", [ROWS + BLK, D], F32).ap()

        banks = [ctx.enter_context(nc.psum_tensor(f"bank{n}", [P, 512], F32))[:, :] for n in range(8)]
        v_mail = (banks[0:4], sem("v_filled"), sem("v_freed"))
        a_mail = (banks[4:7], sem("a_filled"), sem("a_freed"))
        aux = banks[7]

        N = {n: sem(n) for n in (
            "pe_step", "v_step", "act_step", "pool_step",
            "con_in", "x_in", "prm_in", "small_in", "prm_rows",
            "ring_used", "ring_spare", "qkv_raw", "rope_done", "xt_done",
            "p_neg", "p_exp", "p_ready", "pv_full", "pv_taken", "yb_done",
            "kv_used", "st_full", "qblk_ready", "snew", "s_soft", "sneg", "sexp",
            "um_done", "lora_in", "sga", "prep_sq", "prep_e", "exp_done", "prep_done", "stm_done",
            "lm_ready", "mats", "w_ready", "u_ready", "state_ready", "tm_done",
            "srec_out", "srec_out2", "srec_in", "rec_done", "yrec_out", "yrec_in", "ysq", "ya_done", "inv_ready",
            "br_free", "br_in", "sig_done", "merged", "x1_done",
            "mem_in", "memx", "mkv_done", "mkv_out", "mq_done", "m_neg", "m_exp", "m_ready", "mo_done",
            "mkv_used", "mst_ready", "x2_done", "hot_done", "route_done", "xs3_done", "scattered", "pad_in", "pad_out",
            "e_area", "exp_used", "xb_in", "xb_used", "h_sig", "h_done", "yb_out", "y_ready", "yg_in", "yg_used",
            "y_final", "out", "copies", "shift_out", "tab_ready", "ssq", "state_in", "state_out", "gfin_in", "rb_in", "xe_ready",
            "shift_in", "u_raw", "y_raw", "gate_used", "route_a", "route_e", "silu_done", "x3_done", "y_taken", "y_out",
            "shift_ready", "fin_ready", "g_full", "u_full", "ht_full", "ht_done", "y_taken_a", "y_taken_v", "rms", "sq_ready", "sq_done", "seen")}
        ring_in = [sem(f"ring_in{s}") for s in range(2)]
        kv_in = [sem(f"kv_in{s}") for s in range(3)]
        mks_in = [sem(f"mks_in{s}") for s in range(2)]
        mvs_in = [sem(f"mvs_in{s}") for s in range(2)]
        w_in_sem = [sem(f"expert_weights_in{s}") for s in range(2)]
        yg_in = [sem(f"yg_in{s}") for s in range(2)]
        wexp_in = [sem(f"wexp_in{s}") for s in range(2)]

        w_in = a["w_in"].rearrange("(p kt) c -> p kt c", kt=KT)
        w_out = a["w_out"].rearrange("(kt p) c -> p kt c", p=P)
        GATE = APROJ + BPROJ
        chunks = []
        for c in range(0, BPROJ, 512):
            w = min(512, BPROJ - c)
            chunks.append([(slice(0, w), w_in[:, :, APROJ + c:APROJ + c + w])])
        NA = len(chunks)
        feats = []
        for c in (3 * AW, AW, 0, 2 * AW):
            w = min(512, APROJ - c)
            chunks.append([(slice(0, w), w_in[:, :, c:c + w])])
            feats.append(list(range(c // P, (c + w) // P)))
        NR = len(chunks)
        for q in range(4):
            chunks.append([(slice(0, 256), w_in[:, :, GATE + 256 * q:GATE + 256 * q + 256]),
                           (slice(256, 512), w_in[:, :, GATE + D + 256 * q:GATE + D + 256 * q + 256])])
        NGT = len(chunks)
        for c in range(2):
            chunks.append([(slice(0, 512), w_out[:, :, 512 * c:512 * c + 512])])
        NO = len(chunks)
        mkv_w = a["w_mem_kv"].rearrange("(p kt) c -> p kt c", kt=KT)
        for c in range(2):
            chunks.append([(slice(0, 512), mkv_w[:, :, 512 * c:512 * c + 512])])
        NM = len(chunks)
        chunks.append([(slice(0, 512), a["w_mem_q"].rearrange("(p kt) c -> p kt c", kt=KT))])
        chunks.append([(None, a["w_mem_out"].rearrange("(h p) d -> p h d", p=P))])
        loaded = []
        tot = [0, 0]
        for n, ch in enumerate(chunks):
            tot[n % 2] += 16 * len(ch)
            loaded.append(tot[n % 2])

        caches = (a["cache_swa_w128"], a["cache_swa_w512"], a["cache_swa_w2048"])
        units = [(g, b) for g in range(NG) for b in range(NB)]
        wide = [1, NS, NS]
        att = [(i, h) for i in range(NPT) for h in range(4)]

        def key_blocks(i):
            return [(0, j) for j in range(max(0, i - 1), i + 1)] + [(g, j) for g in (1, 2) for j in range(i + 1)]

        FIRST, COUNT, ROW, TOTAL = 0, NE, 2 * NE, 2 * NE + NTAB
        g_ps, u_ps, x_ps, h_ps, d_ps = banks[0], banks[1], banks[2:4], banks[4], banks[5:7]
        mem_units = [(i, h) for i in range(NPT) for h in range(MH)]
        block = ctx.enter_context(nc.Block())

        @block.sync
        def _(sp):
            sp.dma_start(con, cst[:, :]).then_inc(N["con_in"], 16)
            for i, (t0, n) in enumerate(TILES):
                src = a["x_prompt"][0, t0:t0 + n, :] if t0 < SEQ else a["x_sample"].rearrange("b t d -> (b t) d")
                sp.dma_start(x_res[0:n, i, :], src).then_inc(N["x_in"], 16)
            for n, g in enumerate(("norm_mix_g", "norm_mem_g", "norm_memkv_g", "norm_ffn_g")):
                sp.dma_start(gains[:, n, :], a[g].rearrange("(p k) -> p k", k=KT)).then_inc(N["prm_in"], 16)
            for name, r in (("rwkv_mu", MU), ("rwkv_w0", W0), ("rwkv_a0", A0), ("rwkv_k_k", KK_), ("rwkv_k_a", KA),
                            ("rwkv_r_k", RK), ("rwkv_lnx_g", LG), ("rwkv_lnx_b", LB), ("b_gate", BG)):
                v = a[name] if name != "rwkv_r_k" else a[name].rearrange("h d -> (h d)")
                k = v.shape[0] // P
                sp.dma_start(row_b[r:r + k, :], v.rearrange("(j p) -> j p", p=P)).then_inc(N["prm_in"], 16)

            def load_chunk(n):
                if n >= 2:
                    sp.wait_ge(N["ring_used"], n - 1)
                if n == NR + 1:
                    sp.wait_ge(N["ring_spare"], 1)
                for cols_, src in chunks[n]:
                    dst = view(ring_at + 4096 * (n % 2), 4, D) if cols_ is None else ring[n % 2][:, :, cols_]
                    sp.dma_start(dst, src).then_inc(ring_in[n % 2], 16)

            for n in range(2):
                load_chunk(n)
            sp.dma_start(lora[0:64, 0, :], a["rwkv_w2"][:, :]).then_inc(N["small_in"], 16)
            sp.dma_start(lora[64:128, 0, :], a["rwkv_a2"][:, :]).then_inc(N["small_in"], 16)
            sp.dma_start(lora[:, 1, :], a["rwkv_g2"][:, :]).then_inc(N["small_in"], 16)
            sp.dma_start(wr[:, :, 0:4], a["w_router_group"].rearrange("(p k) e -> p k e", k=KT)).then_inc(N["small_in"], 16)
            sp.dma_start(wr[:, :, 4:36], a["w_router_expert"].rearrange("(p k) e -> p k e", k=KT)).then_inc(N["small_in"], 16)
            for n in range(2, NA):
                load_chunk(n)
            sp.wait_ge(N["rope_done"], len(TILES))
            for g, (window, _) in enumerate(GROUPS):
                keep = min(window, SEQ)
                dst = o[f"p_cache{g}"]
                for i in range(NPT - keep // P, NPT):
                    r0 = i * P - (SEQ - keep)
                    for kv in range(2):
                        src = qkv[:, i, BW * (1 + kv) + 256 * g:BW * (1 + kv) + 256 * g + 256]
                        sp.dma_start(dst[0, kv, r0:r0 + P].rearrange("t h d -> t (h d)"), src).then_inc(N["out"], 16)
                for b in range(NB):
                    for kv in range(2):
                        src = qkv[b * NS:(b + 1) * NS, 4, BW * (1 + kv) + 256 * g:BW * (1 + kv) + 256 * g + 256]
                        sp.dma_start(o[f"s_cache{g}"][b, kv, window - NS:window].rearrange("t h d -> t (h d)"), src)\
                          .then_inc(N["out"], 16)
            for n in range(NA, NA + 2):
                load_chunk(n)
            for kv in range(2):
                for m, (g, b) in enumerate(units):
                    z = kv * len(units) + m
                    if z >= 3:
                        sp.wait_ge(N["kv_used"], z - 2)
                    src = caches[g][b, kv].rearrange("(i r) h d -> i r (h d)", r=GROUPS[g][1])[:, 0:wide[g], :]
                    sp.dma_start(kvb[z % 3][:, 0:wide[g], :], src).then_inc(kv_in[z % 3], 16)
            sp.wait_ge(N["yb_done"], 1)
            sp.dma_start(shift_rows[0:NB, :], a["state_shift"][:, :]).then_inc(N["shift_in"], 16)
            for n in range(NA + 2, NR):
                load_chunk(n)
            sp.wait_ge(N["stm_done"], 1)
            sp.dma_start(srec_d.rearrange("v t c -> t v c"), tok_s[0:TS]).then_inc(N["srec_out"], 16)
            sp.wait_ge(N["srec_out"], 16)
            for hf in range(2):
                for b in range(NB):
                    rows = slice(hf * 64 + b * AH, hf * 64 + (b + 1) * AH)
                    for n in range(5):
                        src = srec_d[n, b * NS:(b + 1) * NS, :].rearrange("t (h k) -> h t k", h=AH)
                        sp.dma_start(rec[rows, n, :].rearrange("p (t k) -> p t k", t=NS), src).then_inc(N["srec_in"], 16)
                    src = srec_d[5, b * NS:(b + 1) * NS, :].rearrange("t (h f k) -> h f t k", h=AH, f=2)[:, hf]
                    sp.dma_start(rec_v[rows], src).then_inc(N["srec_in"], 16)
                src = a["state_rwkv"].rearrange("b h (f v) k -> (b h) f (v k)", f=2)[:, hf]
                sp.dma_start(rec_s[hf * 64:(hf + 1) * 64].rearrange("p v k -> p (v k)"), src).then_inc(N["srec_in"], 16)
            sp.wait_ge(N["state_out"], 32)
            load_chunk(NR)
            sp.wait_ge(N["mats"], NPT)
            sp.dma_start(wa, a["w_branch_a"].rearrange("(j p) d -> p j d", p=P)).then_inc(N["br_in"], 16)
            sp.dma_start(wb, a["w_branch_b"].rearrange("(j p) d -> p j d", p=P)).then_inc(N["br_in"], 16)
            for n in range(NR + 1, NO):
                load_chunk(n)
            sp.wait_ge(N["x1_done"], 1)
            sp.wait_ge(N["state_out"], 48)
            sp.dma_start(mem_x, a["mem_prompt"][0].rearrange("(i p) d -> p i d", p=P)).then_inc(N["mem_in"], 16)
            for n in range(NO, len(chunks)):
                load_chunk(n)
            for b in range(NB):
                if b >= 2:
                    sp.wait_ge(N["mkv_used"], b - 1)
                sp.dma_start(mks[b % 2], a["cache_mem_kv"][b, 0].rearrange("(i p) h d -> p i (h d)", p=P)).then_inc(mks_in[b % 2], 16)
            for b in range(NB):
                if b >= 2:
                    sp.wait_ge(N["mkv_used"], NB + b - 1)
                sp.dma_start(mvs[b % 2], a["cache_mem_kv"][b, 1].rearrange("(i p) h d -> p i (h d)", p=P)).then_inc(mvs_in[b % 2], 16)
            sp.wait_ge(N["e_area"], 1)
            sp.wait_ge(N["mkv_out"], 32)
            eg = a["w_exp_gate"].rearrange("e (p k) f -> e p k f", k=KT)
            eu = a["w_exp_up"].rearrange("e (p k) f -> e p k f", k=KT)
            ed = a["w_exp_down"].rearrange("e (c p) d -> e p c d", p=P)

            def load_expert(e, s, started):
                part = 0
                for w, src, k in ((wg, eg, KT), (wu, eu, KT), (wd, ed, 4)):
                    src = src[e] if isinstance(e, int) else src[bass.ds(e, 1)][0]
                    for h in range(2):
                        q = part % 2
                        if started or part >= 2:
                            sp.wait_ge(w_in_sem[q], 48 * e + 16 * (part // 2))
                        if not isinstance(e, int):
                            sp.sem_inc(N["seen"], 1)
                        ks = slice(h * k // 2, (h + 1) * k // 2)
                        sp.dma_start(w[s][:, ks, :], src[:, ks, :]).then_inc(w_in_sem[q], 16)
                        part += 1

            for s in range(2):
                load_expert(s, s, s > 0)
            sp.wait_ge(N["tab_ready"], 1)
            with sp.Fori(1, NE // 2) as j:
                for s in range(2):
                    begun = sp.value_load(tab_of(FIRST, 2 * j + s - 1), min_val=1, max_val=ALLBLK)
                    sp.wait_ge(N["y_ready"], 2 * begun)
                    sp.sem_inc(N["seen"], 1)
                    load_expert(2 * j + s, s, True)
            sp.wait_ge(N["out"], 16 * OUT_CACHES)

        @block.tensor
        def _(pe):
            line = Line(pe, N["pe_step"])
            vm, am = Mail(*v_mail), Mail(*a_mail)
            mm = pe.matmul

            def turn_rows(src, n, s, k):
                for half in range(2):
                    bank = vm.claim(pe)
                    for q in range(4):
                        last = pe.transpose(bank[:, q * P:q * P + n], src[0:n, 4 * half + q:D:KT], ident[0:n, 0:n])
                    last.then_inc(vm.filled, 1)

            def chunk_ready(n):
                pe.wait_ge(ring_in[n % 2], loaded[n])

            def chunk_used(mail):
                pe.wait_ge(mail.filled, mail.put)
                pe.sem_inc(N["ring_used"], 1)

            pe.wait_ge(N["con_in"], 16)
            pe.wait_ge(N["prm_in"], 16 * 13)
            bank = vm.claim(pe)
            pe.transpose(bank[:, 0:NPRM], row_b[0:NPRM, :], ident[0:NPRM, 0:NPRM]).then_inc(vm.filled, 1)
            for i, (t0, n) in enumerate(TILES):
                pe.wait_ge(N["xs3_done"], i + 1)
                turn_rows(xs_tmp[i % 2], n, None, i)
            pe.wait_ge(N["xt_done"], len(TILES))
            for n in range(NA):
                chunk_ready(n)
                w = chunks[n][0][0].stop
                for i, (t0, m) in enumerate(TILES):
                    bank = am.claim(pe)
                    for kt in range(KT):
                        last = mm(bank[0:m, 0:w], x_t[:, kt, t0:t0 + m], ring[n % 2][:, kt, 0:w], start=kt == 0, stop=kt == KT - 1)
                    last.then_inc(am.filled, 1)
                chunk_used(am)
            for i, (t0, m) in enumerate(TILES):
                pe.wait_ge(N["rope_done"], i + 1)
                for half in range(3):
                    bank = vm.claim(pe)
                    for q in range(4):
                        j = 4 * half + q
                        last = pe.transpose(bank[:, q * P:q * P + m], qkv[0:m, i, j * P:(j + 1) * P], ident[0:m, 0:m])
                    last.then_inc(vm.filled, 1)
            pe.wait_ge(vm.freed, vm.put)
            def scores(u):
                i, h = att[u]
                lo = 64 * (h % 2)
                for g in range(NG):
                    js = [j for gg, j in key_blocks(i) if gg == g]
                    bank = vm.claim(pe)
                    mm(bank[:, 0:P * len(js)], qk_t[lo:lo + 64, 2 * g + h // 2, i * P:(i + 1) * P],
                       qk_t[lo:lo + 64, 6 + 2 * g + h // 2, js[0] * P:(js[-1] + 1) * P], start=True, stop=True).then_inc(vm.filled, 1)

            def turn_weights(u):
                kb = key_blocks(att[u][0])
                pe.wait_ge(N["p_ready"], u + 1)
                for c in range(0, len(kb), 4):
                    bank = am.claim(pe)
                    for q in range(c, min(c + 4, len(kb))):
                        last = pe.transpose(bank[:, (q - c) * P:(q - c + 1) * P], s_sb[u % 3][:, q * P:(q + 1) * P], ident)
                    last.then_inc(am.filled, 1)

            def weigh(u):
                i, h = att[u]
                kb = key_blocks(i)
                pe.wait_ge(am.freed, am.put)
                if u >= 1:
                    pe.wait_ge(N["pv_taken"], u)
                lo = 64 * (h % 2)
                for q, (g, j) in enumerate(kb):
                    c = 2 * BW + 256 * g + 64 * h
                    last = mm(aux[lo:lo + 64, 0:P], qkv[:, j, c:c + 64], p_t[u % 2][:, q, :], start=q == 0, stop=q == len(kb) - 1)
                last.then_inc(N["pv_full"], 1)

            scores(0)
            scores(1)
            for u in range(len(att)):
                turn_weights(u)
                if u + 2 < len(att):
                    scores(u + 2)
                weigh(u)
            pe.wait_ge(N["qblk_ready"], 1)
            pe.wait_ge(N["pv_taken"], len(att))

            def turn_keys(m):
                g, b = units[m]
                pe.wait_ge(kv_in[m % 3], 16 * (m // 3 + 1))
                for c in range(0, 2 * wide[g], 4):
                    bank = am.claim(pe)
                    for q in range(c, min(c + 4, 2 * wide[g])):
                        last = pe.transpose(bank[:, (q - c) * P:(q - c + 1) * P], kvb[m % 3][:, q // 2, (q % 2) * P:(q % 2 + 1) * P], ident)
                    last.then_inc(am.filled, 1)
                return am.put

            def cached_scores(m, got):
                g, b = units[m]
                pe.wait_ge(am.freed, got)
                for t in range(wide[g]):
                    for hp in range(2):
                        q = qblk[:, 2 * g + hp, :].rearrange("p (h t) -> p h t", t=TS)
                        dst = aux[:, P * g + 64 * hp:P * g + 64 * hp + 64].rearrange("p (h t) -> p h t", t=TS)
                        ts = slice(b * NS, (b + 1) * NS) if wide[g] == 1 else slice(b * NS + t, b * NS + t + 1)
                        last = mm(dst[:, :, ts], kt_s[m % 2][:, 2 * t + hp, :], q[:, :, ts], start=True, stop=True)
                last.then_inc(N["kv_used"], 1)

            got = turn_keys(0)
            for m in range(len(units)):
                nxt = turn_keys(m + 1) if m + 1 < len(units) else None
                cached_scores(m, got)
                got = nxt
            bank = vm.claim(pe)
            for g in range(NG):
                for hp in range(2):
                    last = mm(bank[0:TS, P * g + 64 * hp:P * g + 64 * hp + 64], qk_t[:, 6 + 2 * g + hp, SEQ:T],
                              qblk[:, 2 * g + hp, :], start=True, stop=True)
            last.then_inc(vm.filled, 1)
            pe.wait_ge(N["snew"], 1)
            bank = vm.claim(pe)
            for g in range(NG):
                pe.transpose(bank[:, g * P:(g + 1) * P], st_sb[:, g, :], ident)
                last = pe.transpose(bank[:, NG * P + g * TS:NG * P + (g + 1) * TS], stn_sb[0:TS, g, :], ident[0:TS, 0:TS])
            last.then_inc(vm.filled, 1)
            pe.wait_ge(N["s_soft"], 1)
            bank = vm.claim(pe)
            for g in range(NG):
                last = pe.transpose(bank[:, g * P:(g + 1) * P], ps_sb[:, g * P:(g + 1) * P], ident)
            last.then_inc(vm.filled, 1)
            bank = vm.claim(pe)
            for g in range(NG):
                last = pe.transpose(bank[0:TS, g * P:(g + 1) * P], ps_sb[:, NG * P + g * TS:NG * P + (g + 1) * TS], ident)
            last.then_inc(vm.filled, 1)
            pe.wait_ge(vm.freed, vm.put)
            for g in range(NG):
                for hp in range(2):
                    c = 2 * BW + 256 * g + P * hp
                    mm(aux[:, 64 * hp:64 * hp + 64], qkv[0:TS, 4, c:c + P], ptn[0:TS, g, 64 * hp:64 * hp + 64],
                       start=g == 0 and hp == 0, stop=False, skip_group_check=True)
            for m, (g, b) in enumerate(units):
                z = len(units) + m
                pe.wait_ge(kv_in[z % 3], 16 * (z // 3 + 1))
                for t in range(wide[g]):
                    for hp in range(2):
                        pr = pts[:, g, 64 * hp:64 * hp + 64].rearrange("p (h t) -> p h t", t=TS)
                        dst = aux[:, 64 * hp:64 * hp + 64].rearrange("p (h t) -> p h t", t=TS)
                        ts = slice(b * NS, (b + 1) * NS) if wide[g] == 1 else slice(b * NS + t, b * NS + t + 1)
                        last = mm(dst[:, :, ts], kvb[z % 3][:, t, hp * P:(hp + 1) * P], pr[:, :, ts], start=False,
                                  stop=m == len(units) - 1, skip_group_check=True)
                last.then_inc(N["kv_used"], 1)
            pe.wait_ge(N["shift_in"], 16)
            for c in range(0, AJ, 4):
                bank = vm.claim(pe)
                for j in range(c, min(c + 4, AJ)):
                    last = pe.transpose(bank[:, (j - c) * NB:(j - c + 1) * NB], shift_rows[0:NB, j * P:(j + 1) * P], ident[0:NB, 0:NB])
                last.then_inc(vm.filled, 1)

            def project(c, between=None):
                chunk_ready(c)
                for q in range(len(feats[c - NA])):
                    for t0, n in HALVES:
                        bank = am.claim(pe)
                        for kt in range(KT):
                            last = mm(bank[:, 0:n], ring[c % 2][:, kt, q * P:(q + 1) * P], x_t[:, kt, t0:t0 + n], start=kt == 0, stop=kt == KT - 1)
                        last.then_inc(am.filled, 1)
                    if between and q == 0:
                        between()
                chunk_used(am)

            def loras(um, n):
                for j in range(4):
                    for lhs, rhs in ((lora[0:64, 0], um[0:64, 12]), (lora[64:128, 0], um[64:128, 12]), (lora[:, 1], um[:, 13])):
                        bank = am.claim(pe)
                        mm(bank[:, 0:n], lhs[:, j * P:(j + 1) * P], rhs, start=True, stop=True).then_inc(am.filled, 1)

            def head_sums(sq, n):
                for j in range(4):
                    bank = vm.claim(pe)
                    mm(bank[:, 0:n], C("blk"), sq[:, j, 0:n], start=True, stop=True).then_inc(vm.filled, 1)

            def head_roots(sq, n):
                bank = vm.claim(pe)
                for j in range(4):
                    last = mm(bank[32 * j:32 * j + 32, 0:n], C("blk")[:, 48:80], sq[:, j, 0:n], start=True, stop=True)
                last.then_inc(vm.filled, 1)

            def spread(n, count):
                pe.wait_ge(N["inv_ready"], count)
                for j in range(4):
                    bank = vm.claim(pe)
                    mm(bank[:, 0:n], C("spread")[32 * j:32 * j + 32, :], inv[32 * j:32 * j + 32, 0:n], start=True, stop=True)\
                        .then_inc(vm.filled, 1)

            def token_rows(src):
                for i in range(NPT):
                    bank = vm.claim(pe)
                    for j in range(4):
                        last = pe.transpose(bank[:, j * P:(j + 1) * P], src[:, j, i * P:(i + 1) * P], ident)
                    last.then_inc(vm.filled, 1)

            project(NA)
            project(NA + 1)
            pe.wait_ge(N["lora_in"], 1)
            loras(um_p, SEQ)
            project(NA + 2)
            pe.wait_ge(N["prep_sq"], 1)
            head_roots(sq_p, SEQ)
            project(NA + 3, lambda: spread(SEQ, 1))
            pe.wait_ge(N["prep_sq"], 2)
            head_sums(sq_p, SEQ)
            pe.wait_ge(N["lora_in"], 2)
            loras(um_s, TS)
            pe.wait_ge(N["prep_done"], 1)
            token_rows(a_p)
            pe.wait_ge(N["prep_sq"], 3)
            head_roots(tmp_s, TS)
            spread(TS, 2)
            token_rows(um_p[:, 4:8])
            pe.wait_ge(N["prep_sq"], 4)
            head_sums(tmp_s, TS)
            token_rows(um_p[:, 8:12])
            for c in range(0, AJ, 4):
                bank = vm.claim(pe)
                for j in range(c, min(c + 4, AJ)):
                    last = pe.transpose(bank[0:NB, (j - c) * P:(j - c + 1) * P], u_s[:, j, NS - 1:TS:NS], ident)
                last.then_inc(vm.filled, 1)
            bank = vm.claim(pe)
            mm(bank[64:64 + AJ, 0:P], u_last, ident, start=True, stop=True).then_inc(vm.filled, 1)
            pe.wait_ge(N["tm_done"], 1)
            for src in (um_s[:, 0:4], um_s[:, 4:8], kk_s, a_s, dec_s, um_s[:, 8:12]):
                bank = vm.claim(pe)
                for j in range(4):
                    last = pe.transpose(bank[0:TS, j * P:(j + 1) * P], src[:, j, :], ident)
                last.then_inc(vm.filled, 1)
            pe.wait_ge(vm.freed, vm.put)

            def heads(par):
                return [(j, 2 * j + par) for j in range(4)]

            r_p, k_p = um_p[:, 0:4], um_p[:, 4:8]
            for i in range(NPT):
                tk = slice(i * P, (i + 1) * P)
                if i >= 1:
                    pe.wait_ge(N["state_ready"], i)
                for lhs, rhs in ((a_p, kk_p), (kk_p, a_p), (k_p, kk_p), (a_p, r_p), (k_p, r_p)):
                    two = [vm.claim(pe), vm.claim(pe)]
                    for par in range(2):
                        lo = 64 * par
                        for j, h in heads(par):
                            last = mm(two[par][:, j * P:(j + 1) * P], lhs[lo:lo + 64, j, tk], rhs[lo:lo + 64, j, tk], start=True, stop=True)
                        last.then_inc(vm.filled, 1)
                for lv, m in enumerate(LEVELS[1:]):
                    final = m == LEVELS[-1]
                    pe.wait_ge(N["lm_ready"], 6 * i + lv + 1)
                    pe.wait_ge(vm.freed, vm.put)
                    for par in range(2):
                        bank = vm.claim(pe)
                        for j in range(4):
                            last = mm(bank[:, j * P:(j + 1) * P], mat_lm[:, 4 * par + j, :], mat_t[:, 4 * par + j, :], start=True, stop=True)
                        last.then_inc(vm.filled, 1)
                    base = vm.put
                    for par in range(2):
                        pe.wait_ge(vm.freed, base - 1 + par)
                        for tt in ((0, 1) if not final else (1,)):
                            bank = vm.claim(pe)
                            for j in range(4):
                                z = 4 * par + j
                                lhs, rhs = (mat_w, mat_tt) if tt else (mat_tt, mat_w)
                                last = mm(bank[:, j * P:(j + 1) * P], lhs[:, z, :], rhs[:, z, :], start=True, stop=True)
                            last.then_inc(vm.filled, 1)
                pe.wait_ge(vm.freed, vm.put)
                two = [vm.claim(pe), vm.claim(pe)]
                for par in range(2):
                    lo = 64 * par
                    for j, h in heads(par):
                        dst = two[par][:, j * 64:j * 64 + 64]
                        mm(dst, kk_p[lo:lo + 64, j, tk], st0m[lo:lo + 64, j, :], start=True, stop=False)
                        last = mm(dst, mat_ak[:, 4 * par + j, :], tm_v[:, i, h * 64:h * 64 + 64], start=False, stop=True)
                    last.then_inc(vm.filled, 1)
                pe.wait_ge(vm.freed, vm.put)
                bank = vm.claim(pe)
                for z in range(8):
                    last = mm(bank[:, z * 64:z * 64 + 64], mat_tt[:, z, :], w_sb[:, z, :], start=True, stop=True)
                last.then_inc(vm.filled, 1)
                pe.wait_ge(vm.freed, vm.put)
                bank = vm.claim(pe)
                for par in range(2):
                    lo = 64 * par
                    for j, h in heads(par):
                        dst = bank[lo:lo + 64, j * 64:j * 64 + 64]
                        mm(dst, tm_b[:, i, h * 64:h * 64 + 64], uu_sb[:, 4 * par + j, :], start=True, stop=False)
                        last = mm(dst, tm_k[:, i, h * 64:h * 64 + 64], tm_v[:, i, h * 64:h * 64 + 64], start=False, stop=True)
                last.then_inc(vm.filled, 1)
                two = [am.claim(pe), am.claim(pe)]
                for par in range(2):
                    lo = 64 * par
                    for j, h in heads(par):
                        dst = two[par][lo:lo + 64, j * P:(j + 1) * P]
                        z = 4 * par + j
                        mm(dst, st0m[lo:lo + 64, j, :], r_p[lo:lo + 64, j, tk], start=True, stop=False)
                        mm(dst, uu_sb[:, z, :], mat_rb[:, z, :], start=False, stop=False)
                        last = mm(dst, tm_v[:, i, h * 64:h * 64 + 64], mat_rk[:, z, :], start=False, stop=True)
                    last.then_inc(am.filled, 1)
                pe.wait_ge(am.filled, am.put)
                pe.sem_inc(N["mats"], 1)
            pe.wait_ge(N["state_ready"], NPT)
            bank = vm.claim(pe)
            for j in range(4):
                last = pe.transpose(bank[0:64, j * P:(j + 1) * P], st0[:, j, :], ident)
            last.then_inc(vm.filled, 1)
            pe.wait_ge(N["yrec_in"], 16)
            bank = vm.claim(pe)
            for j in range(4):
                last = pe.transpose(bank[:, j * TS:(j + 1) * TS], y_tok[0:TS, j * P:(j + 1) * P], ident[0:TS, 0:TS])
            last.then_inc(vm.filled, 1)

            def gates(j, half):
                c = NR + j // 2
                t0, n = HALVES[half]
                if j % 2 == 0 and half == 0:
                    chunk_ready(c)
                for off in (0, 256):
                    bank = am.claim(pe)
                    for kt in range(KT):
                        last = mm(bank[:, 0:n], ring[c % 2][:, kt, off + j % 2 * P:off + (j % 2 + 1) * P], x_t[:, kt, t0:t0 + n],
                                  start=kt == 0, stop=kt == KT - 1)
                    last.then_inc(am.filled, 1)
                if j % 2 == 1 and half == 1:
                    chunk_used(am)

            for part in range(2):
                n = TS if part == 0 else SEQ
                y = y_s if part == 0 else a_p
                sq = tmp_s if part == 0 else tmp_p
                pe.wait_ge(N["ysq"], 2 * part + 1)
                head_sums(y, n)
                gates(part, 0)
                pe.wait_ge(N["ysq"], 2 * part + 2)
                head_roots(sq, n)
                if part == 0:
                    spread(n, 3)
                    gates(0, 1)
                else:
                    gates(1, 1)
                    spread(n, 4)
            pe.wait_ge(N["ya_done"], 1)
            pe.wait_ge(N["br_in"], 32)
            for j in range(KT):
                for half, (t0, n) in enumerate(HALVES):
                    if j + 2 < KT:
                        gates(j + 2, half)
                    for w, y, nk in ((wa, y_all, 4), (wb, yb_t, 2)):
                        bank = vm.claim(pe)
                        for q in range(nk):
                            last = mm(bank[:, 0:n], w[:, q, j * P:(j + 1) * P], y[:, q, t0:t0 + n], start=q == 0, stop=q == nk - 1)
                        last.then_inc(vm.filled, 1)
            pe.wait_ge(N["merged"], 1)

            def out_rows(first, nk, lhs, last_sem):
                for i, (t0, m) in enumerate(TILES):
                    for c in range(2):
                        bank = vm.claim(pe)
                        for k in range(nk):
                            last = mm(bank[0:m, :], lhs[:, k, t0:t0 + m], first(c, k), start=k == 0, stop=k == nk - 1)
                        last.then_inc(vm.filled, 1)

            chunk_ready(NGT)
            chunk_ready(NGT + 1)
            out_rows(lambda c, k: ring[(NGT + c) % 2][:, k, :], KT, m_t, None)
            chunk_used(vm)
            chunk_used(vm)
            for i in range(2):
                pe.wait_ge(N["memx"], i + 1)
                turn_rows(xs2[i % 2], P, None, i)
            pe.wait_ge(vm.freed, vm.put)
            for c in range(2):
                chunk_ready(NO + c)
                for i in range(2):
                    bank = vm.claim(pe)
                    for kt in range(KT):
                        last = mm(bank, mem_t[:, kt, i * P:(i + 1) * P], ring[(NO + c) % 2][:, kt, :], start=kt == 0, stop=kt == KT - 1)
                    last.then_inc(vm.filled, 1)
                chunk_used(vm)
            pe.wait_ge(vm.freed, vm.put)
            for i in range(2):
                bank = vm.claim(pe)
                for h in range(MH):
                    last = pe.transpose(bank[:, h * P:(h + 1) * P], mkv[:, i, h * P:(h + 1) * P], ident)
                last.then_inc(vm.filled, 1)
            for i, (t0, n) in enumerate(TILES):
                pe.wait_ge(N["memx"], 2 + i + 1)
                turn_rows(xs2[i % 2], n, None, i)
            pe.wait_ge(vm.freed, vm.put)
            chunk_ready(NM)
            for h in range(MH):
                for t0, n in HALVES:
                    bank = vm.claim(pe)
                    for kt in range(KT):
                        last = mm(bank[:, 0:n], ring[NM % 2][:, kt, h * P:(h + 1) * P], x_t[:, kt, t0:t0 + n], start=kt == 0, stop=kt == KT - 1)
                    last.then_inc(vm.filled, 1)
            chunk_used(vm)
            pe.wait_ge(vm.freed, vm.put)

            def mem_scores(u):
                i, h = mem_units[u]
                bank = vm.claim(pe)
                mm(bank[:, 0:MEM], q_t[:, h, i * P:(i + 1) * P], mk_t[:, h, :], start=True, stop=True).then_inc(vm.filled, 1)

            def mem_turn(u):
                pe.wait_ge(N["m_ready"], u + 1)
                bank = am.claim(pe)
                for c in range(2):
                    last = pe.transpose(bank[:, c * P:(c + 1) * P], ms_sb[u % 3][:, c * P:(c + 1) * P], ident)
                last.then_inc(am.filled, 1)

            def mem_weigh(u):
                i, h = mem_units[u]
                pe.wait_ge(am.freed, am.put)
                bank = am.claim(pe)
                for c in range(2):
                    last = mm(bank[:, 0:P], mkv[:, c, MW + h * P:MW + (h + 1) * P], mp_t[u % 2][:, c, :], start=c == 0, stop=c == 1)
                last.then_inc(am.filled, 1)

            mem_scores(0)
            mem_scores(1)
            for u in range(len(mem_units)):
                mem_turn(u)
                if u + 2 < len(mem_units):
                    mem_scores(u + 2)
                mem_weigh(u)
            def turn_mem(b):
                pe.wait_ge(mks_in[b % 2], 16 * (b // 2 + 1))
                for c in range(2):
                    bank = am.claim(pe)
                    for h in range(MH):
                        last = pe.transpose(bank[:, h * P:(h + 1) * P], mks[b % 2][:, c, h * P:(h + 1) * P], ident)
                    last.then_inc(am.filled, 1)
                return am.put

            got = turn_mem(0)
            for b in range(NB):
                nxt = turn_mem(b + 1) if b + 1 < NB else None
                pe.wait_ge(am.freed, got)
                for c in range(2):
                    for h in range(MH):
                        last = mm(aux[:, c * P + h * TS + b * NS:c * P + h * TS + (b + 1) * NS], mkt_s[b % 2][:, 4 * c + h, :],
                                  q_t[:, h, SEQ + b * NS:SEQ + (b + 1) * NS], start=True, stop=True)
                last.then_inc(N["mkv_used"], 1)
                got = nxt
            pe.wait_ge(N["mst_ready"], 1)
            bank = vm.claim(pe)
            for c in range(2):
                last = pe.transpose(bank[:, c * P:(c + 1) * P], mst[:, c, :], ident)
            last.then_inc(vm.filled, 1)
            pe.wait_ge(N["m_ready"], len(mem_units) + 1)
            bank = am.claim(pe)
            for c in range(2):
                last = pe.transpose(bank[:, c * P:(c + 1) * P], ms_sb[len(mem_units) % 3][:, c * P:(c + 1) * P], ident)
            last.then_inc(am.filled, 1)
            pe.wait_ge(am.freed, am.put)
            for b in range(NB):
                pe.wait_ge(mvs_in[b % 2], 16 * (b // 2 + 1))
                for h in range(MH):
                    for c in range(2):
                        cs = h * TS + b * NS
                        last = mm(aux[:, cs:cs + NS], mvs[b % 2][:, c, h * P:(h + 1) * P], mp_t[0][:, c, cs:cs + NS],
                                  start=c == 0, stop=c == 1)
                last.then_inc(N["mkv_used"], 1)
            pe.wait_ge(N["mo_done"], 1)
            pe.wait_ge(am.freed, am.put)
            chunk_ready(NM + 1)
            wmo = view(ring_at + 4096 * ((NM + 1) % 2), 4, D)
            out_rows(lambda c, k: wmo[:, k, c * 512:(c + 1) * 512], MH, o_t, None)
            chunk_used(vm)
            pe.wait_ge(N["x2_done"], 1)
            pe.sem_inc(N["e_area"], 1)
            for i, (t0, n) in enumerate(TILES):
                pe.wait_ge(N["xs3_done"], len(TILES) + i + 1)
                turn_rows(xs3[:, i, :], n, None, i)
                pe.wait_ge(vm.freed, vm.put)
                bank = vm.claim(pe)
                for kt in range(KT):
                    last = mm(bank[0:n, 0:36], x_t[:, kt, t0:t0 + n], wr[:, kt, :], start=kt == 0, stop=kt == KT - 1)
                last.then_inc(vm.filled, 1)
            pe.wait_ge(N["hot_done"], 1)
            bank = vm.claim(pe)
            for j, (t0, m) in enumerate(TILES):
                last = mm(bank[:, 0:2 * NE], C("ones")[0:m, :], hot[0:m, j, :], start=j == 0, stop=j == len(TILES) - 1)
            last.then_inc(vm.filled, 1)
            for i, (t0, n) in enumerate(TILES):
                bank = vm.claim(pe)
                for j in range(i + 1):
                    m = TILES[j][1]
                    lhs = C("ones")[0:m, 0:n] if j < i else C("strict")[0:m, 0:n]
                    last = mm(bank[0:n, 0:2 * NE], lhs, hot[0:m, j, :], start=j == 0, stop=j == i)
                last.then_inc(vm.filled, 1)
            pe.wait_ge(N["tab_ready"], 1)
            def turn_block():
                for kt in range(KT):
                    last = pe.transpose(x_ps[kt // 4][:, kt % 4 * BLK:(kt % 4 + 1) * BLK], xb[:, kt:D:KT], ident)
                last.then_inc(N["xb_used"], 1)

            pe.wait_ge(N["xb_in"], 16)
            turn_block()
            with pe.Fori(0, NE // 2) as jj:
                table = [(pe.value_load(tab_of(FIRST, 2 * jj + s), min_val=0, max_val=ALLBLK),
                          pe.value_load(tab_of(COUNT, 2 * jj + s), min_val=1, max_val=MAXBLK)) for s in range(2)]
                for s in range(2):
                    first, blocks = table[s]
                    for q in range(2):
                        pe.wait_ge(w_in_sem[q], 48 * (2 * jj + s + 1))
                    pe.sem_inc(N["seen"], 1)
                    with pe.Fori(0, blocks) as m:
                        n = pe.snap(first + m)
                        pe.wait_ge(N["xe_ready"], n + 1)
                        for dst, w, full in ((g_ps, wg[s], N["g_full"]), (u_ps, wu[s], N["u_full"])):
                            for kt in range(KT):
                                last = mm(dst, x_e[:, kt, :], w[:, kt, :], start=kt == 0, stop=kt == KT - 1)
                            last.then_inc(full, 1)
                        pe.wait_ge(N["xb_in"], 16 * n + 32)
                        pe.sem_inc(N["seen"], 1)
                        turn_block()
                        pe.wait_ge(N["h_done"], n + 1)
                        pe.sem_inc(N["seen"], 1)
                        for k in range(4):
                            last = pe.transpose(h_ps[:, k * BLK:(k + 1) * BLK], h_b[:, k * P:(k + 1) * P], ident)
                        last.then_inc(N["ht_full"], 1)
                        pe.wait_ge(N["ht_done"], n + 1)
                        for c in range(2):
                            for k in range(4):
                                last = mm(d_ps[c], h_t[:, k, :], wd[s][:, k, c * 512:(c + 1) * 512], start=k == 0, stop=k == 3)
                            last.then_inc(N["y_ready"], 1)

        @block.scalar
        def _(act):
            line = Line(act, N["act_step"])
            am = Mail(*a_mail)

            def f(out, in_, func, sem=None, **kw):
                line.do(nc.scalar.activation(out, in_, func, **kw), sem)

            def rms(rows, junk):
                for col, (src, n) in enumerate(rows):
                    f(junk[0:n], src, ACT.Square, accum_out=stat[0:n, col:col + 1])
                full = sum(n == P for _, n in rows)
                f(stat[:, 0:full], stat[:, 0:full], ACT.Sqrt, scale=1.0 / D, bias=C("eps"))
                if full < len(rows):
                    n = rows[-1][1]
                    f(stat[0:n, full:full + 1], stat[0:n, full:full + 1], ACT.Sqrt, scale=1.0 / D, bias=C("eps")[0:n])
                act.sem_inc(N["rms"], 1)

            stream = [(x_res[0:n, i, :], n) for i, (t0, n) in enumerate(TILES)]

            act.wait_ge(N["x_in"], 16 * len(TILES))
            act.wait_ge(N["con_in"], 16)
            rms(stream, view(s0 + 2560, D))
            for c in range(NA):
                w = chunks[c][0][0].stop
                for i, (t0, n) in enumerate(TILES):
                    bank = am.take(act)
                    f(qkv[0:n, i, 512 * c:512 * c + w], bank[0:n, 0:w], ACT.Copy, am.freed)
            act.sem_inc(N["qkv_raw"], 1)

            def exp_unit(u):
                i, h = att[u]
                n = P * len(key_blocks(i))
                c = 8 + 4 * (u % 3)
                act.wait_ge(N["p_neg"], u + 1)
                f(s_sb[u % 3][:, 0:n], s_sb[u % 3][:, 0:n], ACT.Exp, N["p_exp"], bias=stat[:, c + 1:c + 2], scale=0.125,
                  accum_out=stat[:, c + 2:c + 3])

            def take_unit(u):
                i, h = att[u]
                kb = key_blocks(i)
                for c in range(0, len(kb), 4):
                    k = min(4, len(kb) - c)
                    bank = am.take(act)
                    f(p_t[u % 2][:, c:c + k, :], bank[:, 0:k * P].rearrange("p (a b) -> p a b", b=P), ACT.Copy, am.freed)
                act.wait_ge(N["pv_full"], u + 1)
                lo = 64 * (h % 2)
                f(yb_t[lo:lo + 64, h // 2, i * P:(i + 1) * P], aux[lo:lo + 64, 0:P], ACT.Copy, N["pv_taken"])

            exp_unit(0)
            exp_unit(1)
            for u in range(len(att)):
                take_unit(u)
                if u + 2 < len(att):
                    exp_unit(u + 2)
            for m, (g, b) in enumerate(units):
                for c in range(0, 2 * wide[g], 4):
                    k = min(4, 2 * wide[g] - c)
                    bank = am.take(act)
                    f(kt_s[m % 2][:, c:c + k, :], bank[:, 0:k * P].rearrange("p (a b) -> p a b", b=P), ACT.Copy, am.freed)
            act.wait_ge(N["sneg"], 1)
            f(ps_sb, ps_sb, ACT.Exp, N["sexp"], bias=stat[:, 17:18], scale=0.125, accum_out=stat[:, 18:19])
            act.wait_ge(N["yb_done"], 1)
            act.wait_ge(N["out"], 16 * OUT_CACHES)
            def take_feature(j):
                half = HALVES[1][0]
                f(u_p[:, j, 0:half], am.take(act)[:, 0:half], ACT.Copy, am.freed)
                bank = am.take(act)
                f(u_p[:, j, half:SEQ], bank[:, 0:SEQ - half], ACT.Copy)
                f(u_s[:, j, :], bank[:, SEQ - half:half], ACT.Copy, am.freed)
                act.sem_inc(N["u_raw"], 1)

            def squash(um, part):
                act.wait_ge(N["um_done"], part + 1)
                f(um[0:64, 12, :], um[0:64, 12, :], ACT.Tanh)
                f(um[:, 13, :], um[:, 13, :], ACT.Sigmoid, N["lora_in"])

            def take_loras(sg, aa, gg, n):
                for j in range(4):
                    f(sg[:, j, 0:n], am.take(act)[:, 0:n], ACT.Sigmoid, am.freed, bias=prm[:, W0 + j:W0 + j + 1])
                    f(aa[:, j, 0:n], am.take(act)[:, 0:n], ACT.Sigmoid, am.freed, bias=prm[:, A0 + j:A0 + j + 1])
                    f(gg[:, j, 0:n], am.take(act)[:, 0:n], ACT.Copy, am.freed)
                act.sem_inc(N["sga"], 1)

            for j in feats[0] + feats[1][0:1]:
                take_feature(j)
            squash(um_p, 0)
            for j in feats[1][1:]:
                take_feature(j)
            take_loras(sg_p, a_p, g_p, SEQ)
            for j in feats[2] + feats[3][0:1]:
                take_feature(j)
            act.wait_ge(N["sq_ready"], 1)
            f(inv, inv, ACT.Sqrt, N["sq_done"])
            act.wait_ge(N["prep_e"], 1)
            f(sg_p, sg_p, ACT.Exp)
            f(tmp_p, c_p, ACT.Exp)
            f(c_p, c_p, ACT.Exp, scale=-1.0)
            f(pmid, pmid, ACT.Exp)
            act.sem_inc(N["exp_done"], 1)
            for j in feats[3][1:]:
                take_feature(j)
            squash(um_s, 1)
            take_loras(dec_s, a_s, g_s, TS)
            act.wait_ge(N["sq_ready"], 2)
            f(inv[:, 0:TS], inv[:, 0:TS], ACT.Sqrt, N["sq_done"])
            f(dec_s, dec_s, ACT.Exp, scale=-float(np.exp(np.float32(-0.5))))
            act.sem_inc(N["exp_done"], 1)
            for i in range(NPT):
                for par in range(2):
                    lo = 64 * par
                    bank = am.take(act)
                    f(a_p[lo:lo + 64, :, i * P:(i + 1) * P], bank[lo:lo + 64, :].rearrange("p (a b) -> p a b", b=P), ACT.Copy, am.freed)
            act.sem_inc(N["y_raw"], 1)

            def gates(j, half):
                t0, n = HALVES[half]
                if j >= 3:
                    act.wait_ge(N["gate_used"], 2 * (j - 3) + half + 1)
                for k in range(2):
                    b = BG + 8 * k + j
                    f(gate_sb[j % 3][:, k, t0:t0 + n], am.take(act)[:, 0:n], ACT.Sigmoid, am.freed, bias=prm[:, b:b + 1])
                act.sem_inc(N["sig_done"], 1)

            gates(0, 0)
            act.wait_ge(N["sq_ready"], 3)
            f(inv[:, 0:TS], inv[:, 0:TS], ACT.Sqrt, N["sq_done"])
            gates(0, 1)
            gates(1, 0)
            act.wait_ge(N["sq_ready"], 4)
            f(inv, inv, ACT.Sqrt, N["sq_done"])
            gates(1, 1)
            for j in range(2, KT):
                for half in range(2):
                    gates(j, half)
            act.wait_ge(N["x1_done"], 1)
            act.wait_ge(N["mem_in"], 16)
            rms([(mem_x[:, i, :], P) for i in range(2)] + stream, view(Z + 21060, D))
            MS = float(MD) ** -0.5
            nu = len(mem_units)

            def mem_exp(u):
                c, s = 20 + 4 * (u % 3), ms_sb[u % 3]
                act.wait_ge(N["m_neg"], u + 1)
                f(s, s, ACT.Exp, N["m_exp"], bias=stat[:, c + 1:c + 2], scale=MS, accum_out=stat[:, c + 2:c + 3])

            mem_exp(0)
            mem_exp(1)
            for u in range(nu):
                i, h = mem_units[u]
                f(mp_t[u % 2], am.take(act)[:, 0:MEM].rearrange("p (a b) -> p a b", b=P), ACT.Copy, am.freed)
                f(o_t[:, h, i * P:(i + 1) * P], am.take(act)[:, 0:P], ACT.Copy, am.freed)
                if u + 2 < nu:
                    mem_exp(u + 2)
            for b in range(NB):
                for c in range(2):
                    f(mkt_s[b % 2][:, 4 * c:4 * c + 4, :], am.take(act)[:, :].rearrange("p (a b) -> p a b", b=P), ACT.Copy, am.freed)
            mem_exp(nu)
            f(mp_t[0], am.take(act)[:, 0:MEM].rearrange("p (a b) -> p a b", b=P), ACT.Copy, am.freed)
            act.wait_ge(N["x2_done"], 1)
            rms(stream, y_b)
            for i, (t0, n) in enumerate(TILES):
                act.wait_ge(N["route_a"], i + 1)
                f(rs[0:n, 160:164], lg[0:n, 0:4], ACT.Exp, bias=rs[0:n, 24:25], accum_out=rs[0:n, 25:26])
                f(rs[0:n, 27:28], rs[0:n, 26:27], ACT.Exp)
                act.sem_inc(N["route_e"], 1)
            act.wait_ge(N["tab_ready"], 1)
            total = act.value_load(tab_i[0:1, TOTAL:TOTAL + 1], min_val=NE, max_val=ALLBLK)
            with act.Fori(0, total) as n:
                act.wait_ge(N["g_full"], n + 1)
                nc.scalar.activation(h_sg, g_ps, ACT.Silu).then_inc(N["silu_done"], 1)
                act.wait_ge(N["ht_full"], n + 1)
                nc.scalar.activation(h_t, h_ps.rearrange("p (a b) -> p a b", b=BLK), ACT.Copy).then_inc(N["ht_done"], 1)
                act.wait_ge(N["yb_out"], 16 * n + 16)
                act.wait_ge(N["y_ready"], 2 * n + 1)
                nc.scalar.activation(y_b[:, 0:512], d_ps[0], ACT.Copy).then_inc(N["y_taken_a"], 1)
            act.wait_ge(N["x3_done"], len(TILES))
            rms(stream, view(E0 + 3072, D))

        @block.vector
        def _(dve):
            line = Line(dve, N["v_step"])
            vm = Mail(*v_mail)
            V = nc.vector

            def tt(out, x, y, op, sem=None):
                line.do(V.tensor_tensor(out, x, y, op), sem)

            def ts(out, x, s1, s2, op0, op1=None, sem=None):
                line.do(V.tensor_scalar(out, x, s1, s2, op0) if op1 is None else V.tensor_scalar(out, x, s1, s2, op0, op1), sem)

            def stt(out, x, s, y, op0, op1, sem=None):
                line.do(V.scalar_tensor_tensor(out=out, in0=x, scalar=s, in1=y, op0=op0, op1=op1), sem)

            def cp(out, x, sem=None):
                line.do(V.tensor_copy(out, x), sem)

            def tell(s):
                dve.sem_inc(s, 1)

            def q4(bank, w=P):
                return bank[:, 0:4 * w].rearrange("p (a b) -> p a b", b=w)

            def last_dim(x, n):
                return x.unsqueeze(len(x.shape)).to_broadcast(list(x.shape) + [n])

            def mid(x, n):
                return x.unsqueeze(1).to_broadcast([x.shape[0], n, x.shape[1]])

            def rstd(n, col):
                line.do(V.reciprocal(stat[0:n, col:col + 1], stat[0:n, col:col + 1]))

            def rsqrt(x, part):
                tell(N["sq_ready"])
                dve.wait_ge(N["sq_done"], part)
                line.do(V.reciprocal(x, x))
                tell(N["inv_ready"])

            def turned(dst, t0, n, gain):
                for half in range(2):
                    bank = vm.take(dve)
                    tt(dst[:, 4 * half:4 * half + 4, t0:t0 + n], q4(bank)[:, :, 0:n],
                       last_dim(gains[:, gain, 4 * half:4 * half + 4], n), ALU.mult, vm.freed)

            cp(prm[:, 0:NPRM], vm.take(dve)[:, 0:NPRM], vm.freed)
            ts(omka, prm[:, KA:KA + 4], -1.0, 1.0, ALU.mult, ALU.add)
            for i in range(len(TILES) + 1):
                if i < len(TILES):
                    n = TILES[i][1]
                    dve.wait_ge(N["rms"], 1)
                    rstd(n, i)
                    ts(xs_tmp[i % 2][0:n], x_res[0:n, i, :], stat[0:n, i:i + 1], None, ALU.mult)
                    tell(N["xs3_done"])
                if i >= 1:
                    turned(x_t, *TILES[i - 1], 0)
                    tell(N["xt_done"])
            dve.wait_ge(N["qkv_raw"], 1)
            for i in range(len(TILES) + 1):
                if i < len(TILES):
                    n = TILES[i][1]
                    qk = qkv[0:n, i, 0:2 * BW].rearrange("p (h d) -> p h d", d=64)
                    x1, x2 = qk[:, :, 0:8], qk[:, :, 8:16]
                    co = mid(C("rope")[0:n, 16 * i:16 * i + 8], 24)
                    si = mid(C("rope")[0:n, 16 * i + 8:16 * i + 16], 24)
                    tt(rt[0][0:n], x1, co, ALU.mult)
                    tt(rt[1][0:n], x2, si, ALU.mult)
                    tt(rt[2][0:n], x2, co, ALU.mult)
                    tt(rt[3][0:n], x1, si, ALU.mult)
                    tt(x1, rt[0][0:n], rt[1][0:n], ALU.subtract)
                    tt(x2, rt[2][0:n], rt[3][0:n], ALU.add)
                    tell(N["rope_done"])
                if i >= 1:
                    t0, n = TILES[i - 1]
                    for half in range(3):
                        cp(qk_t[:, 4 * half:4 * half + 4, t0:t0 + n], q4(vm.take(dve))[:, :, 0:n], vm.freed)

            def mask_unit(u):
                i, h = att[u]
                kb = key_blocks(i)
                s = s_sb[u % 3]
                at_ = 0
                for g in range(NG):
                    k = len([1 for gg, _ in kb if gg == g])
                    bank = vm.take(dve)
                    if k > 1:
                        tt(s[:, at_:at_ + (k - 1) * P].rearrange("p (a b) -> p a b", b=P),
                           bank[:, 0:(k - 1) * P].rearrange("p (a b) -> p a b", b=P), mid(C(f"off{g}"), k - 1), ALU.add)
                    tt(s[:, at_ + (k - 1) * P:at_ + k * P], bank[:, (k - 1) * P:k * P], C(f"diag{g}"), ALU.add, vm.freed)
                    at_ += k * P
                c = 8 + 4 * (u % 3)
                line.do(V.reduce_max(stat[:, c:c + 1], s[:, 0:at_], AX))
                ts(stat[:, c + 1:c + 2], stat[:, c:c + 1], -0.125, None, ALU.mult, sem=N["p_neg"])

            def scale_unit(u):
                i, h = att[u]
                n = P * len(key_blocks(i))
                c = 8 + 4 * (u % 3)
                dve.wait_ge(N["p_exp"], u + 1)
                line.do(V.reciprocal(stat[:, c + 3:c + 4], stat[:, c + 2:c + 3]))
                ts(s_sb[u % 3][:, 0:n], s_sb[u % 3][:, 0:n], stat[:, c + 3:c + 4], None, ALU.mult, sem=N["p_ready"])

            mask_unit(0)
            mask_unit(1)
            for u in range(len(att)):
                scale_unit(u)
                if u + 2 < len(att):
                    mask_unit(u + 2)
            dve.wait_ge(N["pv_taken"], len(att))
            line.do(V.memset(qblk, 0.0))
            for hh in range(2):
                lo = 64 * hh
                cp(qblk[lo:lo + 64, :, TS * hh:TS * hh + TS], qk_t[lo:lo + 64, 0:6, SEQ:T])
            tell(N["qblk_ready"])
            dve.wait_ge(N["kv_used"], len(units))
            cp(st_sb, aux[:, 0:NG * P].rearrange("p (a b) -> p a b", b=P))
            cp(stn_sb[0:TS], vm.take(dve)[0:TS, 0:NG * P].rearrange("p (a b) -> p a b", b=P), vm.freed)
            tell(N["snew"])
            tt(ps_sb, vm.take(dve)[:, 0:480], C("samp"), ALU.add, vm.freed)
            line.do(V.reduce_max(stat[:, 16:17], ps_sb, AX))
            ts(stat[:, 17:18], stat[:, 16:17], -0.125, None, ALU.mult, sem=N["sneg"])
            dve.wait_ge(N["sexp"], 1)
            line.do(V.reciprocal(stat[:, 19:20], stat[:, 18:19]))
            ts(ps_sb, ps_sb, stat[:, 19:20], None, ALU.mult, sem=N["s_soft"])
            cp(pts, vm.take(dve)[:, 0:NG * P].rearrange("p (a b) -> p a b", b=P), vm.freed)
            cp(ptn[0:TS], vm.take(dve)[0:TS, 0:NG * P].rearrange("p (a b) -> p a b", b=P), vm.freed)
            dve.wait_ge(N["kv_used"], 2 * len(units))
            for hh in range(2):
                lo = 64 * hh
                cp(yb_t[lo:lo + 64, :, SEQ:T], aux[lo:lo + 64, 0:P].rearrange("p (a b c) -> p a b c", b=2, c=TS)[:, :, hh, :])
            tell(N["yb_done"])
            us4 = u_s.rearrange("p j (b t) -> p j b t", t=NS)
            ums4 = um_s.rearrange("p j (b t) -> p j b t", t=NS)
            dve.wait_ge(N["out"], 16 * OUT_CACHES)
            for c in range(0, AJ, 4):
                k = min(4, AJ - c)
                cp(ums4[:, c:c + k, :, 0], vm.take(dve)[:, 0:k * NB].rearrange("p (a b) -> p a b", b=NB), vm.freed)
            seen = 0
            decay_rate = -float(np.exp(np.float32(-0.5)))

            def shift(js):
                nonlocal seen
                for j in js:
                    seen += 1
                    dve.wait_ge(N["u_raw"], seen)
                    ts(um_p[:, j, 0:1], u_p[:, j, 0:1], -1.0, None, ALU.mult)
                    tt(um_p[:, j, 1:SEQ], u_p[:, j, 0:SEQ - 1], u_p[:, j, 1:SEQ], ALU.subtract)
                    stt(um_p[:, j, :], um_p[:, j, :], prm[:, MU + j:MU + j + 1], u_p[:, j, :], ALU.mult, ALU.add)
                    cp(u_last[:, j:j + 1], u_p[:, j, SEQ - 1:SEQ])

            def norm_k(kk, k, aa, tmp, r, n, part):
                ts(inv[:, 0:n], vm.take(dve)[:, 0:n], 1e-24, None, ALU.max, sem=vm.freed)
                rsqrt(inv[:, 0:n], part)
                dve.wait_ge(N["sga"], part)
                for j in range(4):
                    ts(tmp[:, j], aa[:, j], prm[:, KA + j:KA + j + 1], omka[:, j:j + 1], ALU.mult, ALU.add)
                tt(k, k, tmp, ALU.mult)
                for j in range(4):
                    tt(kk[:, j], kk[:, j], vm.take(dve)[:, 0:n], ALU.mult, vm.freed)
                tt(aa, aa, kk, ALU.mult)
                tt(tmp, r, k, ALU.mult)
                tt(tmp, tmp, last_dim(prm[:, RK:RK + 4], n), ALU.mult, N["prep_sq"])

            c_all, sg_all = c_p.rearrange("p a b -> p (a b)"), sg_p.rearrange("p a b -> p (a b)")
            r, k, v = um_p[:, 0:4], um_p[:, 4:8], um_p[:, 8:12]
            shift(feats[0])
            tell(N["um_done"])
            shift(feats[1])
            tt(kk_p, k, last_dim(prm[:, KK_:KK_ + 4], SEQ), ALU.mult)
            tt(sq_p, kk_p, kk_p, ALU.mult, N["prep_sq"])
            dve.wait_ge(N["sga"], 1)
            ts(sg_p, sg_p, decay_rate, None, ALU.mult)
            for z in range(4 * NPT):
                chunk = slice(z * P, (z + 1) * P)
                line.do(V.tensor_tensor_scan(c_all[:, chunk], C("ones"), sg_all[:, chunk], 0.0, ALU.mult, ALU.add))
            c16 = c_p.rearrange("p j (i t) -> p (j i) t", t=P)
            pm16 = pmid.rearrange("p a b -> p (a b)")
            cp(pm16, c16[:, :, P // 2 - 1])
            tt(c16, c16, last_dim(pm16, P), ALU.subtract)
            tt(sg_p, c_p, sg_p, ALU.subtract)
            shift(feats[2])
            tell(N["prep_e"])
            norm_k(kk_p, k, a_p, sq_p, r, SEQ, 1)
            dve.wait_ge(N["exp_done"], 1)
            tt(r, r, tmp_p, ALU.mult)
            cp(pend.rearrange("p a b -> p (a b)"), tmp_p.rearrange("p j (i t) -> p (j i) t", t=P)[:, :, P - 1])
            stt(kk_p.rearrange("p a b -> p (a b)"), kk_p.rearrange("p a b -> p (a b)"), -1.0, sg_p.rearrange("p a b -> p (a b)"), ALU.mult, ALU.mult)
            tt(k, k, c_p, ALU.mult)
            tt(a_p, a_p, c_p, ALU.mult)
            tell(N["prep_done"])
            shift(feats[3])
            tt(ums4[:, :, :, 0], ums4[:, :, :, 0], us4[:, :, :, 0], ALU.subtract)
            tt(ums4[:, :, :, 1:NS], us4[:, :, :, 0:NS - 1], us4[:, :, :, 1:NS], ALU.subtract)
            tt(um_s, um_s, last_dim(prm[:, MU:MU + AJ], TS), ALU.mult)
            tt(um_s, um_s, u_s, ALU.add)
            tell(N["um_done"])
            for j in range(4):
                tt(bon_p[:, j], vm.take(dve)[:, :], v[:, j], ALU.mult, vm.freed)
            rs_, ks_, vs_ = um_s[:, 0:4], um_s[:, 4:8], um_s[:, 8:12]
            tt(kk_s, ks_, last_dim(prm[:, KK_:KK_ + 4], TS), ALU.mult)
            tt(tmp_s, kk_s, kk_s, ALU.mult, N["prep_sq"])
            for i in range(NPT):
                cp(tm_b[:, i, :], vm.take(dve)[:, :], vm.freed)
            norm_k(kk_s, ks_, a_s, tmp_s, rs_, TS, 2)
            for i in range(NPT):
                cp(tm_k[:, i, :], vm.take(dve)[:, :], vm.freed)
            for j in range(4):
                tt(bon_s[:, j], vm.take(dve)[:, 0:TS], vs_[:, j], ALU.mult, vm.freed)
            dve.wait_ge(N["exp_done"], 2)
            tell(N["tm_done"])
            for i in range(NPT):
                cp(tm_v[:, i, :], vm.take(dve)[:, :], vm.freed)
            for c in range(0, AJ, 4):
                w = P * min(4, AJ - c)
                cp(last_s[0:NB, c * P:c * P + w], vm.take(dve)[0:NB, 0:w], vm.freed)
            cp(last_p, vm.take(dve)[64:64 + AJ, 0:P], vm.freed)
            tell(N["shift_ready"])
            for z in range(6):
                cp(tok_s[0:TS, z, :], vm.take(dve)[0:TS, :], vm.freed)
            tell(N["stm_done"])
            dve.wait_ge(N["shift_out"], 32)
            line.do(V.memset(st0, 0.0))
            line.do(V.memset(st0m, 0.0))
            for i in range(NPT):
                for dst, mask, plus in ((mat_l, None, None), (mat_t, "low1t", 1), (mat_ak, "strict", 0), (mat_rb, "incl", 0), (mat_rk, "incl", 0)):
                    for par in range(2):
                        bank = vm.take(dve)
                        d4 = dst[:, 4 * par:4 * par + 4, :]
                        if mask is None:
                            cp(d4, q4(bank), vm.freed)
                        else:
                            tt(d4, q4(bank), mid(C(mask), 4), ALU.mult, vm.freed)
                            if plus:
                                tt(d4, d4, mid(ident, 4), ALU.add)
                tt(mat_tt, mat_l, mid(C("low1"), 8), ALU.mult)
                tt(mat_tt, mat_tt, mid(ident, 8), ALU.add)
                tt(mat_lm, mat_l, mid(C("low2"), 8), ALU.mult, N["lm_ready"])
                for lv, m in enumerate(LEVELS[1:]):
                    final = m == LEVELS[-1]
                    for par in range(2):
                        cp(mat_w[:, 4 * par:4 * par + 4, :], q4(vm.take(dve)), vm.freed)
                    if not final:
                        tt(mat_lm, mat_l, mid(C(f"low{2 * m}"), 8), ALU.mult, N["lm_ready"])
                    for par in range(2):
                        for dst in ((mat_t, mat_tt) if not final else (mat_tt,)):
                            d4 = dst[:, 4 * par:4 * par + 4, :]
                            tt(d4, d4, q4(vm.take(dve)), ALU.add, vm.freed)
                for par in range(2):
                    cp(w_sb[:, 4 * par:4 * par + 4, :], q4(vm.take(dve), 64), vm.freed)
                cp(uu_sb, vm.take(dve)[:, :].rearrange("p (a b) -> p a b", b=64), vm.freed)
                tt(st0, st0m, q4(vm.take(dve), 64), ALU.add, vm.freed)
                tt(st0, st0, last_dim(pend[:, :, i], 64), ALU.mult)
                dve.wait_ge(N["mats"], i + 1)
                if i + 1 < NPT:
                    tt(st0m, st0, last_dim(pmid[:, :, i + 1], 64), ALU.mult)
                tell(N["state_ready"])
            cp(fin_s[0:64], vm.take(dve)[0:64, :], vm.freed)
            tell(N["fin_ready"])
            cp(y_s, vm.take(dve)[:, 0:4 * TS].rearrange("p (a b) -> p a b", b=TS), vm.freed)
            dve.wait_ge(N["y_raw"], 1)
            for part in range(2):
                n = TS if part == 0 else SEQ
                y, tmp, bon, gg = (y_s, tmp_s, bon_s, g_s) if part == 0 else (a_p, tmp_p, bon_p, g_p)
                tell(N["ysq"])
                for j in range(4):
                    stt(y[:, j], vm.take(dve)[:, 0:n], -1.0 / AD, y[:, j], ALU.mult, ALU.add, vm.freed)
                tt(tmp, y, y, ALU.mult)
                tell(N["ysq"])
                ts(inv[:, 0:n], vm.take(dve)[:, 0:n], 1.0 / AD, LNX_EPS, ALU.mult, ALU.add, sem=vm.freed)
                rsqrt(inv[:, 0:n], part + 3)
                for j in range(4):
                    tt(y[:, j], y[:, j], vm.take(dve)[:, 0:n], ALU.mult, vm.freed)
                    ts(y[:, j], y[:, j], prm[:, LG + j:LG + j + 1], prm[:, LB + j:LB + j + 1], ALU.mult, ALU.add)
                tt(y, y, bon, ALU.add)
                tt(y_all[:, :, SEQ:T] if part == 0 else y_all[:, :, 0:SEQ], y, gg, ALU.mult)
                if part == 0:
                    tell(N["ring_spare"])
            tell(N["ya_done"])
            z = 0
            for j in range(KT):
                for t0, n in HALVES:
                    dve.wait_ge(N["sig_done"], z + 1)
                    tt(mg[:, 0:n], vm.take(dve)[:, 0:n], gate_sb[j % 3][:, 0, t0:t0 + n], ALU.mult, vm.freed)
                    tt(m_t[:, j, t0:t0 + n], vm.take(dve)[:, 0:n], gate_sb[j % 3][:, 1, t0:t0 + n], ALU.mult, vm.freed)
                    tt(m_t[:, j, t0:t0 + n], m_t[:, j, t0:t0 + n], mg[:, 0:n], ALU.add, N["gate_used"])
                    z += 1
            tell(N["merged"])

            def add_rows():
                for i, (t0, m) in enumerate(TILES):
                    for c in range(2):
                        x = x_res[0:m, i, c * 512:(c + 1) * 512]
                        tt(x, x, vm.take(dve)[0:m, :], ALU.add, vm.freed)

            add_rows()
            tell(N["x1_done"])
            def norm_turn(srcs, col0, gain, dst):
                for i in range(len(srcs) + 1):
                    if i < len(srcs):
                        x, t0, n = srcs[i]
                        dve.wait_ge(N["rms"], 2)
                        rstd(n, col0 + i)
                        ts(xs2[i % 2][0:n], x, stat[0:n, col0 + i:col0 + i + 1], None, ALU.mult)
                        tell(N["memx"])
                    if i >= 1:
                        turned(dst, srcs[i - 1][1], srcs[i - 1][2], gain)

            norm_turn([(mem_x[:, i, :], i * P, P) for i in range(2)], 0, 2, mem_t)
            for c in range(2):
                for i in range(2):
                    cp(mkv[:, i, c * 512:(c + 1) * 512], vm.take(dve)[:, :], vm.freed)
            tell(N["mkv_done"])
            for i in range(2):
                cp(mk_t[:, :, i * P:(i + 1) * P], q4(vm.take(dve)), vm.freed)
            norm_turn([(x_res[0:n, i, :], t0, n) for i, (t0, n) in enumerate(TILES)], 2, 1, x_t)
            for h in range(MH):
                for t0, n in HALVES:
                    cp(q_t[:, h, t0:t0 + n], vm.take(dve)[:, 0:n], vm.freed)
            MS = float(MD) ** -0.5
            nu = len(mem_units)

            def mem_mask(u):
                c = 20 + 4 * (u % 3)
                cp(ms_sb[u % 3], vm.take(dve)[:, 0:MEM], vm.freed)
                line.do(V.reduce_max(stat[:, c:c + 1], ms_sb[u % 3], AX))
                ts(stat[:, c + 1:c + 2], stat[:, c:c + 1], -MS, None, ALU.mult, sem=N["m_neg"])

            def mem_scale(u):
                c = 20 + 4 * (u % 3)
                dve.wait_ge(N["m_exp"], u + 1)
                line.do(V.reciprocal(stat[:, c + 3:c + 4], stat[:, c + 2:c + 3]))
                ts(ms_sb[u % 3], ms_sb[u % 3], stat[:, c + 3:c + 4], None, ALU.mult, sem=N["m_ready"])

            mem_mask(0)
            mem_mask(1)
            for u in range(nu):
                mem_scale(u)
                if u + 2 < nu:
                    mem_mask(u + 2)
            dve.wait_ge(N["mkv_used"], NB)
            cp(mst, aux[:, 0:2 * P].rearrange("p (a b) -> p a b", b=P), N["mst_ready"])
            mem_mask(nu)
            mem_scale(nu)
            dve.wait_ge(N["mkv_used"], 2 * NB)
            cp(o_t[:, :, SEQ:T], aux[:, 0:MH * TS].rearrange("p (a b) -> p a b", b=TS), N["mo_done"])
            add_rows()
            tell(N["x2_done"])
            for i, (t0, n) in enumerate(TILES):
                dve.wait_ge(N["rms"], 3)
                rstd(n, i)
                if i == 0:
                    dve.wait_ge(N["mkv_out"], 32)
                ts(xs3[0:n, i, :], x_res[0:n, i, :], stat[0:n, i:i + 1], None, ALU.mult)
                tell(N["xs3_done"])
            ru = rs.bitcast(U32)
            dve.wait_ge(N["rb_in"], 32)
            for i, (t0, n) in enumerate(TILES):
                turned(x_t, t0, n, 3)
                z = slice(0, n)
                tt(lg[z], vm.take(dve)[z, 0:36], rbias[z], ALU.add, vm.freed)
                line.do(V.memset(rs[z, 0:8], 2 * NEG))
                cp(rs[z, 0:4], lg[z, 0:4])
                line.do(V.max(rs[z, 8:16], rs[z, 0:8]))
                line.do(V.max_index(ru[z, 16:24], rs[z, 8:16], rs[z, 0:8]))
                cp(rs[z, 30:31], ru[z, 16:17])
                ts(rs[z, 24:25], rs[z, 8:9], -1.0, None, ALU.mult)
                ts(rs[z, 32:64], C("grp")[z], rs[z, 30:31], None, ALU.is_equal)
                ts(rs[z, 64:96], rs[z, 32:64], -NEG, NEG, ALU.mult, ALU.add)
                tt(rs[z, 96:128], lg[z, 4:36], rs[z, 32:64], ALU.mult)
                tt(rs[z, 96:128], rs[z, 96:128], rs[z, 64:96], ALU.add)
                line.do(V.max(rs[z, 128:136], rs[z, 96:128]))
                line.do(V.max_index(ru[z, 136:144], rs[z, 128:136], rs[z, 96:128]))
                cp(rs[z, 144:146], ru[z, 136:138])
                for k in range(2):
                    ts(hot[z, i, NE * k:NE * k + NE], C("iota")[z], rs[z, 144 + k:145 + k], None, ALU.is_equal)
                tt(rs[z, 26:27], rs[z, 129:130], rs[z, 128:129], ALU.subtract)
                tell(N["route_a"])
                dve.wait_ge(N["route_e"], i + 1)
                ts(rs[z, 28:29], rs[z, 27:28], 1.0, None, ALU.add)
                tt(rs[z, 28:29], rs[z, 28:29], rs[z, 25:26], ALU.mult)
                line.do(V.reciprocal(gate[z, i, 0:1], rs[z, 28:29]))
                tt(gate[z, i, 1:2], gate[z, i, 0:1], rs[z, 27:28], ALU.mult)
            tell(N["hot_done"])
            bank = vm.take(dve)
            cnt, base, nblk = rs[:, 0:32], rs[:, 32:64], rs[:, 64:96]
            cp(cnt, bank[:, 0:NE])
            tt(cnt, cnt, bank[:, NE:2 * NE], ALU.add, vm.freed)
            one = C("ones")[:, 0:NE]
            line.do(V.tensor_tensor_scan(base, one, cnt, 0.0, ALU.mult, ALU.add))
            tt(base, base, cnt, ALU.subtract)
            tt(cnt3, last_dim(cnt, MAXBLK - 1), mid(C("thr"), NE), ALU.is_gt)
            line.do(V.reduce_sum(nblk, cnt3, AX))
            ts(nblk, nblk, 1.0, None, ALU.add)
            first_ = rs[:, 96:128]
            line.do(V.tensor_tensor_scan(first_, one, nblk, 0.0, ALU.mult, ALU.add))
            cp(tab_i[:, TOTAL:TOTAL + 1], first_[:, NE - 1:NE])
            tt(first_, first_, nblk, ALU.subtract)
            cp(tab_i[:, FIRST:FIRST + NE], first_)
            cp(tab_i[:, COUNT:COUNT + NE], nblk)
            tt(row3, mid(first_, NTAB), last_dim(C("count"), NE), ALU.is_gt)
            stt(nblk, first_, -float(BLK), base, ALU.mult, ALU.add)
            stt(row3, row3, 1e6, mid(nblk, NTAB), ALU.mult, ALU.add)
            line.do(V.tensor_reduce(rs[:, 128:128 + NTAB], row3, AX, ALU.min))
            stt(rs[:, 128:128 + NTAB], C("count"), float(BLK), rs[:, 128:128 + NTAB], ALU.mult, ALU.add)
            ts(tab_i[:, ROW:ROW + NTAB], rs[:, 128:128 + NTAB], float(ROWS), None, ALU.min)
            tell(N["tab_ready"])
            for i, (t0, n) in enumerate(TILES):
                z = slice(0, n)
                bank = vm.take(dve)
                tt(rs[z, 128:160], bank[z, 0:NE], base[z], ALU.add)
                tt(rs[z, 128:160], rs[z, 128:160], bank[z, NE:2 * NE], ALU.add, vm.freed)
                for k in range(2):
                    tt(rs[z, 160:192], rs[z, 128:160], hot[z, i, NE * k:NE * k + NE], ALU.mult)
                    line.do(V.reduce_sum(slot_f[z, 2 * i + k:2 * i + k + 1], rs[z, 160:192], AX))
                cp(slot_i[z, 2 * i:2 * i + 2], slot_f[z, 2 * i:2 * i + 2])
            tell(N["route_done"])
            def take_block():
                for half in range(2):
                    k = slice(4 * half, 4 * half + 4)
                    last = V.tensor_tensor(x_e[:, k, :], x_ps[half].rearrange("p (a b) -> p a b", b=BLK), last_dim(gains[:, 3, k], BLK), ALU.mult)
                last.then_inc(N["xe_ready"], 1)

            dve.wait_ge(N["scattered"], 16 * 2 * len(TILES))
            dve.wait_ge(N["xb_used"], 1)
            take_block()
            total = dve.value_load(tab_i[0:1, TOTAL:TOTAL + 1], min_val=NE, max_val=ALLBLK)
            with dve.Fori(0, total) as n:
                dve.wait_ge(N["silu_done"], n + 1)
                dve.wait_ge(N["u_full"], n + 1)
                V.tensor_tensor(h_b, h_sg, u_ps, ALU.mult).then_inc(N["h_done"], 1)
                dve.wait_ge(N["xb_used"], n + 2)
                take_block()
                dve.wait_ge(N["yb_out"], 16 * n + 16)
                dve.wait_ge(N["y_ready"], 2 * n + 2)
                V.tensor_copy(y_b[:, 512:1024], d_ps[1]).then_inc(N["y_taken_v"], 1)
            for i, (t0, n) in enumerate(TILES):
                for k in range(2):
                    dve.wait_ge(N["yg_in"], 16 * 2 * len(TILES))
                    stt(x_res[0:n, i, :], yg[2 * i + k][0:n], gate[0:n, i, k:k + 1], x_res[0:n, i, :], ALU.mult, ALU.add, N["yg_used"])
                tell(N["x3_done"])
            dve.wait_ge(N["gfin_in"], 16)
            for i, (t0, n) in enumerate(TILES):
                dve.wait_ge(N["rms"], 4)
                rstd(n, i)
                stt(x_res[0:n, i, :], x_res[0:n, i, :], stat[0:n, i:i + 1], gfin[0:n], ALU.mult, ALU.mult)
                tell(N["y_final"])

        @block.gpsimd
        def _(pool):
            line = Line(pool, N["pool_step"])
            G = nc.gpsimd

            def tt(out, x, y, op):
                line.do(G.tensor_tensor(out, x, y, op))

            pool.wait_ge(N["ring_used"], NA - 1)
            copied = 0
            for g, (window, _) in enumerate(GROUPS):
                for b in range(NB):
                    src = caches[g][b, :, NS:window].rearrange("k (r q) h d -> k r (q h d)", q=NS)
                    dst = o[f"s_cache{g}"][b, :, 0:window - NS].rearrange("k (r q) h d -> k r (q h d)", q=NS)
                    if copied:
                        pool.wait_ge(N["copies"], 16 * copied)
                    pool.dma_start(dst, src).then_inc(N["copies"], 16)
                    copied += 1
            pool.wait_ge(N["shift_ready"], 1)
            pool.dma_start(o["s_shift"][:, :], last_s[0:NB, :]).then_inc(N["shift_out"], 16)
            pool.dma_start(o["p_shift"][0].rearrange("(j p) -> j p", p=P), last_p).then_inc(N["shift_out"], 16)
            pool.wait_ge(N["srec_in"], 16 * 2 * (6 * NB + 1))
            line.do(G.memset(rec_sa[:, 0, :], 0.0))
            for t in range(NS):
                def vec(n):
                    return rec[:, n, t * 64:(t + 1) * 64].unsqueeze(1).to_broadcast([P, 32, 64])

                def val(x):
                    return x.unsqueeze(2).to_broadcast([P, 32, 64])

                def row_sums(dst, src):
                    w = 32
                    while w >= 1:
                        last = dst.unsqueeze(2) if w == 1 else src[:, :, 0:w]
                        tt(last, src[:, :, 0:w], src[:, :, w:2 * w], ALU.add)
                        w //= 2

                tt(rec_t, rec_s, vec(2), ALU.mult)
                row_sums(rec_sa[:, 0, :], rec_t)
                tt(rec_s, rec_s, vec(4), ALU.mult)
                tt(rec_t, val(rec_sa[:, 0, :]), vec(3), ALU.mult)
                tt(rec_s, rec_s, rec_t, ALU.subtract)
                tt(rec_t, val(rec_v[:, t, :]), vec(1), ALU.mult)
                tt(rec_s, rec_s, rec_t, ALU.add)
                tt(rec_t, rec_s, vec(0), ALU.mult)
                row_sums(rec_y[:, t, :], rec_t)
            for hf in range(2):
                rows = slice(hf * 64, (hf + 1) * 64)
                dst = o["s_rwkv"].rearrange("b h (f v) k -> (b h) f (v k)", f=2)[:, hf]
                pool.dma_start(dst, rec_s[rows].rearrange("p v k -> p (v k)")).then_inc(N["state_out"], 16)
                for b in range(NB):
                    r8 = slice(hf * 64 + b * AH, hf * 64 + (b + 1) * AH)
                    dst = yrec_d[b * NS:(b + 1) * NS, :].rearrange("t (h f k) -> h f t k", h=AH, f=2)[:, hf]
                    pool.dma_start(dst, rec_y[r8]).then_inc(N["yrec_out"], 16)
            pool.wait_ge(N["yrec_out"], 16 * 2 * NB)
            pool.dma_start(y_tok[0:TS, :], yrec_d[:, :]).then_inc(N["yrec_in"], 16)
            pool.wait_ge(N["state_out"], 32)
            pool.wait_ge(N["fin_ready"], 1)
            pool.dma_start(o["p_rwkv"][0].rearrange("h v k -> v h k"), fin_s[0:64].rearrange("p (h k) -> p h k", k=64))\
                .then_inc(N["state_out"], 16)
            pool.wait_ge(N["mkv_done"], 1)
            for i in range(2):
                pool.dma_start(o["p_mem"][0, :, i * P:(i + 1) * P].rearrange("k p h d -> p k (h d)"),
                               mkv[:, i, :].rearrange("p (k c) -> p k c", k=2)).then_inc(N["mkv_out"], 16)
            pool.wait_ge(N["x2_done"], 1)
            line.do(G.memset(xb, 0.0))
            pool.dma_start(xs_d[ROWS:ROWS + BLK, :], xb).then_inc(N["pad_out"], 16)
            pool.dma_start(ys_d[ROWS:ROWS + BLK, :], xb).then_inc(N["yb_out"], 16)
            pool.dma_start(rbias[:, 0:4], a["b_router_group"].partition_broadcast(P)).then_inc(N["rb_in"], 16)
            pool.dma_start(rbias[:, 4:36], a["b_router_expert"].partition_broadcast(P)).then_inc(N["rb_in"], 16)
            pool.wait_ge(N["route_done"], 1)
            for i, (t0, n) in enumerate(TILES):
                for k in range(2):
                    pool.indirect_dma_start(out=xs_d[0:ROWS, :], out_offset=bass.IndirectOffsetOnAxis(ap=slot_i[0:n, 2 * i + k:2 * i + k + 1], axis=0),
                                            in_=xs3[0:n, i, :], in_offset=None, bounds_check=ROWS - 1).then_inc(N["scattered"], 16)
            pool.wait_ge(N["scattered"], 16 * 2 * len(TILES))
            pool.wait_ge(N["pad_out"], 16)
            pool.wait_ge(N["yb_out"], 16)
            row0 = pool.value_load(tab_of(ROW, 0), min_val=0, max_val=ROWS)
            pool.dma_start(xb, xs_d[bass.ds(row0, BLK), :]).then_inc(N["xb_in"], 16)
            total = pool.value_load(tab_i[0:1, TOTAL:TOTAL + 1], min_val=NE, max_val=ALLBLK)
            with pool.Fori(0, total) as n:
                row = pool.value_load(tab_of(ROW, n), min_val=0, max_val=ROWS)
                ahead = pool.value_load(tab_of(ROW, n + 1), min_val=0, max_val=ROWS)
                pool.wait_ge(N["xb_used"], n + 1)
                pool.sem_inc(N["seen"], 1)
                pool.dma_start(xb, xs_d[bass.ds(ahead, BLK), :]).then_inc(N["xb_in"], 16)
                pool.wait_ge(N["y_taken_a"], n + 1)
                pool.wait_ge(N["y_taken_v"], n + 1)
                pool.wait_ge(N["yb_out"], 16 * n + 16)
                pool.sem_inc(N["seen"], 1)
                pool.dma_start(ys_d[bass.ds(row, BLK), :], y_b).then_inc(N["yb_out"], 16)
            pool.wait_ge(N["yb_out"], 16 * total + 16)
            pool.sem_inc(N["seen"], 1)
            pool.dma_start(gfin, a["norm_final_g"].partition_broadcast(P)).then_inc(N["gfin_in"], 16)
            for i, (t0, n) in enumerate(TILES):
                for k in range(2):
                    pool.indirect_dma_start(out=yg[2 * i + k][0:n], out_offset=None, in_=ys_d[0:ROWS, :],
                                            in_offset=bass.IndirectOffsetOnAxis(ap=slot_i[0:n, 2 * i + k:2 * i + k + 1], axis=0),
                                            bounds_check=ROWS - 1).then_inc(N["yg_in"], 16)
            for i, (t0, n) in enumerate(TILES):
                pool.wait_ge(N["y_final"], i + 1)
                dst = o["y_prompt"][0, t0:t0 + n, :] if t0 < SEQ else o["y_sample"].rearrange("b t d -> (b t) d")
                pool.dma_start(dst, x_res[0:n, i, :]).then_inc(N["y_out"], 16)
            pool.wait_ge(N["y_out"], 16 * len(TILES))
            pool.wait_ge(N["copies"], 16 * NG * NB)
            pool.wait_ge(N["shift_out"], 32)
            pool.wait_ge(N["state_out"], 48)
            pool.wait_ge(N["mkv_out"], 32)


_INS = ['x_prompt', 'x_sample', 'state_rwkv', 'state_shift', 'cache_swa_w128', 'cache_swa_w512', 'cache_swa_w2048',
        'cache_mem_kv', 'mem_prompt', 'norm_mix_g', 'w_in', 'b_gate', 'rwkv_mu', 'rwkv_w0', 'rwkv_w2', 'rwkv_a0', 'rwkv_a2',
        'rwkv_g2', 'rwkv_k_k', 'rwkv_k_a', 'rwkv_r_k', 'rwkv_lnx_g', 'rwkv_lnx_b', 'w_branch_a', 'w_branch_b', 'w_out',
        'norm_mem_g', 'norm_memkv_g', 'w_mem_q', 'w_mem_kv', 'w_mem_out', 'norm_ffn_g', 'w_router_group', 'b_router_group',
        'w_router_expert', 'b_router_expert', 'w_exp_gate', 'w_exp_up', 'w_exp_down', 'norm_final_g']
_OUTS = [('y_prompt', (1, SEQ, D)), ('y_sample', (NB, NS, D)), ('p_rwkv', (1, AH, AD, AD)), ('p_shift', (1, APROJ)),
         ('p_cache0', (1, 2, 128, 4, 64)), ('p_cache1', (1, 2, 512, 4, 64)), ('p_cache2', (1, 2, 512, 4, 64)),
         ('p_mem', (1, 2, MEM, MH, MD)), ('s_rwkv', (NB, AH, AD, AD)), ('s_shift', (NB, APROJ)),
         ('s_cache0', (NB, 2, 128, 4, 64)), ('s_cache1', (NB, 2, 512, 4, 64)), ('s_cache2', (NB, 2, 2048, 4, 64))]


def kernel(**inputs):
    import concourse.bacc as _bacc
    from concourse.bass_utils import run_bass_kernel_spmd as _run

    nc = _bacc.Bacc("TRN2", target_bir_lowering=False, num_devices=1)
    arrays, ins, outs = {}, {}, {}
    for name in _INS:
        x = np.ascontiguousarray(inputs[name])
        arrays[f"in_{name}"] = x
        ins[name] = nc.dram_tensor(f"in_{name}", x.shape, mybir.dt.from_np(x.dtype), kind="ExternalInput").ap()
    table = np.concatenate(list(constants().values()), axis=1)
    arrays["constants"] = table
    cst = nc.dram_tensor("constants", table.shape, F32, kind="ExternalInput").ap()
    for name, shape in _OUTS:
        outs[name] = nc.dram_tensor(f"out_{name}", shape, F32, kind="ExternalOutput").ap()
    build(nc, ins, outs, cst)
    r = _run(nc, [arrays], core_ids=[0])
    return tuple(r.results[0][f"out_{name}"] for name, _ in _OUTS)
```

```python
from contextlib import ExitStack

import numpy as np
import concourse.bass as bass
from concourse import mybir

F32 = mybir.dt.float32
I32 = mybir.dt.int32
U32 = mybir.dt.uint32
ALU = mybir.AluOpType
ACT = mybir.ActivationFunctionType
AX = mybir.AxisListType.X

P = 128
D = 1024
KT = D // P
SEQ = 512
NB = 8
NS = 4
TS = NB * NS
T = SEQ + TS
TILES = [(i * P, P) for i in range(SEQ // P)] + [(SEQ, TS)]
HALVES = [(0, T // 2), (T // 2, T // 2)]
NPT = SEQ // P
PAST = 2048
AH, AD = 8, 64
AW = AH * AD
APROJ = 3 * AW + 64 + 64 + 128
AJ = APROJ // P
GROUPS = ((128, 1), (512, 4), (2048, 16))
NG = len(GROUPS)
BW = 4 * NG * 64
BPROJ = 3 * BW
MEM = 256
MH, MD = 4, 128
MW = MH * MD
NE, NGR, EPG = 32, 4, 8
FF = 512
EPS = 1e-6
LNX_EPS = 64e-5
NEG = -1e30
BLK = P
ROWS = 2 * T
MAXBLK = -(-T // BLK)
ALLBLK = NE + ROWS // BLK
NTAB = ALLBLK + 1
LEVELS = (1, 2, 4, 8, 16, 32, 64)


def constants():
    q, k = np.arange(P)[:, None], np.arange(P)[None, :]
    out = {}

    def put(name, a):
        out[name] = np.ascontiguousarray(np.broadcast_to(a, (P, a.shape[-1])), dtype=np.float32)

    put("ident", (q == k) * 1.0)
    put("ones", np.ones((P, P)))
    put("blk", (q // AD == k // AD) * 1.0)
    put("strict", (q < k) * 1.0)
    put("incl", (q <= k) * 1.0)
    for m in LEVELS:
        put(f"low{m}", ((q // (2 * m) == k // (2 * m)) & ((k // m) % 2 == 1) & ((q // m) % 2 == 0)) * 1.0)
    put("low1t", ((q // 2 == k // 2) & (q % 2 == 1) & (k % 2 == 0)) * 1.0)
    put("off0", np.where(k >= q, 0, NEG))
    put("diag0", np.where(k <= q, 0, NEG))
    for g in (1, 2):
        dil = GROUPS[g][1]
        put(f"off{g}", np.where((q - k) % dil == 0, 0, NEG))
        put(f"diag{g}", np.where(((q - k) % dil == 0) & (k <= q), 0, NEG))
    tok = np.arange(P) % TS
    b, t = tok // NS, tok % NS
    nb, nt = np.arange(TS) // NS, np.arange(TS) % NS
    cached = [np.where(k >= t[:, None], 0, NEG), np.zeros((P, P)), np.zeros((P, P))]
    same = b[:, None] == nb[None, :]
    new = [np.where(same & (nt[None, :] <= t[:, None]), 0, NEG)] + [np.where(same & (nt[None, :] == t[:, None]), 0, NEG)] * 2
    put("pick", np.arange(NS)[None, :] == t[:, None])
    put("samp", np.concatenate(cached + new, axis=1))
    put("spread", (q % 32 == np.where(k < AD, 0, 31)) * 1.0)
    half = 8
    inv = (np.float32(500000.0) ** (-np.arange(half, dtype=np.float32) * np.float32(2.0) / np.float32(16))).astype(np.float32)
    rope = np.zeros((P, len(TILES), 2 * half), np.float32)
    for i, (t0, n) in enumerate(TILES):
        pos = np.arange(t0, t0 + n) if t0 < SEQ else PAST + np.arange(TS) % NS
        ang = pos.astype(np.float32)[:, None] * inv[None, :]
        rope[:n, i, :half], rope[:n, i, half:] = np.cos(ang), np.sin(ang)
    put("rope", rope.reshape(P, -1))
    put("iota", np.arange(NE)[None, :] * 1.0)
    put("grp", (np.arange(NE) // EPG)[None, :] * 1.0)
    put("eps", np.full((1, 1), EPS))
    put("count", np.arange(NTAB)[None, :] * 1.0)
    put("thr", (BLK * (1 + np.arange(MAXBLK - 1)))[None, :] * 1.0)
    return out


def const_layout():
    at, n = {}, 0
    for name, a in constants().items():
        at[name] = (n, a.shape[1])
        n += a.shape[1]
    return at, n


class Mail:

    def __init__(self, banks, filled, freed):
        self.banks, self.filled, self.freed = banks, filled, freed
        self.put = self.got = 0

    def claim(self, pe):
        if self.put >= len(self.banks):
            pe.wait_ge(self.freed, self.put - len(self.banks) + 1)
        self.put += 1
        return self.banks[(self.put - 1) % len(self.banks)]

    def take(self, eng):
        eng.wait_ge(self.filled, self.got + 1)
        self.got += 1
        return self.banks[(self.got - 1) % len(self.banks)]


class Line:

    def __init__(self, eng, step):
        self.eng, self.step, self.n = eng, step, {}

    def do(self, ins, sem=None):
        key = sem or self.step
        ins.then_inc(key, 1)
        self.n[key.name] = self.n.get(key.name, 0) + 1
        self.eng.wait_ge(key, self.n[key.name])



def build(nc, a, o, cst):
    with ExitStack() as ctx:
        def sem(name):
            return ctx.enter_context(nc.semaphore(name))

        CL, NC = const_layout()
        cols = (nc.sbuf_usable_end - nc.sbuf_base) // 4 // 16 * 16 - 16
        arena = ctx.enter_context(nc.sbuf_tensor("arena", [P, cols], F32))
        top = [0]

        def at(n):
            top[0] += n
            return top[0] - n

        def view(off, *shape):
            n = int(np.prod(shape))
            v = arena[:, off:off + n]
            if len(shape) == 2:
                v = v.rearrange("p (a b) -> p a b", b=shape[1])
            if len(shape) == 3:
                v = v.rearrange("p (a b c) -> p a b c", b=shape[1], c=shape[2])
            return v

        con = view(at(NC), NC)
        x_res = view(at(5 * D), 5, D)
        x_t = view(at(KT * T), KT, T)
        prm = view(at(64), 64)
        gains = view(at(4 * KT), 4, KT)
        omka = view(at(4), 4)
        lora = view(at(2 * AW), 2, AW)
        wr = view(at(KT * 36), KT, 36)
        yb_t = view(at(2 * T), 2, T)
        stat = view(at(64), 64)
        ring_at = at(2 * 4096)
        ring = [view(ring_at + 4096 * s, KT, 512) for s in range(2)]
        AR = top[0]

        def C(name):
            n, w = CL[name]
            return con[:, n:n + w]

        ident = C("ident")
        MU, W0, A0, KK_, KA, RK, LG, LB, BG = 0, 14, 18, 22, 26, 30, 34, 38, 42
        NPRM = 58

        qkv = view(AR, 5, BPROJ)
        qk_t = view(AR + 5 * BPROJ, 12, T)
        rt = [view(AR + 5 * BPROJ + 12 * T + 192 * n, 24, 8) for n in range(4)]
        s0 = AR + 5 * BPROJ + 12 * T + 768
        s_sb = [view(s0 + c, 1280) for c in (0, 1280, 8320)]
        p_t = [view(s0 + 2560 + 1280 * n, 10, P) for n in range(2)]
        kvb = [view(s0 + 5120 + 1024 * n, 4, 256) for n in range(3)]
        row_b = view(s0 + 5120 + 3072, P)
        assert s0 + 8320 + 1280 <= cols, (s0, cols)
        xs_tmp = [view(s0 + 1024 * n, D) for n in range(2)]
        kt_s = [view(s0 + 1280 + 1024 * n, 8, P) for n in range(2)]
        q_new = view(s0 - 768, NG * 2, P)
        q_own = view(ring_at, NG * 2, NB, P)
        p_own0 = view(AR + 5 * BPROJ, NB, P)
        p_own = view(AR + 5 * BPROJ + NB * P, TS, P)
        own_tmp = view(s0 + 8320, NS, P)
        y_own = view(s0 + 8320 + 512, 64)
        ps_sb = view(s0, 480)
        pts = view(s0 + 512, NG, P)
        ptn = view(s0 + 896, NG, P)

        U = AR
        u_p, u_s = view(U, AJ, SEQ), view(U + 7168, AJ, TS)
        UM = AR + 7616
        um_p, um_s = view(UM, AJ, SEQ), view(UM + 7168, AJ, TS)
        SL = UM + 7616
        a_p, kk_p, sg_p, c_p, g_p, bon_p = (view(SL + 2048 * n, 4, SEQ) for n in range(6))
        sq_p = bon_p
        SM = SL + 6 * 2048
        tmp_p, tm_b, tm_k = (view(U + 2048 * n, 4, SEQ) for n in range(3))
        tm_v = sg_p
        mat_l, mat_t = view(SL + 3 * 2048, 8, P), view(SL + 3 * 2048 + 1024, 8, P)
        mat_tt, mat_lm, mat_w = (view(UM + 4096 + 1024 * n, 8, P) for n in range(3))
        mat_rb, mat_rk, mat_ak = view(U, 8, P), view(U + 1024, 8, P), view(U + 6144, 8, P)
        w_sb, uu_sb = view(SM, 8, 64), view(SM + 512, 8, 64)
        st0, st0m = view(SM + 1024, 4, 64), view(SM + 1280, 4, 64)
        pmid, pend = view(SM + APROJ + 14, 4, 4), view(SM + APROJ + 30, 4, 4)
        assert SM + APROJ + 46 <= cols, (SM, cols)
        R0 = ring_at
        a_s, kk_s, dec_s, g_s, bon_s, tmp_s = (view(R0 + 128 * n, 4, TS) for n in range(6))
        inv = view(SM + 1024, SEQ)
        y_s = view(SM, 4, TS)
        rec = view(R0 + 1024, 5, NS * 64)
        rec_v, rec_y, rec_sa = (view(R0 + 2304 + 128 * n, NS, 32) for n in range(3))
        tok_s = view(R0 + 4096, 6, AW)
        rec_s, rec_t = view(R0 + 4096, 32, 64), view(R0 + 6144, 32, 64)
        y_tok = view(R0 + 2752, AW)

        wa, wb = view(U + 2048, 4, D), view(UM + KT * T + 256, 2, D)
        m_t = view(UM, KT, T)
        y_all = view(SL + 2048, 4, T)
        gate_sb = [view(SL + 2048 + (4 + 2 * n) * T, 2, T) for n in range(3)]
        mg = view(SL + 2048 + 10 * T, T)
        Z = AR
        mem_x = view(Z, 2, D)
        mem_t = view(SL, KT, MEM)
        mkv = view(Z + 4096, 2, 2 * MW)
        mk_t = view(Z + 6144, MH, MEM)
        q_t = view(Z + 7168, MH, T)
        o_t = view(Z + 9344, MH, T)
        ms_sb = [view(Z + c, 256) for c in (11520, 11776, 22100)]
        mp_t = [view(Z + 12032 + 256 * n, 2, P) for n in range(2)]
        mks = [view(Z + 12544 + 1024 * n, 2, MW) for n in range(2)]
        mvs = [view(Z + 14592 + 1024 * n, 2, MW) for n in range(2)]
        mkt_s = [view(Z + 16640 + 1024 * n, 8, P) for n in range(2)]
        mp_own = view(Z + 18944, 2, NB, P)
        mo_own = view(Z + 21000, P)
        mq_own = view(Z + 22400, MH, NB, P)
        xs2 = [view(SL + 5 * 2048 + D * n, D) for n in range(2)]
        rms_junk = view(SL + 4 * 2048, D)
        wg = [view(ring_at, KT, FF), view(Z, KT, FF)]
        wu = [view(ring_at + 4096, KT, FF), view(Z + 4096, KT, FF)]
        wd = [view(Z + 8192, 4, D), view(Z + 12288, 4, D)]
        E0 = Z + 16384
        xs3 = view(E0, 5, D)
        x_e = view(E0, KT, BLK)
        h_sg, h_b, h_t = view(E0 + 1024, FF), view(E0 + 1536, FF), view(E0 + 2048, 4, BLK)
        xb = view(E0 + 5120, D)
        y_b = view(E0 + 6144, D)
        hot = view(E0 + 7168, 5, 2 * NE)
        slot_f = view(E0 + 7488, 10)
        slot_i = view(E0 + 7498, 10).bitcast(U32)
        gate = view(E0 + 7508, 5, 2)
        rbias = view(E0 + 7556, 36)
        lg = view(E0 + 6144, 5, 36)
        r_grp, r_max = view(E0 + 6324, 5, 8), view(E0 + 6364, 5, 8)
        r_idx = view(E0 + 6404, 5, 8).bitcast(U32)
        r_num, r_exp = view(E0 + 6444, 5, 2), view(E0 + 6454, 5, 5)
        r_in, r_off = view(E0 + 6480, 5, NE), view(E0 + 6640, 5, NE)
        r_sum, r_two = view(E0 + 6800, 5), view(E0 + 6805, 5)
        rs = view(E0 + 7592, 200)
        tab_i = view(E0 + 7792, 2 * NE + NTAB + 1).bitcast(I32)
        cnt3 = view(E0 + 7920, NE, MAXBLK - 1)
        row3 = view(E0 + 8080, NTAB, NE)
        yg = [view(Z + D * n, D) for n in range(2 * len(TILES))]
        gfin = view(Z + 10 * D, D)
        assert E0 + 8080 + NTAB * NE <= cols, (E0, cols)
        shift_rows = view(SL + 3 * 2048, APROJ)
        last_s = view(SM, APROJ)
        last_p = view(SM, P)[64:64 + AJ]
        u_last = view(SM + APROJ, AJ)
        fin_s = view(SM + 512, AW)
        OUT_CACHES = sum(2 * (min(w, SEQ) // P) for w, _ in GROUPS) + 2 * NB * NG

        def tab_of(part, e):
            return tab_i[0:1, bass.ds(part + e, 1)]

        srec_d = nc.dram_tensor("scratch_sample_vectors", [6, TS, AW], F32).ap()
        yrec_d = nc.dram_tensor("scratch_sample_y", [TS, AW], F32).ap()
        xs_d = nc.dram_tensor("scratch_rows_by_expert", [ROWS + BLK, D], F32).ap()
        ys_d = nc.dram_tensor("scratch_expert_rows", [ROWS + BLK, D], F32).ap()

        banks = [ctx.enter_context(nc.psum_tensor(f"bank{n}", [P, 512], F32))[:, :] for n in range(8)]
        v_mail = (banks[0:4], sem("v_filled"), sem("v_freed"))
        a_mail = (banks[4:7], sem("a_filled"), sem("a_freed"))
        aux = banks[7]

        N = {n: sem(n) for n in (
            "v_step", "act_step", "pool_step", "con_in", "x_in", "prm_in", "small_in", "ring_used", "ring_spare", "qkv_raw",
            "rope_done", "xt_done", "p_neg", "p_exp", "p_ready", "pv_full", "pv_taken", "yb_done", "kv_used", "q_new_ready",
            "s_soft", "sneg", "sexp", "um_done", "lora_in", "sga", "prep_sq", "prep_e", "exp_done", "prep_done", "stm_done",
            "lm_ready", "mats", "state_ready", "tm_done", "srec_out", "srec_in", "yrec_out", "yrec_in", "ysq", "ya_done",
            "inv_ready", "l_ready", "lt_taken", "lg_in", "lg_clear", "v_many", "q_own_clear", "q_own_ready", "p_own_ready",
            "y_own_ready", "mq_ready", "mp_turned", "mp_ready", "mo_ready", "br_in", "sig_done", "merged", "x1_done",
            "mem_in", "memx", "mkv_done", "mkv_out", "m_neg", "m_exp", "m_ready", "mo_done", "mkv_used", "x2_rows", "x2_done",
            "hot_done", "route_done", "xs3_done", "scattered", "pad_out", "e_area", "xb_in", "xb_used", "h_done", "yb_out",
            "y_ready", "y_final", "out", "copies", "shift_out", "tab_ready", "state_out", "gfin_in", "rb_in", "xe_ready",
            "shift_in", "u_raw", "y_raw", "gate_used", "route_a", "route_e", "silu_done", "x3_done", "y_out", "shift_ready",
            "fin_ready", "g_full", "u_full", "ht_full", "ht_done", "y_taken_a", "y_taken_v", "rms", "sq_ready", "sq_done",
            "seen")}
        ring_in = [sem(f"ring_in{s}") for s in range(2)]
        kv_in = [sem(f"kv_in{s}") for s in range(3)]
        mks_in = [sem(f"mks_in{s}") for s in range(2)]
        mvs_in = [sem(f"mvs_in{s}") for s in range(2)]
        w_in_sem = [sem(f"expert_weights_in{s}") for s in range(2)]
        yg_in = [sem(f"gathered{i}") for i in range(len(TILES))]

        w_in = a["w_in"].rearrange("(p kt) c -> p kt c", kt=KT)
        w_out = a["w_out"].rearrange("(kt p) c -> p kt c", p=P)
        GATE = APROJ + BPROJ
        chunks = []
        for c in range(0, BPROJ, 512):
            w = min(512, BPROJ - c)
            chunks.append([(slice(0, w), w_in[:, :, APROJ + c:APROJ + c + w])])
        NA = len(chunks)
        feats = []
        for c in (3 * AW, AW, 0, 2 * AW):
            w = min(512, APROJ - c)
            chunks.append([(slice(0, w), w_in[:, :, c:c + w])])
            feats.append(list(range(c // P, (c + w) // P)))
        NR = len(chunks)
        for q in range(4):
            chunks.append([(slice(0, 256), w_in[:, :, GATE + 256 * q:GATE + 256 * q + 256]),
                           (slice(256, 512), w_in[:, :, GATE + D + 256 * q:GATE + D + 256 * q + 256])])
        NGT = len(chunks)
        for c in range(2):
            chunks.append([(slice(0, 512), w_out[:, :, 512 * c:512 * c + 512])])
        NO = len(chunks)
        mkv_w = a["w_mem_kv"].rearrange("(p kt) c -> p kt c", kt=KT)
        for c in range(2):
            chunks.append([(slice(0, 512), mkv_w[:, :, 512 * c:512 * c + 512])])
        NM = len(chunks)
        chunks.append([(slice(0, 512), a["w_mem_q"].rearrange("(p kt) c -> p kt c", kt=KT))])
        chunks.append([(None, a["w_mem_out"].rearrange("(h p) d -> p h d", p=P))])
        loaded = []
        tot = [0, 0]
        for n, ch in enumerate(chunks):
            tot[n % 2] += 16 * len(ch)
            loaded.append(tot[n % 2])

        caches = (a["cache_swa_w128"], a["cache_swa_w512"], a["cache_swa_w2048"])
        units = [(g, b) for g in range(NG) for b in range(NB)]
        wide = [1, NS, NS]
        att = [(i, h) for i in range(NPT) for h in range(4)]

        def key_blocks(i):
            return [(0, j) for j in range(max(0, i - 1), i + 1)] + [(g, j) for g in (1, 2) for j in range(i + 1)]

        FIRST, COUNT, ROW, TOTAL = 0, NE, 2 * NE, 2 * NE + NTAB
        g_ps, u_ps, x_ps, h_ps, d_ps = banks[0], banks[1], banks[2:4], banks[4], banks[5:7]
        mem_units = [(i, h) for i in range(NPT) for h in range(MH)]
        block = ctx.enter_context(nc.Block())

        @block.sync
        def _(sp):
            for i, (t0, n) in enumerate(TILES):
                src = a["x_prompt"][0, t0:t0 + n, :] if t0 < SEQ else a["x_sample"].rearrange("b t d -> (b t) d")
                sp.dma_start(x_res[0:n, i, :], src).then_inc(N["x_in"], 16)
            sp.dma_start(con, cst[:, :]).then_inc(N["con_in"], 16)
            for n, g in enumerate(("norm_mix_g", "norm_mem_g", "norm_memkv_g", "norm_ffn_g")):
                sp.dma_start(gains[:, n, :], a[g].rearrange("(p k) -> p k", k=KT)).then_inc(N["prm_in"], 16)
            for name, r in (("rwkv_mu", MU), ("rwkv_w0", W0), ("rwkv_a0", A0), ("rwkv_k_k", KK_), ("rwkv_k_a", KA),
                            ("rwkv_r_k", RK), ("rwkv_lnx_g", LG), ("rwkv_lnx_b", LB), ("b_gate", BG)):
                v = a[name] if name != "rwkv_r_k" else a[name].rearrange("h d -> (h d)")
                k = v.shape[0] // P
                sp.dma_start(row_b[r:r + k, :], v.rearrange("(j p) -> j p", p=P)).then_inc(N["prm_in"], 16)

            def load_chunk(n):
                if n >= 2:
                    sp.wait_ge(N["ring_used"], n - 1)
                if n == NR + 1:
                    sp.wait_ge(N["ring_spare"], 1)
                for cols_, src in chunks[n]:
                    dst = view(ring_at + 4096 * (n % 2), 4, D) if cols_ is None else ring[n % 2][:, :, cols_]
                    sp.dma_start(dst, src).then_inc(ring_in[n % 2], 16)

            for n in range(2):
                load_chunk(n)
            sp.dma_start(lora[0:64, 0, :], a["rwkv_w2"][:, :]).then_inc(N["small_in"], 16)
            sp.dma_start(lora[64:128, 0, :], a["rwkv_a2"][:, :]).then_inc(N["small_in"], 16)
            sp.dma_start(lora[:, 1, :], a["rwkv_g2"][:, :]).then_inc(N["small_in"], 16)
            sp.dma_start(wr[:, :, 0:4], a["w_router_group"].rearrange("(p k) e -> p k e", k=KT)).then_inc(N["small_in"], 16)
            sp.dma_start(wr[:, :, 4:36], a["w_router_expert"].rearrange("(p k) e -> p k e", k=KT)).then_inc(N["small_in"], 16)
            for n in range(2, NA):
                load_chunk(n)
            sp.wait_ge(N["rope_done"], len(TILES))
            sp.wait_ge(N["qkv_raw"], 2)
            for g, (window, _) in enumerate(GROUPS):
                keep = min(window, SEQ)
                dst = o[f"p_cache{g}"]
                for i in range(NPT - keep // P, NPT):
                    r0 = i * P - (SEQ - keep)
                    for kv in range(2):
                        src = qkv[:, i, BW * (1 + kv) + 256 * g:BW * (1 + kv) + 256 * g + 256]
                        sp.dma_start(dst[0, kv, r0:r0 + P].rearrange("t h d -> t (h d)"), src).then_inc(N["out"], 16)
                for b in range(NB):
                    for kv in range(2):
                        src = qkv[b * NS:(b + 1) * NS, 4, BW * (1 + kv) + 256 * g:BW * (1 + kv) + 256 * g + 256]
                        sp.dma_start(o[f"s_cache{g}"][b, kv, window - NS:window].rearrange("t h d -> t (h d)"), src)\
                          .then_inc(N["out"], 16)
            for kv in range(2):
                if kv == 1:
                    sp.wait_ge(N["kv_used"], len(units))
                    for n in range(NA, NA + 2):
                        load_chunk(n)
                for m, (g, b) in enumerate(units):
                    z = kv * len(units) + m
                    if z >= 3:
                        sp.wait_ge(N["kv_used"], z - 2)
                    src = caches[g][b, kv].rearrange("(i r) h d -> i r (h d)", r=GROUPS[g][1])[:, 0:wide[g], :]
                    sp.dma_start(kvb[z % 3][:, 0:wide[g], :], src).then_inc(kv_in[z % 3], 16)
            sp.wait_ge(N["yb_done"], 1)
            sp.dma_start(shift_rows[0:NB, :], a["state_shift"][:, :]).then_inc(N["shift_in"], 16)
            for n in range(NA + 2, NR):
                load_chunk(n)
            sp.wait_ge(N["stm_done"], 1)
            sp.dma_start(srec_d.rearrange("v t c -> t v c"), tok_s[0:TS]).then_inc(N["srec_out"], 16)
            sp.wait_ge(N["srec_out"], 16)
            for hf in range(2):
                for b in range(NB):
                    rows = slice(hf * 64 + b * AH, hf * 64 + (b + 1) * AH)
                    for n in range(5):
                        src = srec_d[n, b * NS:(b + 1) * NS, :].rearrange("t (h k) -> h t k", h=AH)
                        sp.dma_start(rec[rows, n, :].rearrange("p (t k) -> p t k", t=NS), src).then_inc(N["srec_in"], 16)
                    src = srec_d[5, b * NS:(b + 1) * NS, :].rearrange("t (h f k) -> h f t k", h=AH, f=2)[:, hf]
                    sp.dma_start(rec_v[rows], src).then_inc(N["srec_in"], 16)
                src = a["state_rwkv"].rearrange("b h (f v) k -> (b h) f (v k)", f=2)[:, hf]
                sp.dma_start(rec_s[hf * 64:(hf + 1) * 64].rearrange("p v k -> p (v k)"), src).then_inc(N["srec_in"], 16)
            sp.wait_ge(N["state_out"], 32)
            load_chunk(NR)
            sp.wait_ge(N["mats"], NPT)
            sp.dma_start(wa, a["w_branch_a"].rearrange("(j p) d -> p j d", p=P)).then_inc(N["br_in"], 16)
            sp.dma_start(wb, a["w_branch_b"].rearrange("(j p) d -> p j d", p=P)).then_inc(N["br_in"], 16)
            load_chunk(NR + 1)
            sp.wait_ge(N["ya_done"], 1)
            sp.dma_start(mem_x, a["mem_prompt"][0].rearrange("(i p) d -> p i d", p=P)).then_inc(N["mem_in"], 16)
            for n in range(NR + 2, NO):
                load_chunk(n)
            for n in range(NO, len(chunks)):
                load_chunk(n)
            sp.wait_ge(N["x1_done"], 1)
            for b in range(NB):
                if b >= 2:
                    sp.wait_ge(N["mkv_used"], b - 1)
                sp.dma_start(mks[b % 2], a["cache_mem_kv"][b, 0].rearrange("(i p) h d -> p i (h d)", p=P)).then_inc(mks_in[b % 2], 16)
            for b in range(NB):
                if b >= 2:
                    sp.wait_ge(N["mkv_used"], NB + b - 1)
                sp.dma_start(mvs[b % 2], a["cache_mem_kv"][b, 1].rearrange("(i p) h d -> p i (h d)", p=P)).then_inc(mvs_in[b % 2], 16)
            sp.wait_ge(N["e_area"], 1)
            sp.wait_ge(N["mkv_out"], 32)
            eg = a["w_exp_gate"].rearrange("e (p k) f -> e p k f", k=KT)
            eu = a["w_exp_up"].rearrange("e (p k) f -> e p k f", k=KT)
            ed = a["w_exp_down"].rearrange("e (c p) d -> e p c d", p=P)

            def load_expert(e, s, started):
                part = 0
                for w, src, k in ((wg, eg, KT), (wu, eu, KT), (wd, ed, 4)):
                    src = src[e] if isinstance(e, int) else src[bass.ds(e, 1)][0]
                    for h in range(2):
                        q = part % 2
                        if started or part >= 2:
                            sp.wait_ge(w_in_sem[q], 48 * e + 16 * (part // 2))
                        if not isinstance(e, int):
                            sp.sem_inc(N["seen"], 1)
                        ks = slice(h * k // 2, (h + 1) * k // 2)
                        sp.dma_start(w[s][:, ks, :], src[:, ks, :]).then_inc(w_in_sem[q], 16)
                        part += 1

            for s in range(2):
                load_expert(s, s, s > 0)
            sp.wait_ge(N["tab_ready"], 1)
            with sp.Fori(1, NE // 2) as j:
                for s in range(2):
                    begun = sp.value_load(tab_of(FIRST, 2 * j + s - 1), min_val=1, max_val=ALLBLK)
                    sp.wait_ge(N["y_ready"], 2 * begun)
                    sp.sem_inc(N["seen"], 1)
                    load_expert(2 * j + s, s, True)
            sp.wait_ge(N["out"], 16 * OUT_CACHES)
            for i, (t0, n) in enumerate(TILES):
                sp.wait_ge(N["y_final"], i + 1)
                dst = o["y_prompt"][0, t0:t0 + n, :] if t0 < SEQ else o["y_sample"].rearrange("b t d -> (b t) d")
                sp.dma_start(dst, x_res[0:n, i, :]).then_inc(N["y_out"], 16)
            sp.wait_ge(N["y_out"], 16 * len(TILES))

        @block.tensor
        def _(pe):
            vm, am = Mail(*v_mail), Mail(*a_mail)
            mm = pe.matmul

            def turn_rows(src, n):
                for half in range(2):
                    bank = vm.claim(pe)
                    for q in range(4):
                        last = pe.transpose(bank[:, q * P:q * P + n], src[0:n, 4 * half + q:D:KT], ident[0:n, 0:n])
                    last.then_inc(vm.filled, 1)

            def chunk_ready(n):
                pe.wait_ge(ring_in[n % 2], loaded[n])

            def chunk_used(mail):
                pe.wait_ge(mail.filled, mail.put)
                pe.sem_inc(N["ring_used"], 1)

            pe.wait_ge(N["con_in"], 16)
            pe.wait_ge(N["prm_in"], 16 * 13)
            bank = vm.claim(pe)
            pe.transpose(bank[:, 0:NPRM], row_b[0:NPRM, :], ident[0:NPRM, 0:NPRM]).then_inc(vm.filled, 1)
            for i, (t0, n) in enumerate(TILES):
                pe.wait_ge(N["xs3_done"], i + 1)
                turn_rows(xs_tmp[i % 2], n)

            def turn_qk(i, m):
                pe.wait_ge(N["rope_done"], i + 1)
                for half in range(3):
                    bank = vm.claim(pe)
                    for q in range(4):
                        j = 4 * half + q
                        last = pe.transpose(bank[:, q * P:q * P + m], qkv[0:m, i, j * P:(j + 1) * P], ident[0:m, 0:m])
                    last.then_inc(vm.filled, 1)

            pe.wait_ge(N["xt_done"], len(TILES))
            for n in range(NA):
                chunk_ready(n)
                w = chunks[n][0][0].stop
                for i, (t0, m) in enumerate(TILES):
                    if n == NA - 1:
                        turn_qk(i, m)
                    bank = am.claim(pe)
                    for kt in range(KT):
                        last = mm(bank[0:m, 0:w], x_t[:, kt, t0:t0 + m], ring[n % 2][:, kt, 0:w], start=kt == 0, stop=kt == KT - 1)
                    last.then_inc(am.filled, 1)
                chunk_used(am)
            pe.wait_ge(vm.freed, vm.put)
            pe.wait_ge(N["qkv_raw"], 2)

            def scores(u):
                i, h = att[u]
                lo = 64 * (h % 2)
                for g in range(NG):
                    js = [j for gg, j in key_blocks(i) if gg == g]
                    bank = vm.claim(pe)
                    mm(bank[:, 0:P * len(js)], qk_t[lo:lo + 64, 2 * g + h // 2, i * P:(i + 1) * P],
                       qk_t[lo:lo + 64, 6 + 2 * g + h // 2, js[0] * P:(js[-1] + 1) * P], start=True, stop=True).then_inc(vm.filled, 1)

            def turn_weights(u):
                kb = key_blocks(att[u][0])
                pe.wait_ge(N["p_ready"], u + 1)
                for c in range(0, len(kb), 4):
                    bank = am.claim(pe)
                    for q in range(c, min(c + 4, len(kb))):
                        last = pe.transpose(bank[:, (q - c) * P:(q - c + 1) * P], s_sb[u % 3][:, q * P:(q + 1) * P], ident)
                    last.then_inc(am.filled, 1)

            def weigh(u):
                i, h = att[u]
                kb = key_blocks(i)
                pe.wait_ge(am.freed, am.put)
                if u >= 1:
                    pe.wait_ge(N["pv_taken"], u)
                lo = 64 * (h % 2)
                for q, (g, j) in enumerate(kb):
                    c = 2 * BW + 256 * g + 64 * h
                    last = mm(aux[lo:lo + 64, 0:P], qkv[:, j, c:c + 64], p_t[u % 2][:, q, :], start=q == 0, stop=q == len(kb) - 1)
                last.then_inc(N["pv_full"], 1)

            scores(0)
            scores(1)
            for u in range(len(att)):
                turn_weights(u)
                if u + 2 < len(att):
                    scores(u + 2)
                weigh(u)
            pe.wait_ge(N["q_new_ready"], 1)
            pe.wait_ge(N["pv_taken"], len(att))

            def turn_keys(m):
                g, b = units[m]
                pe.wait_ge(kv_in[m % 3], 16 * (m // 3 + 1))
                for c in range(0, 2 * wide[g], 4):
                    bank = am.claim(pe)
                    for q in range(c, min(c + 4, 2 * wide[g])):
                        last = pe.transpose(bank[:, (q - c) * P:(q - c + 1) * P], kvb[m % 3][:, q // 2, (q % 2) * P:(q % 2 + 1) * P], ident)
                    last.then_inc(am.filled, 1)
                return am.put

            bank = vm.claim(pe)
            for g in range(NG):
                for hp in range(2):
                    last = mm(bank[:, g * TS:(g + 1) * TS], q_new[:, 2 * g + hp, :], qk_t[:, 6 + 2 * g + hp, SEQ:T],
                              start=hp == 0, stop=hp == 1)
            last.then_inc(vm.filled, 1)

            def cached_scores(m, got, bank):
                g, b = units[m]
                pe.wait_ge(am.freed, got)
                pe.wait_ge(N["q_own_ready"], g + 1)
                w = wide[g]
                for hp in range(2):
                    last = mm(bank[:, 0:w * P].rearrange("p (t k) -> p t k", k=P), q_own[:, 2 * g + hp, b, :],
                              kt_s[m % 2][:, hp:2 * w:2, :], start=b == 0 and hp == 0, stop=b == NB - 1 and hp == 1)
                last.then_inc(N["kv_used"], 1)

            got = turn_keys(0)
            for m in range(len(units)):
                if units[m][1] == 0:
                    bank = vm.claim(pe)
                nxt = turn_keys(m + 1) if m + 1 < len(units) else None
                cached_scores(m, got, bank)
                if units[m][1] == NB - 1:
                    pe.wait_ge(N["kv_used"], m + 1)
                    pe.sem_inc(vm.filled, 1)
                got = nxt
            pe.wait_ge(N["s_soft"], 1)
            bank = vm.claim(pe)
            for g in range(NG):
                last = pe.transpose(bank[:, g * P:(g + 1) * P], ps_sb[:, g * P:(g + 1) * P], ident)
            last.then_inc(vm.filled, 1)
            bank = vm.claim(pe)
            for g in range(NG):
                last = pe.transpose(bank[0:TS, g * P:(g + 1) * P], ps_sb[:, NG * P + g * TS:NG * P + (g + 1) * TS], ident)
            last.then_inc(vm.filled, 1)
            pe.wait_ge(vm.freed, vm.put)
            for g in range(NG):
                c = 2 * BW + 256 * g
                mm(aux[:, 0:256], ptn[0:TS, g, :], qkv[0:TS, 4, c:c + 256], start=g == 0, stop=False)
            for m, (g, b) in enumerate(units):
                z = len(units) + m
                pe.wait_ge(kv_in[z % 3], 16 * (z // 3 + 1))
                pe.wait_ge(N["p_own_ready"], g + 1)
                for t in range(wide[g]):
                    pr = p_own0[:, b, :] if wide[g] == 1 else p_own[:, b * NS + t, :]
                    last = mm(aux[:, 0:256], pr, kvb[z % 3][:, t, :], start=False, stop=m == len(units) - 1 and t == wide[g] - 1)
                last.then_inc(N["kv_used"], 1)
            pe.wait_ge(N["y_own_ready"], 1)
            bank = vm.claim(pe)
            for lo in (0, 64):
                last = mm(bank[lo:lo + 64, 0:P], y_own, ident, start=True, stop=True)
            last.then_inc(vm.filled, 1)
            pe.wait_ge(N["shift_in"], 16)
            for c in range(0, AJ, 4):
                bank = vm.claim(pe)
                for j in range(c, min(c + 4, AJ)):
                    last = pe.transpose(bank[:, (j - c) * NB:(j - c + 1) * NB], shift_rows[0:NB, j * P:(j + 1) * P], ident[0:NB, 0:NB])
                last.then_inc(vm.filled, 1)

            def project(c, between=None):
                chunk_ready(c)
                for q in range(len(feats[c - NA])):
                    for t0, n in HALVES:
                        bank = am.claim(pe)
                        for kt in range(KT):
                            last = mm(bank[:, 0:n], ring[c % 2][:, kt, q * P:(q + 1) * P], x_t[:, kt, t0:t0 + n], start=kt == 0, stop=kt == KT - 1)
                        last.then_inc(am.filled, 1)
                    if between and q == 0:
                        between()
                chunk_used(am)

            def loras(um, n):
                for j in range(4):
                    for lhs, rhs in ((lora[0:64, 0], um[0:64, 12]), (lora[64:128, 0], um[64:128, 12]), (lora[:, 1], um[:, 13])):
                        bank = am.claim(pe)
                        mm(bank[:, 0:n], lhs[:, j * P:(j + 1) * P], rhs, start=True, stop=True).then_inc(am.filled, 1)

            def head_sums(sq, n):
                for j in range(4):
                    bank = vm.claim(pe)
                    mm(bank[:, 0:n], C("blk"), sq[:, j, 0:n], start=True, stop=True).then_inc(vm.filled, 1)

            def head_roots(sq, n):
                bank = vm.claim(pe)
                for j in range(4):
                    last = mm(bank[32 * j:32 * j + 32, 0:n], C("blk")[:, 48:80], sq[:, j, 0:n], start=True, stop=True)
                last.then_inc(vm.filled, 1)

            def spread(n, count):
                pe.wait_ge(N["inv_ready"], count)
                for j in range(4):
                    bank = vm.claim(pe)
                    mm(bank[:, 0:n], C("spread")[32 * j:32 * j + 32, :], inv[32 * j:32 * j + 32, 0:n], start=True, stop=True)\
                        .then_inc(vm.filled, 1)

            def token_rows(src):
                for i in range(NPT):
                    bank = vm.claim(pe)
                    for j in range(4):
                        last = pe.transpose(bank[:, j * P:(j + 1) * P], src[:, j, i * P:(i + 1) * P], ident)
                    last.then_inc(vm.filled, 1)

            project(NA)
            project(NA + 1)
            pe.wait_ge(N["small_in"], 16 * 5)
            pe.wait_ge(N["lora_in"], 1)
            loras(um_p, SEQ)
            project(NA + 2)
            pe.wait_ge(N["prep_sq"], 1)
            head_roots(sq_p, SEQ)
            project(NA + 3, lambda: spread(SEQ, 1))
            pe.wait_ge(N["prep_sq"], 2)
            head_sums(sq_p, SEQ)
            pe.wait_ge(N["lora_in"], 2)
            loras(um_s, TS)
            pe.wait_ge(N["prep_done"], 1)
            token_rows(a_p)
            pe.wait_ge(N["prep_sq"], 3)
            head_roots(tmp_s, TS)
            spread(TS, 2)
            token_rows(um_p[:, 4:8])
            pe.wait_ge(N["prep_sq"], 4)
            head_sums(tmp_s, TS)
            token_rows(um_p[:, 8:12])
            for c in range(0, AJ, 4):
                bank = vm.claim(pe)
                for j in range(c, min(c + 4, AJ)):
                    last = pe.transpose(bank[0:NB, (j - c) * P:(j - c + 1) * P], u_s[:, j, NS - 1:TS:NS], ident)
                last.then_inc(vm.filled, 1)
            bank = vm.claim(pe)
            mm(bank[64:64 + AJ, 0:P], u_last, ident, start=True, stop=True).then_inc(vm.filled, 1)
            pe.wait_ge(N["tm_done"], 1)
            for src in (um_s[:, 0:4], um_s[:, 4:8], kk_s, a_s, dec_s, um_s[:, 8:12]):
                bank = vm.claim(pe)
                for j in range(4):
                    last = pe.transpose(bank[0:TS, j * P:(j + 1) * P], src[:, j, :], ident)
                last.then_inc(vm.filled, 1)
            pe.wait_ge(vm.freed, vm.put)

            def heads(par):
                return [(j, 2 * j + par) for j in range(4)]

            r_p, k_p = um_p[:, 0:4], um_p[:, 4:8]
            for i in range(NPT):
                tk = slice(i * P, (i + 1) * P)
                if i >= 1:
                    pe.wait_ge(N["state_ready"], i)
                for n, (lhs, rhs) in enumerate(((a_p, kk_p), (kk_p, a_p), (k_p, kk_p), (a_p, r_p), (k_p, r_p))):
                    mail = vm if n else am
                    two = [mail.claim(pe), mail.claim(pe)]
                    for par in range(2):
                        lo = 64 * par
                        for j, h in heads(par):
                            last = mm(two[par][:, j * P:(j + 1) * P], lhs[lo:lo + 64, j, tk], rhs[lo:lo + 64, j, tk], start=True, stop=True)
                        last.then_inc(mail.filled, 1)
                for lv, m in enumerate(LEVELS[1:]):
                    final = m == LEVELS[-1]
                    pe.wait_ge(N["lm_ready"], 6 * i + lv + 1)
                    updated = vm.put
                    for par in range(2):
                        pe.wait_ge(vm.freed, updated - (2 if par == 0 and lv else 0))
                        bank = am.claim(pe)
                        for j in range(4):
                            last = mm(bank[:, j * P:(j + 1) * P], mat_lm[:, 4 * par + j, :], mat_t[:, 4 * par + j, :], start=True, stop=True)
                        last.then_inc(am.filled, 1)
                    for par in range(2):
                        pe.wait_ge(am.freed, am.put - 1 + par)
                        for tt in ((0, 1) if not final else (1,)):
                            bank = vm.claim(pe)
                            for j in range(4):
                                z = 4 * par + j
                                lhs, rhs = (mat_w, mat_tt) if tt else (mat_tt, mat_w)
                                last = mm(bank[:, j * P:(j + 1) * P], lhs[:, z, :], rhs[:, z, :], start=True, stop=True)
                            last.then_inc(vm.filled, 1)
                pe.wait_ge(vm.freed, vm.put)
                two = [vm.claim(pe), vm.claim(pe)]
                for par in range(2):
                    lo = 64 * par
                    for j, h in heads(par):
                        dst = two[par][:, j * 64:j * 64 + 64]
                        mm(dst, kk_p[lo:lo + 64, j, tk], st0m[lo:lo + 64, j, :], start=True, stop=False)
                        last = mm(dst, mat_ak[:, 4 * par + j, :], tm_v[:, i, h * 64:h * 64 + 64], start=False, stop=True)
                    last.then_inc(vm.filled, 1)
                pe.wait_ge(vm.freed, vm.put)
                bank = vm.claim(pe)
                for z in range(8):
                    last = mm(bank[:, z * 64:z * 64 + 64], mat_tt[:, z, :], w_sb[:, z, :], start=True, stop=True)
                last.then_inc(vm.filled, 1)
                pe.wait_ge(vm.freed, vm.put)
                bank = vm.claim(pe)
                for par in range(2):
                    lo = 64 * par
                    for j, h in heads(par):
                        dst = bank[lo:lo + 64, j * 64:j * 64 + 64]
                        mm(dst, tm_b[:, i, h * 64:h * 64 + 64], uu_sb[:, 4 * par + j, :], start=True, stop=False)
                        last = mm(dst, tm_k[:, i, h * 64:h * 64 + 64], tm_v[:, i, h * 64:h * 64 + 64], start=False, stop=True)
                last.then_inc(vm.filled, 1)
                two = [am.claim(pe), am.claim(pe)]
                for par in range(2):
                    lo = 64 * par
                    for j, h in heads(par):
                        dst = two[par][lo:lo + 64, j * P:(j + 1) * P]
                        z = 4 * par + j
                        mm(dst, st0m[lo:lo + 64, j, :], r_p[lo:lo + 64, j, tk], start=True, stop=False)
                        mm(dst, uu_sb[:, z, :], mat_rb[:, z, :], start=False, stop=False)
                        last = mm(dst, tm_v[:, i, h * 64:h * 64 + 64], mat_rk[:, z, :], start=False, stop=True)
                    last.then_inc(am.filled, 1)
                pe.wait_ge(am.filled, am.put)
                pe.sem_inc(N["mats"], 1)
            pe.wait_ge(N["state_ready"], NPT)
            bank = vm.claim(pe)
            for j in range(4):
                last = pe.transpose(bank[0:64, j * P:(j + 1) * P], st0[:, j, :], ident)
            last.then_inc(vm.filled, 1)
            pe.wait_ge(N["yrec_in"], 16)
            bank = vm.claim(pe)
            for j in range(4):
                last = pe.transpose(bank[:, j * TS:(j + 1) * TS], y_tok[0:TS, j * P:(j + 1) * P], ident[0:TS, 0:TS])
            last.then_inc(vm.filled, 1)

            def gates(j, half):
                c = NR + j // 2
                t0, n = HALVES[half]
                if j % 2 == 0 and half == 0:
                    chunk_ready(c)
                for off in (0, 256):
                    bank = am.claim(pe)
                    for kt in range(KT):
                        last = mm(bank[:, 0:n], ring[c % 2][:, kt, off + j % 2 * P:off + (j % 2 + 1) * P], x_t[:, kt, t0:t0 + n],
                                  start=kt == 0, stop=kt == KT - 1)
                    last.then_inc(am.filled, 1)
                if j % 2 == 1 and half == 1:
                    chunk_used(am)

            for part in range(2):
                n = TS if part == 0 else SEQ
                y = y_s if part == 0 else a_p
                sq = tmp_s if part == 0 else tmp_p
                pe.wait_ge(N["ysq"], 2 * part + 1)
                head_sums(y, n)
                gates(part, 0)
                pe.wait_ge(N["ysq"], 2 * part + 2)
                head_roots(sq, n)
                if part == 0:
                    spread(n, 3)
                    gates(0, 1)
                else:
                    gates(1, 1)
                    spread(n, 4)
            for j in range(KT):
                for half, (t0, n) in enumerate(HALVES):
                    if j + 2 < KT:
                        gates(j + 2, half)
                    if j == 0 and half == 0:
                        pe.wait_ge(N["ya_done"], 1)
                        pe.wait_ge(N["br_in"], 32)
                    for w, y, nk in ((wa, y_all, 4), (wb, yb_t, 2)):
                        bank = vm.claim(pe)
                        for q in range(nk):
                            last = mm(bank[:, 0:n], w[:, q, j * P:(j + 1) * P], y[:, q, t0:t0 + n], start=q == 0, stop=q == nk - 1)
                        last.then_inc(vm.filled, 1)
            for i in range(2):
                pe.wait_ge(N["memx"], i + 1)
                turn_rows(xs2[i % 2], P)
            pe.wait_ge(N["merged"], 1)

            def out_rows(n, own, weight, nk, lhs):
                for c in range(2):
                    if own:
                        chunk_ready(n + c)
                    for t0, m in TILES:
                        bank = vm.claim(pe)
                        for k in range(nk):
                            last = mm(bank[0:m, :], lhs[:, k, t0:t0 + m], weight(c, k), start=k == 0, stop=k == nk - 1)
                        last.then_inc(vm.filled, 1)
                    if own:
                        chunk_used(vm)

            out_rows(NGT, True, lambda c, k: ring[(NGT + c) % 2][:, k, :], KT, m_t)
            for c in range(2):
                chunk_ready(NO + c)
                for i in range(2):
                    bank = vm.claim(pe)
                    for kt in range(KT):
                        last = mm(bank, mem_t[:, kt, i * P:(i + 1) * P], ring[(NO + c) % 2][:, kt, :], start=kt == 0, stop=kt == KT - 1)
                    last.then_inc(vm.filled, 1)
                chunk_used(vm)
            pe.wait_ge(vm.freed, vm.put)
            for i in range(2):
                bank = vm.claim(pe)
                for h in range(MH):
                    last = pe.transpose(bank[:, h * P:(h + 1) * P], mkv[:, i, h * P:(h + 1) * P], ident)
                last.then_inc(vm.filled, 1)
            for i, (t0, n) in enumerate(TILES):
                pe.wait_ge(N["memx"], 2 + i + 1)
                turn_rows(xs2[i % 2], n)
            pe.wait_ge(vm.freed, vm.put)
            chunk_ready(NM)
            for h in range(MH):
                for t0, n in HALVES:
                    bank = vm.claim(pe)
                    for kt in range(KT):
                        last = mm(bank[:, 0:n], ring[NM % 2][:, kt, h * P:(h + 1) * P], x_t[:, kt, t0:t0 + n], start=kt == 0, stop=kt == KT - 1)
                    last.then_inc(vm.filled, 1)
            chunk_used(vm)
            pe.wait_ge(vm.freed, vm.put)

            def mem_scores(u):
                i, h = mem_units[u]
                bank = vm.claim(pe)
                mm(bank[:, 0:MEM], q_t[:, h, i * P:(i + 1) * P], mk_t[:, h, :], start=True, stop=True).then_inc(vm.filled, 1)

            def mem_turn(u):
                pe.wait_ge(N["m_ready"], u + 1)
                bank = am.claim(pe)
                for c in range(2):
                    last = pe.transpose(bank[:, c * P:(c + 1) * P], ms_sb[u % 3][:, c * P:(c + 1) * P], ident)
                last.then_inc(am.filled, 1)

            def mem_weigh(u):
                i, h = mem_units[u]
                pe.wait_ge(am.freed, am.put)
                bank = am.claim(pe)
                for c in range(2):
                    last = mm(bank[:, 0:P], mkv[:, c, MW + h * P:MW + (h + 1) * P], mp_t[u % 2][:, c, :], start=c == 0, stop=c == 1)
                last.then_inc(am.filled, 1)

            mem_scores(0)
            mem_scores(1)
            for u in range(len(mem_units)):
                mem_turn(u)
                if u + 2 < len(mem_units):
                    mem_scores(u + 2)
                mem_weigh(u)
            def turn_mem(b):
                pe.wait_ge(mks_in[b % 2], 16 * (b // 2 + 1))
                for c in range(2):
                    bank = am.claim(pe)
                    for h in range(MH):
                        last = pe.transpose(bank[:, h * P:(h + 1) * P], mks[b % 2][:, c, h * P:(h + 1) * P], ident)
                    last.then_inc(am.filled, 1)
                return am.put

            got = turn_mem(0)
            pe.wait_ge(N["mq_ready"], 1)
            bank = vm.claim(pe)
            for b in range(NB):
                nxt = turn_mem(b + 1) if b + 1 < NB else None
                pe.wait_ge(am.freed, got)
                pe.sem_inc(N["mkv_used"], 1)
                for h in range(MH):
                    last = mm(bank[:, 0:MEM].rearrange("p (c k) -> p c k", k=P), mq_own[:, h, b, :], mkt_s[b % 2][:, h:2 * MH:MH, :],
                              start=b == 0 and h == 0, stop=b == NB - 1 and h == MH - 1)
                got = nxt
            last.then_inc(vm.filled, 1)
            pe.wait_ge(N["m_ready"], len(mem_units) + 1)
            bank = am.claim(pe)
            for c in range(2):
                last = pe.transpose(bank[:, c * P:(c + 1) * P], ms_sb[len(mem_units) % 3][:, c * P:(c + 1) * P], ident)
            last.then_inc(am.filled, 1)
            pe.wait_ge(N["mp_ready"], 1)
            for b in range(NB):
                pe.wait_ge(mvs_in[b % 2], 16 * (b // 2 + 1))
                for c in range(2):
                    last = mm(aux[:, 0:MW], mp_own[:, c, b, :], mvs[b % 2][:, c, :], start=b == 0 and c == 0, stop=b == NB - 1 and c == 1)
                last.then_inc(N["mkv_used"], 1)
            pe.wait_ge(N["mo_ready"], 1)
            bank = vm.claim(pe)
            pe.transpose(bank[:, 0:P], mo_own, ident).then_inc(vm.filled, 1)
            pe.wait_ge(N["mo_done"], 1)
            pe.wait_ge(am.freed, am.put)
            chunk_ready(NM + 1)
            wmo = view(ring_at + 4096 * ((NM + 1) % 2), 4, D)
            out_rows(NM + 1, False, lambda c, k: wmo[:, k, c * 512:(c + 1) * 512], MH, o_t)
            chunk_used(vm)
            pe.wait_ge(N["x2_done"], 1)
            pe.sem_inc(N["e_area"], 1)
            turned = 0
            for i in range(len(TILES) + 1):
                if i < len(TILES):
                    pe.wait_ge(N["xs3_done"], len(TILES) + i + 1)
                    turn_rows(xs3[:, i, :], TILES[i][1])
                if i >= 1:
                    t0, n = TILES[i - 1]
                    pe.wait_ge(vm.freed, turned)
                    bank = am.claim(pe)
                    for kt in range(KT):
                        last = mm(bank[0:n, 0:36], x_t[:, kt, t0:t0 + n], wr[:, kt, :], start=kt == 0, stop=kt == KT - 1)
                    last.then_inc(am.filled, 1)
                turned = vm.put
            pe.wait_ge(N["hot_done"], 1)
            bank = vm.claim(pe)
            for j, (t0, m) in enumerate(TILES):
                last = mm(bank[:, 0:2 * NE], C("ones")[0:m, :], hot[0:m, j, :], start=j == 0, stop=j == len(TILES) - 1)
            last.then_inc(vm.filled, 1)
            for i, (t0, n) in enumerate(TILES):
                bank = vm.claim(pe)
                for j in range(i + 1):
                    m = TILES[j][1]
                    lhs = C("ones")[0:m, 0:n] if j < i else C("strict")[0:m, 0:n]
                    last = mm(bank[0:n, 0:2 * NE], lhs, hot[0:m, j, :], start=j == 0, stop=j == i)
                last.then_inc(vm.filled, 1)
            pe.wait_ge(N["tab_ready"], 1)
            def turn_block():
                for kt in range(KT):
                    last = pe.transpose(x_ps[kt // 4][:, kt % 4 * BLK:(kt % 4 + 1) * BLK], xb[:, kt:D:KT], ident)
                last.then_inc(N["xb_used"], 1)

            pe.wait_ge(N["xb_in"], 16)
            turn_block()
            with pe.Fori(0, NE // 2) as jj:
                table = [(pe.value_load(tab_of(FIRST, 2 * jj + s), min_val=0, max_val=ALLBLK),
                          pe.value_load(tab_of(COUNT, 2 * jj + s), min_val=1, max_val=MAXBLK)) for s in range(2)]
                for s in range(2):
                    first, blocks = table[s]
                    for q in range(2):
                        pe.wait_ge(w_in_sem[q], 48 * (2 * jj + s + 1))
                    pe.sem_inc(N["seen"], 1)
                    with pe.Fori(0, blocks) as m:
                        n = pe.snap(first + m)
                        pe.wait_ge(N["xe_ready"], n + 1)
                        for dst, w, full in ((g_ps, wg[s], N["g_full"]), (u_ps, wu[s], N["u_full"])):
                            for kt in range(KT):
                                last = mm(dst, x_e[:, kt, :], w[:, kt, :], start=kt == 0, stop=kt == KT - 1)
                            last.then_inc(full, 1)
                        pe.wait_ge(N["xb_in"], 16 * n + 32)
                        pe.sem_inc(N["seen"], 1)
                        turn_block()
                        pe.wait_ge(N["h_done"], n + 1)
                        pe.sem_inc(N["seen"], 1)
                        for k in range(4):
                            last = pe.transpose(h_ps[:, k * BLK:(k + 1) * BLK], h_b[:, k * P:(k + 1) * P], ident)
                        last.then_inc(N["ht_full"], 1)
                        pe.wait_ge(N["ht_done"], n + 1)
                        for c in range(2):
                            for k in range(4):
                                last = mm(d_ps[c], h_t[:, k, :], wd[s][:, k, c * 512:(c + 1) * 512], start=k == 0, stop=k == 3)
                            last.then_inc(N["y_ready"], 1)

        @block.scalar
        def _(act):
            line = Line(act, N["act_step"])
            am = Mail(*a_mail)

            def f(out, in_, func, sem=None, **kw):
                line.do(nc.scalar.activation(out, in_, func, **kw), sem)

            def rms(rows, junk, first=0, rows_done=None):
                for col, (src, n) in enumerate(rows, first):
                    if rows_done:
                        act.wait_ge(rows_done, col - first + 1)
                    f(junk[0:n], src, ACT.Square, accum_out=stat[0:n, col:col + 1])
                act.wait_ge(N["con_in"], 16)
                full = first + sum(n == P for _, n in rows)
                if full > first:
                    f(stat[:, first:full], stat[:, first:full], ACT.Sqrt, scale=1.0 / D, bias=C("eps"))
                if full < first + len(rows):
                    n = rows[-1][1]
                    f(stat[0:n, full:full + 1], stat[0:n, full:full + 1], ACT.Sqrt, scale=1.0 / D, bias=C("eps")[0:n])
                act.sem_inc(N["rms"], 1)

            stream = [(x_res[0:n, i, :], n) for i, (t0, n) in enumerate(TILES)]

            act.wait_ge(N["x_in"], 16 * len(TILES))
            rms(stream, view(s0 + 2560, D))
            for c in range(NA):
                w = chunks[c][0][0].stop
                for i, (t0, n) in enumerate(TILES):
                    bank = am.take(act)
                    f(qkv[0:n, i, 512 * c:512 * c + w], bank[0:n, 0:w], ACT.Copy, am.freed)
                if c == 2 * BW // 512 - 1 or c == NA - 1:
                    act.sem_inc(N["qkv_raw"], 1)

            def exp_unit(u):
                i, h = att[u]
                n = P * len(key_blocks(i))
                c = 8 + 4 * (u % 3)
                act.wait_ge(N["p_neg"], u + 1)
                f(s_sb[u % 3][:, 0:n], s_sb[u % 3][:, 0:n], ACT.Exp, N["p_exp"], bias=stat[:, c + 1:c + 2], scale=0.125,
                  accum_out=stat[:, c + 2:c + 3])

            def take_unit(u):
                i, h = att[u]
                kb = key_blocks(i)
                for c in range(0, len(kb), 4):
                    k = min(4, len(kb) - c)
                    bank = am.take(act)
                    f(p_t[u % 2][:, c:c + k, :], bank[:, 0:k * P].rearrange("p (a b) -> p a b", b=P), ACT.Copy, am.freed)
                act.wait_ge(N["pv_full"], u + 1)
                lo = 64 * (h % 2)
                f(yb_t[lo:lo + 64, h // 2, i * P:(i + 1) * P], aux[lo:lo + 64, 0:P], ACT.Copy, N["pv_taken"])

            exp_unit(0)
            exp_unit(1)
            for u in range(len(att)):
                take_unit(u)
                if u + 2 < len(att):
                    exp_unit(u + 2)
            for m, (g, b) in enumerate(units):
                for c in range(0, 2 * wide[g], 4):
                    k = min(4, 2 * wide[g] - c)
                    bank = am.take(act)
                    f(kt_s[m % 2][:, c:c + k, :], bank[:, 0:k * P].rearrange("p (a b) -> p a b", b=P), ACT.Copy, am.freed)
            act.wait_ge(N["sneg"], 1)
            f(ps_sb, ps_sb, ACT.Exp, N["sexp"], bias=stat[:, 17:18], scale=0.125, accum_out=stat[:, 18:19])
            act.wait_ge(N["yb_done"], 1)
            act.wait_ge(N["out"], 16 * OUT_CACHES)
            def take_feature(j):
                half = HALVES[1][0]
                f(u_p[:, j, 0:half], am.take(act)[:, 0:half], ACT.Copy, am.freed)
                bank = am.take(act)
                f(u_p[:, j, half:SEQ], bank[:, 0:SEQ - half], ACT.Copy)
                f(u_s[:, j, :], bank[:, SEQ - half:half], ACT.Copy, am.freed)
                act.sem_inc(N["u_raw"], 1)

            def squash(um, part):
                act.wait_ge(N["um_done"], part + 1)
                f(um[0:64, 12, :], um[0:64, 12, :], ACT.Tanh)
                f(um[:, 13, :], um[:, 13, :], ACT.Sigmoid, N["lora_in"])

            def take_loras(sg, aa, gg, n):
                for j in range(4):
                    f(sg[:, j, 0:n], am.take(act)[:, 0:n], ACT.Sigmoid, am.freed, bias=prm[:, W0 + j:W0 + j + 1])
                    f(aa[:, j, 0:n], am.take(act)[:, 0:n], ACT.Sigmoid, am.freed, bias=prm[:, A0 + j:A0 + j + 1])
                    f(gg[:, j, 0:n], am.take(act)[:, 0:n], ACT.Copy, am.freed)
                act.sem_inc(N["sga"], 1)

            for j in feats[0] + feats[1][0:1]:
                take_feature(j)
            squash(um_p, 0)
            for j in feats[1][1:]:
                take_feature(j)
            take_loras(sg_p, a_p, g_p, SEQ)
            for j in feats[2] + feats[3][0:1]:
                take_feature(j)
            act.wait_ge(N["sq_ready"], 1)
            f(inv, inv, ACT.Sqrt, N["sq_done"])
            act.wait_ge(N["prep_e"], 1)
            f(sg_p, sg_p, ACT.Exp)
            f(tmp_p, c_p, ACT.Exp)
            f(c_p, c_p, ACT.Exp, scale=-1.0)
            f(pmid, pmid, ACT.Exp)
            act.sem_inc(N["exp_done"], 1)
            for j in feats[3][1:]:
                take_feature(j)
            squash(um_s, 1)
            take_loras(dec_s, a_s, g_s, TS)
            act.wait_ge(N["sq_ready"], 2)
            f(inv[:, 0:TS], inv[:, 0:TS], ACT.Sqrt, N["sq_done"])
            f(dec_s, dec_s, ACT.Exp, scale=-float(np.exp(np.float32(-0.5))))
            act.sem_inc(N["exp_done"], 1)
            for i in range(NPT):
                for par in range(2):
                    f(mat_l[:, 4 * par:4 * par + 4, :], am.take(act).rearrange("p (a b) -> p a b", b=P), ACT.Copy, am.freed)
                act.sem_inc(N["l_ready"], 1)
                for _ in LEVELS[1:]:
                    for par in range(2):
                        f(mat_w[:, 4 * par:4 * par + 4, :], am.take(act).rearrange("p (a b) -> p a b", b=P), ACT.Copy, am.freed)
                    act.sem_inc(N["lt_taken"], 1)
                for par in range(2):
                    lo = 64 * par
                    bank = am.take(act)
                    f(a_p[lo:lo + 64, :, i * P:(i + 1) * P], bank[lo:lo + 64, :].rearrange("p (a b) -> p a b", b=P), ACT.Copy, am.freed)
            act.sem_inc(N["y_raw"], 1)

            def gates(j, half):
                t0, n = HALVES[half]
                if j >= 3:
                    act.wait_ge(N["gate_used"], 2 * (j - 3) + half + 1)
                for k in range(2):
                    b = BG + 8 * k + j
                    f(gate_sb[j % 3][:, k, t0:t0 + n], am.take(act)[:, 0:n], ACT.Sigmoid, am.freed, bias=prm[:, b:b + 1])
                act.sem_inc(N["sig_done"], 1)

            gates(0, 0)
            act.wait_ge(N["sq_ready"], 3)
            f(inv[:, 0:TS], inv[:, 0:TS], ACT.Sqrt, N["sq_done"])
            gates(0, 1)
            gates(1, 0)
            act.wait_ge(N["sq_ready"], 4)
            f(inv, inv, ACT.Sqrt, N["sq_done"])
            gates(1, 1)
            for j in range(2, KT):
                for half in range(2):
                    gates(j, half)
                if j == 4:
                    act.wait_ge(N["ya_done"], 1)
                    act.wait_ge(N["mem_in"], 16)
                    rms([(mem_x[:, i, :], P) for i in range(2)], rms_junk)
            act.wait_ge(N["x1_done"], 1)
            rms(stream, rms_junk, 2)
            MS = float(MD) ** -0.5
            nu = len(mem_units)

            def mem_exp(u):
                c, s = 20 + 4 * (u % 3), ms_sb[u % 3]
                act.wait_ge(N["m_neg"], u + 1)
                f(s, s, ACT.Exp, N["m_exp"], bias=stat[:, c + 1:c + 2], scale=MS, accum_out=stat[:, c + 2:c + 3])

            mem_exp(0)
            mem_exp(1)
            for u in range(nu):
                i, h = mem_units[u]
                f(mp_t[u % 2], am.take(act)[:, 0:MEM].rearrange("p (a b) -> p a b", b=P), ACT.Copy, am.freed)
                f(o_t[:, h, i * P:(i + 1) * P], am.take(act)[:, 0:P], ACT.Copy, am.freed)
                if u + 2 < nu:
                    mem_exp(u + 2)
            for b in range(NB):
                for c in range(2):
                    f(mkt_s[b % 2][:, 4 * c:4 * c + 4, :], am.take(act)[:, :].rearrange("p (a b) -> p a b", b=P), ACT.Copy, am.freed)
            mem_exp(nu)
            f(mp_t[0], am.take(act)[:, 0:MEM].rearrange("p (a b) -> p a b", b=P), ACT.Copy, am.freed)
            act.sem_inc(N["mp_turned"], 1)
            rms(stream, y_b, rows_done=N["x2_rows"])
            for i, (t0, n) in enumerate(TILES):
                if i == 0:
                    act.wait_ge(N["lg_clear"], 1)
                f(lg[0:n, i, :], am.take(act)[0:n, 0:36], ACT.Copy, am.freed)
            act.sem_inc(N["lg_in"], 1)
            act.wait_ge(N["route_a"], 1)
            f(r_exp, r_exp, ACT.Exp)
            act.sem_inc(N["route_e"], 1)
            act.wait_ge(N["tab_ready"], 1)
            total = act.value_load(tab_i[0:1, TOTAL:TOTAL + 1], min_val=NE, max_val=ALLBLK)
            with act.Fori(0, total) as n:
                act.wait_ge(N["g_full"], n + 1)
                nc.scalar.activation(h_sg, g_ps, ACT.Silu).then_inc(N["silu_done"], 1)
                act.wait_ge(N["ht_full"], n + 1)
                nc.scalar.activation(h_t, h_ps.rearrange("p (a b) -> p a b", b=BLK), ACT.Copy).then_inc(N["ht_done"], 1)
                act.wait_ge(N["yb_out"], 16 * n + 16)
                act.wait_ge(N["y_ready"], 2 * n + 1)
                nc.scalar.activation(y_b[:, 0:512], d_ps[0], ACT.Copy).then_inc(N["y_taken_a"], 1)
            for i, (t0, n) in enumerate(TILES):
                act.wait_ge(N["x3_done"], i + 1)
                rms(stream[i:i + 1], view(E0 + 3072, D), i)

        @block.vector
        def _(dve):
            line = Line(dve, N["v_step"])
            vm = Mail(*v_mail)
            V = nc.vector

            def tt(out, x, y, op, sem=None):
                line.do(V.tensor_tensor(out, x, y, op), sem)

            def ts(out, x, s1, s2, op0, op1=None, sem=None):
                line.do(V.tensor_scalar(out, x, s1, s2, op0) if op1 is None else V.tensor_scalar(out, x, s1, s2, op0, op1), sem)

            def stt(out, x, s, y, op0, op1, sem=None):
                line.do(V.scalar_tensor_tensor(out=out, in0=x, scalar=s, in1=y, op0=op0, op1=op1), sem)

            def cp(out, x, sem=None):
                line.do(V.tensor_copy(out, x), sem)

            def tell(s):
                dve.sem_inc(s, 1)

            def q4(bank, w=P):
                return bank[:, 0:4 * w].rearrange("p (a b) -> p a b", b=w)

            def last_dim(x, n):
                return x.unsqueeze(len(x.shape)).to_broadcast(list(x.shape) + [n])

            def mid(x, n):
                return x.unsqueeze(1).to_broadcast([x.shape[0], n, x.shape[1]])

            def diagonal(x, first, n, step, w):
                rows = [list(x.ap[0])] + [[step, n], [1, w]]
                return bass.AP(tensor=x.tensor, offset=x.offset + first, ap=rows)

            def rstd(n, col):
                line.do(V.reciprocal(stat[0:n, col:col + 1], stat[0:n, col:col + 1]))

            def rsqrt(x, part):
                tell(N["sq_ready"])
                dve.wait_ge(N["sq_done"], part)
                line.do(V.reciprocal(x, x))
                tell(N["inv_ready"])

            def turned(dst, t0, n, gain):
                for half in range(2):
                    bank = vm.take(dve)
                    tt(dst[:, 4 * half:4 * half + 4, t0:t0 + n], q4(bank)[:, :, 0:n],
                       last_dim(gains[:, gain, 4 * half:4 * half + 4], n), ALU.mult, vm.freed)

            cp(prm[:, 0:NPRM], vm.take(dve)[:, 0:NPRM], vm.freed)
            ts(omka, prm[:, KA:KA + 4], -1.0, 1.0, ALU.mult, ALU.add)
            for i in range(len(TILES) + 1):
                if i < len(TILES):
                    n = TILES[i][1]
                    dve.wait_ge(N["rms"], 1)
                    rstd(n, i)
                    ts(xs_tmp[i % 2][0:n], x_res[0:n, i, :], stat[0:n, i:i + 1], None, ALU.mult)
                    tell(N["xs3_done"])
                if i >= 1:
                    turned(x_t, *TILES[i - 1], 0)
                    tell(N["xt_done"])
            dve.wait_ge(N["qkv_raw"], 1)
            for i in range(2 * len(TILES)):
                if i < len(TILES):
                    n = TILES[i][1]
                    qk = qkv[0:n, i, 0:2 * BW].rearrange("p (h d) -> p h d", d=64)
                    x1, x2 = qk[:, :, 0:8], qk[:, :, 8:16]
                    co = mid(C("rope")[0:n, 16 * i:16 * i + 8], 24)
                    si = mid(C("rope")[0:n, 16 * i + 8:16 * i + 16], 24)
                    tt(rt[0][0:n], x1, co, ALU.mult)
                    tt(rt[1][0:n], x2, si, ALU.mult)
                    tt(rt[2][0:n], x2, co, ALU.mult)
                    tt(rt[3][0:n], x1, si, ALU.mult)
                    tt(x1, rt[0][0:n], rt[1][0:n], ALU.subtract)
                    tt(x2, rt[2][0:n], rt[3][0:n], ALU.add)
                    tell(N["rope_done"])
                else:
                    t0, n = TILES[i - len(TILES)]
                    for half in range(3):
                        cp(qk_t[:, 4 * half:4 * half + 4, t0:t0 + n], q4(vm.take(dve))[:, :, 0:n], vm.freed)

            def mask_unit(u):
                i, h = att[u]
                kb = key_blocks(i)
                s = s_sb[u % 3]
                at_ = 0
                for g in range(NG):
                    k = len([1 for gg, _ in kb if gg == g])
                    bank = vm.take(dve)
                    if k > 1:
                        tt(s[:, at_:at_ + (k - 1) * P].rearrange("p (a b) -> p a b", b=P),
                           bank[:, 0:(k - 1) * P].rearrange("p (a b) -> p a b", b=P), mid(C(f"off{g}"), k - 1), ALU.add)
                    tt(s[:, at_ + (k - 1) * P:at_ + k * P], bank[:, (k - 1) * P:k * P], C(f"diag{g}"), ALU.add, vm.freed)
                    at_ += k * P
                c = 8 + 4 * (u % 3)
                line.do(V.reduce_max(stat[:, c:c + 1], s[:, 0:at_], AX))
                ts(stat[:, c + 1:c + 2], stat[:, c:c + 1], -0.125, None, ALU.mult, sem=N["p_neg"])

            def scale_unit(u):
                i, h = att[u]
                n = P * len(key_blocks(i))
                c = 8 + 4 * (u % 3)
                dve.wait_ge(N["p_exp"], u + 1)
                line.do(V.reciprocal(stat[:, c + 3:c + 4], stat[:, c + 2:c + 3]))
                ts(s_sb[u % 3][:, 0:n], s_sb[u % 3][:, 0:n], stat[:, c + 3:c + 4], None, ALU.mult, sem=N["p_ready"])

            mask_unit(0)
            mask_unit(1)
            for u in range(len(att)):
                scale_unit(u)
                if u + 2 < len(att):
                    mask_unit(u + 2)
            dve.wait_ge(N["pv_taken"], len(att))
            line.do(V.memset(q_new, 0.0))
            for h in range(4):
                hp, lo = h // 2, 64 * (h % 2)
                cp(q_new[lo:lo + 64, hp:2 * NG:2, TS * h:TS * h + TS], qk_t[lo:lo + 64, hp:2 * NG:2, SEQ:T])
            tell(N["q_new_ready"])
            dve.wait_ge(N["q_own_clear"], 1)
            for g in range(NG):
                for h in range(4):
                    hp, lo = h // 2, 64 * (h % 2)
                    own = diagonal(q_own[lo:lo + 64, 2 * g + hp].rearrange("p b c -> p (b c)"), TS * h, NB, P + NS, NS)
                    cp(own, qk_t[lo:lo + 64, 2 * g + hp, SEQ:T].rearrange("p (b t) -> p b t", t=NS))
                tell(N["q_own_ready"])
            tt(ps_sb[:, NG * P:480], vm.take(dve)[:, 0:NG * TS], C("samp")[:, NG * P:480], ALU.add, vm.freed)
            line.do(V.memset(view(AR + 5 * BPROJ, (NB + TS) * P), 0.0))
            tt(ps_sb[:, 0:P], vm.take(dve)[:, 0:P], C("samp")[:, 0:P], ALU.add, vm.freed)
            for g in range(1, NG):
                tt(own_tmp, vm.take(dve)[:, :].rearrange("p (t k) -> p t k", k=P), last_dim(C("pick"), P), ALU.mult, vm.freed)
                line.do(V.reduce_sum(ps_sb[:, g * P:(g + 1) * P], own_tmp.rearrange("p t k -> p k t"), AX))
            line.do(V.reduce_max(stat[:, 16:17], ps_sb, AX))
            ts(stat[:, 17:18], stat[:, 16:17], -0.125, None, ALU.mult, sem=N["sneg"])
            dve.wait_ge(N["sexp"], 1)
            line.do(V.reciprocal(stat[:, 19:20], stat[:, 18:19]))
            ts(ps_sb, ps_sb, stat[:, 19:20], None, ALU.mult, sem=N["s_soft"])
            cp(pts, vm.take(dve)[:, 0:NG * P].rearrange("p (a b) -> p a b", b=P), vm.freed)
            cp(ptn[0:TS], vm.take(dve)[0:TS, 0:NG * P].rearrange("p (a b) -> p a b", b=P), vm.freed)
            for g in range(NG):
                if g == 2:
                    dve.wait_ge(N["kv_used"], len(units) + 2 * NB)
                for h in range(4):
                    pr = pts[:, g, TS * h:TS * h + TS]
                    if g == 0:
                        cp(diagonal(p_own0.rearrange("p b c -> p (b c)"), TS * h, NB, P + NS, NS), pr.rearrange("p (b t) -> p b t", t=NS))
                    else:
                        cp(diagonal(p_own.rearrange("p b c -> p (b c)"), TS * h, TS, P + 1, 1), pr.unsqueeze(2))
                tell(N["p_own_ready"])
            dve.wait_ge(N["kv_used"], 2 * len(units))
            for h in range(4):
                cp(y_own[TS * h:TS * h + TS], aux[TS * h:TS * h + TS, 64 * h:64 * h + 64])
            tell(N["y_own_ready"])
            bank = vm.take(dve)
            for lo in (0, 64):
                cp(yb_t[lo:lo + 64, :, SEQ:T], bank[lo:lo + 64, 0:P].rearrange("p (a b c) -> p a b c", b=2, c=TS)[:, :, lo // 64, :],
                   vm.freed if lo else None)
            tell(N["yb_done"])
            us4 = u_s.rearrange("p j (b t) -> p j b t", t=NS)
            ums4 = um_s.rearrange("p j (b t) -> p j b t", t=NS)
            dve.wait_ge(N["out"], 16 * OUT_CACHES)
            for c in range(0, AJ, 4):
                k = min(4, AJ - c)
                cp(ums4[:, c:c + k, :, 0], vm.take(dve)[:, 0:k * NB].rearrange("p (a b) -> p a b", b=NB), vm.freed)
            seen = 0
            decay_rate = -float(np.exp(np.float32(-0.5)))

            def shift(js):
                nonlocal seen
                for j in js:
                    seen += 1
                    dve.wait_ge(N["u_raw"], seen)
                    ts(um_p[:, j, 0:1], u_p[:, j, 0:1], -1.0, None, ALU.mult)
                    tt(um_p[:, j, 1:SEQ], u_p[:, j, 0:SEQ - 1], u_p[:, j, 1:SEQ], ALU.subtract)
                    stt(um_p[:, j, :], um_p[:, j, :], prm[:, MU + j:MU + j + 1], u_p[:, j, :], ALU.mult, ALU.add)
                    cp(u_last[:, j:j + 1], u_p[:, j, SEQ - 1:SEQ])

            def norm_k(kk, k, aa, tmp, r, n, part):
                ts(inv[:, 0:n], vm.take(dve)[:, 0:n], 1e-24, None, ALU.max, sem=vm.freed)
                rsqrt(inv[:, 0:n], part)
                dve.wait_ge(N["sga"], part)
                for j in range(4):
                    ts(tmp[:, j], aa[:, j], prm[:, KA + j:KA + j + 1], omka[:, j:j + 1], ALU.mult, ALU.add)
                tt(k, k, tmp, ALU.mult)
                for j in range(4):
                    tt(kk[:, j], kk[:, j], vm.take(dve)[:, 0:n], ALU.mult, vm.freed)
                tt(aa, aa, kk, ALU.mult)
                tt(tmp, r, k, ALU.mult)
                tt(tmp, tmp, last_dim(prm[:, RK:RK + 4], n), ALU.mult, N["prep_sq"])

            c_all, sg_all = c_p.rearrange("p a b -> p (a b)"), sg_p.rearrange("p a b -> p (a b)")
            r, k, v = um_p[:, 0:4], um_p[:, 4:8], um_p[:, 8:12]
            shift(feats[0])
            tell(N["um_done"])
            shift(feats[1])
            tt(kk_p, k, last_dim(prm[:, KK_:KK_ + 4], SEQ), ALU.mult)
            tt(sq_p, kk_p, kk_p, ALU.mult, N["prep_sq"])
            dve.wait_ge(N["sga"], 1)
            ts(sg_p, sg_p, decay_rate, None, ALU.mult)
            for z in range(4 * NPT):
                chunk = slice(z * P, (z + 1) * P)
                line.do(V.tensor_tensor_scan(c_all[:, chunk], C("ones"), sg_all[:, chunk], 0.0, ALU.mult, ALU.add))
            c16 = c_p.rearrange("p j (i t) -> p (j i) t", t=P)
            pm16 = pmid.rearrange("p a b -> p (a b)")
            cp(pm16, c16[:, :, P // 2 - 1])
            tt(c16, c16, last_dim(pm16, P), ALU.subtract)
            tt(sg_p, c_p, sg_p, ALU.subtract)
            shift(feats[2])
            tell(N["prep_e"])
            norm_k(kk_p, k, a_p, sq_p, r, SEQ, 1)
            dve.wait_ge(N["exp_done"], 1)
            tt(r, r, tmp_p, ALU.mult)
            cp(pend.rearrange("p a b -> p (a b)"), tmp_p.rearrange("p j (i t) -> p (j i) t", t=P)[:, :, P - 1])
            stt(kk_p.rearrange("p a b -> p (a b)"), kk_p.rearrange("p a b -> p (a b)"), -1.0, sg_p.rearrange("p a b -> p (a b)"), ALU.mult, ALU.mult)
            tt(k, k, c_p, ALU.mult)
            tt(a_p, a_p, c_p, ALU.mult)
            tell(N["prep_done"])
            shift(feats[3])
            tt(ums4[:, :, :, 0], ums4[:, :, :, 0], us4[:, :, :, 0], ALU.subtract)
            tt(ums4[:, :, :, 1:NS], us4[:, :, :, 0:NS - 1], us4[:, :, :, 1:NS], ALU.subtract)
            tt(um_s, um_s, last_dim(prm[:, MU:MU + AJ], TS), ALU.mult)
            tt(um_s, um_s, u_s, ALU.add)
            tell(N["um_done"])
            for j in range(4):
                tt(bon_p[:, j], vm.take(dve)[:, :], v[:, j], ALU.mult, vm.freed)
            rs_, ks_, vs_ = um_s[:, 0:4], um_s[:, 4:8], um_s[:, 8:12]
            tt(kk_s, ks_, last_dim(prm[:, KK_:KK_ + 4], TS), ALU.mult)
            tt(tmp_s, kk_s, kk_s, ALU.mult, N["prep_sq"])
            for i in range(NPT):
                cp(tm_b[:, i, :], vm.take(dve)[:, :], vm.freed)
            norm_k(kk_s, ks_, a_s, tmp_s, rs_, TS, 2)
            for i in range(NPT):
                cp(tm_k[:, i, :], vm.take(dve)[:, :], vm.freed)
            for j in range(4):
                tt(bon_s[:, j], vm.take(dve)[:, 0:TS], vs_[:, j], ALU.mult, vm.freed)
            dve.wait_ge(N["exp_done"], 2)
            tell(N["tm_done"])
            for i in range(NPT):
                cp(tm_v[:, i, :], vm.take(dve)[:, :], vm.freed)
            for c in range(0, AJ, 4):
                w = P * min(4, AJ - c)
                cp(last_s[0:NB, c * P:c * P + w], vm.take(dve)[0:NB, 0:w], vm.freed)
            cp(last_p, vm.take(dve)[64:64 + AJ, 0:P], vm.freed)
            tell(N["shift_ready"])
            for z in range(6):
                cp(tok_s[0:TS, z, :], vm.take(dve)[0:TS, :], vm.freed)
            tell(N["stm_done"])
            dve.wait_ge(N["shift_out"], 32)
            line.do(V.memset(st0, 0.0))
            line.do(V.memset(st0m, 0.0))
            for i in range(NPT):
                for dst, mask, plus in ((mat_t, "low1t", 1), (mat_ak, "strict", 0), (mat_rb, "incl", 0), (mat_rk, "incl", 0)):
                    for par in range(2):
                        bank = vm.take(dve)
                        d4 = dst[:, 4 * par:4 * par + 4, :]
                        tt(d4, q4(bank), mid(C(mask), 4), ALU.mult, vm.freed)
                        if plus:
                            tt(d4, d4, mid(ident, 4), ALU.add)
                dve.wait_ge(N["l_ready"], i + 1)
                tt(mat_tt, mat_l, mid(C("low1"), 8), ALU.mult)
                tt(mat_tt, mat_tt, mid(ident, 8), ALU.add)
                tt(mat_lm, mat_l, mid(C("low2"), 8), ALU.mult, N["lm_ready"])
                for lv, m in enumerate(LEVELS[1:]):
                    final = m == LEVELS[-1]
                    dve.wait_ge(N["lt_taken"], len(LEVELS[1:]) * i + lv + 1)
                    if not final:
                        tt(mat_lm, mat_l, mid(C(f"low{2 * m}"), 8), ALU.mult, N["lm_ready"])
                    for par in range(2):
                        for dst in ((mat_t, mat_tt) if not final else (mat_tt,)):
                            d4 = dst[:, 4 * par:4 * par + 4, :]
                            tt(d4, d4, q4(vm.take(dve)), ALU.add, vm.freed)
                for par in range(2):
                    cp(w_sb[:, 4 * par:4 * par + 4, :], q4(vm.take(dve), 64), vm.freed)
                cp(uu_sb, vm.take(dve)[:, :].rearrange("p (a b) -> p a b", b=64), vm.freed)
                tt(st0, st0m, q4(vm.take(dve), 64), ALU.add, vm.freed)
                tt(st0, st0, last_dim(pend[:, :, i], 64), ALU.mult)
                dve.wait_ge(N["mats"], i + 1)
                if i + 1 < NPT:
                    tt(st0m, st0, last_dim(pmid[:, :, i + 1], 64), ALU.mult)
                tell(N["state_ready"])
            cp(fin_s[0:64], vm.take(dve)[0:64, :], vm.freed)
            tell(N["fin_ready"])
            cp(y_s, vm.take(dve)[:, 0:4 * TS].rearrange("p (a b) -> p a b", b=TS), vm.freed)
            dve.wait_ge(N["y_raw"], 1)
            for part in range(2):
                n = TS if part == 0 else SEQ
                y, tmp, bon, gg = (y_s, tmp_s, bon_s, g_s) if part == 0 else (a_p, tmp_p, bon_p, g_p)
                tell(N["ysq"])
                for j in range(4):
                    stt(y[:, j], vm.take(dve)[:, 0:n], -1.0 / AD, y[:, j], ALU.mult, ALU.add, vm.freed)
                tt(tmp, y, y, ALU.mult)
                tell(N["ysq"])
                ts(inv[:, 0:n], vm.take(dve)[:, 0:n], 1.0 / AD, LNX_EPS, ALU.mult, ALU.add, sem=vm.freed)
                rsqrt(inv[:, 0:n], part + 3)
                for j in range(4):
                    tt(y[:, j], y[:, j], vm.take(dve)[:, 0:n], ALU.mult, vm.freed)
                    ts(y[:, j], y[:, j], prm[:, LG + j:LG + j + 1], prm[:, LB + j:LB + j + 1], ALU.mult, ALU.add)
                tt(y, y, bon, ALU.add)
                tt(y_all[:, :, SEQ:T] if part == 0 else y_all[:, :, 0:SEQ], y, gg, ALU.mult)
                if part == 0:
                    tell(N["ring_spare"])
            tell(N["ya_done"])
            def norm_rows(srcs, col0, count):
                for i, (x, t0, n) in enumerate(srcs, col0):
                    dve.wait_ge(N["rms"], count)
                    rstd(n, i)
                    ts(xs2[i % 2][0:n], x, stat[0:n, i:i + 1], None, ALU.mult)
                    tell(N["memx"])

            def turn_normed(srcs, gain, dst):
                for x, t0, n in srcs:
                    turned(dst, t0, n, gain)

            z = 0
            for j in range(KT):
                for t0, n in HALVES:
                    dve.wait_ge(N["sig_done"], z + 1)
                    tt(mg[:, 0:n], vm.take(dve)[:, 0:n], gate_sb[j % 3][:, 0, t0:t0 + n], ALU.mult, vm.freed)
                    tt(m_t[:, j, t0:t0 + n], vm.take(dve)[:, 0:n], gate_sb[j % 3][:, 1, t0:t0 + n], ALU.mult, vm.freed)
                    tt(m_t[:, j, t0:t0 + n], m_t[:, j, t0:t0 + n], mg[:, 0:n], ALU.add, N["gate_used"])
                    z += 1
                if j == 5:
                    mem_rows = [(mem_x[:, i, :], i * P, P) for i in range(2)]
                    norm_rows(mem_rows, 0, 2)
            tell(N["merged"])
            turn_normed(mem_rows, 2, mem_t)

            def add_rows(done=None):
                for c in range(2):
                    for i, (t0, m) in enumerate(TILES):
                        x = x_res[0:m, i, c * 512:(c + 1) * 512]
                        tt(x, x, vm.take(dve)[0:m, :], ALU.add, vm.freed)
                        if done and c == 1:
                            tell(done)

            add_rows()
            tell(N["x1_done"])
            for c in range(2):
                for i in range(2):
                    cp(mkv[:, i, c * 512:(c + 1) * 512], vm.take(dve)[:, :], vm.freed)
            tell(N["mkv_done"])
            for i in range(2):
                cp(mk_t[:, :, i * P:(i + 1) * P], q4(vm.take(dve)), vm.freed)
            rows = [(x_res[0:n, i, :], t0, n) for i, (t0, n) in enumerate(TILES)]
            norm_rows(rows[0:2], 2, 3)
            for i in range(len(rows)):
                turn_normed(rows[i:i + 1], 1, x_t)
                if i + 2 < len(rows):
                    norm_rows(rows[i + 2:i + 3], 4 + i, 3)
            line.do(V.memset(mq_own, 0.0))
            line.do(V.memset(mp_own, 0.0))
            for h in range(MH):
                for t0, n in HALVES:
                    cp(q_t[:, h, t0:t0 + n], vm.take(dve)[:, 0:n], vm.freed)
                cp(diagonal(mq_own[:, h].rearrange("p b c -> p (b c)"), TS * h, NB, P + NS, NS),
                   q_t[:, h, SEQ:T].rearrange("p (b t) -> p b t", t=NS))
            tell(N["mq_ready"])
            MS = float(MD) ** -0.5
            nu = len(mem_units)

            def mem_mask(u):
                c = 20 + 4 * (u % 3)
                cp(ms_sb[u % 3], vm.take(dve)[:, 0:MEM], vm.freed)
                line.do(V.reduce_max(stat[:, c:c + 1], ms_sb[u % 3], AX))
                ts(stat[:, c + 1:c + 2], stat[:, c:c + 1], -MS, None, ALU.mult, sem=N["m_neg"])

            def mem_scale(u):
                c = 20 + 4 * (u % 3)
                dve.wait_ge(N["m_exp"], u + 1)
                line.do(V.reciprocal(stat[:, c + 3:c + 4], stat[:, c + 2:c + 3]))
                ts(ms_sb[u % 3], ms_sb[u % 3], stat[:, c + 3:c + 4], None, ALU.mult, sem=N["m_ready"])

            mem_mask(0)
            mem_mask(1)
            for u in range(nu):
                mem_scale(u)
                if u + 2 < nu:
                    mem_mask(u + 2)
            mem_mask(nu)
            mem_scale(nu)
            dve.wait_ge(N["mp_turned"], 1)
            for c in range(2):
                for h in range(MH):
                    cp(diagonal(mp_own[:, c].rearrange("p b c -> p (b c)"), TS * h, NB, P + NS, NS),
                       mp_t[0][:, c, TS * h:TS * h + TS].rearrange("p (b t) -> p b t", t=NS))
            tell(N["mp_ready"])
            dve.wait_ge(N["mkv_used"], 2 * NB)
            for h in range(MH):
                cp(mo_own[TS * h:TS * h + TS], aux[TS * h:TS * h + TS, P * h:P * h + P])
            tell(N["mo_ready"])
            cp(o_t[:, :, SEQ:T], vm.take(dve)[:, 0:P].rearrange("p (a b) -> p a b", b=TS), vm.freed)
            tell(N["mo_done"])
            add_rows(N["x2_rows"])
            tell(N["x2_done"])
            for i, (t0, n) in enumerate(TILES):
                dve.wait_ge(N["rms"], 4)
                rstd(n, i)
                if i == 0:
                    dve.wait_ge(N["mkv_out"], 32)
                ts(xs3[0:n, i, :], x_res[0:n, i, :], stat[0:n, i:i + 1], None, ALU.mult)
                tell(N["xs3_done"])
            line.do(V.memset(lg[:, len(TILES) - 1, :], 0.0))
            line.do(V.memset(r_grp, 2 * NEG))
            tell(N["lg_clear"])
            for t0, n in TILES:
                turned(x_t, t0, n, 3)
            dve.wait_ge(N["rb_in"], 32)
            dve.wait_ge(N["lg_in"], 1)
            nt = len(TILES)
            tt(lg, lg, mid(rbias, nt), ALU.add)
            cp(r_grp[:, :, 0:4], lg[:, :, 0:4])
            for i in range(nt):
                V.max(r_max[:, i, :], r_grp[:, i, :]).then_inc(N["v_many"], 1)
            dve.wait_ge(N["v_many"], nt)
            for i in range(nt):
                V.max_index(r_idx[:, i, :], r_max[:, i, :], r_grp[:, i, :]).then_inc(N["v_many"], 1)
            dve.wait_ge(N["v_many"], 2 * nt)
            cp(r_num[:, :, 0:1], r_idx[:, :, 0:1])
            tt(r_exp[:, :, 0:4], lg[:, :, 0:4], r_max[:, :, 0:1].to_broadcast([P, nt, 4]), ALU.subtract)
            tt(r_in, mid(C("grp"), nt), r_num[:, :, 0:1].to_broadcast([P, nt, NE]), ALU.is_equal)
            ts(r_off, r_in, -NEG, NEG, ALU.mult, ALU.add)
            tt(r_in, lg[:, :, 4:36], r_in, ALU.mult)
            tt(r_in, r_in, r_off, ALU.add)
            for i in range(nt):
                V.max(r_max[:, i, :], r_in[:, i, :]).then_inc(N["v_many"], 1)
            dve.wait_ge(N["v_many"], 3 * nt)
            for i in range(nt):
                V.max_index(r_idx[:, i, :], r_max[:, i, :], r_in[:, i, :]).then_inc(N["v_many"], 1)
            dve.wait_ge(N["v_many"], 4 * nt)
            tt(r_exp[:, :, 4:5], r_max[:, :, 1:2], r_max[:, :, 0:1], ALU.subtract)
            tell(N["route_a"])
            cp(r_num, r_idx[:, :, 0:2])
            for k in range(2):
                tt(hot[:, :, NE * k:NE * k + NE], mid(C("iota"), nt), r_num[:, :, k:k + 1].to_broadcast([P, nt, NE]), ALU.is_equal)
            tell(N["hot_done"])
            dve.wait_ge(N["route_e"], 1)
            line.do(V.reduce_sum(r_sum, r_exp[:, :, 0:4], AX))
            ts(r_two, r_exp[:, :, 4:5].rearrange("p a b -> p (a b)"), 1.0, None, ALU.add)
            tt(r_two, r_two, r_sum, ALU.mult)
            line.do(V.reciprocal(gate[:, :, 0], r_two))
            tt(gate[:, :, 1:2], gate[:, :, 0:1], r_exp[:, :, 4:5], ALU.mult)
            bank = vm.take(dve)
            cnt, base, nblk = rs[:, 0:32], rs[:, 32:64], rs[:, 64:96]
            cp(cnt, bank[:, 0:NE])
            tt(cnt, cnt, bank[:, NE:2 * NE], ALU.add, vm.freed)
            one = C("ones")[:, 0:NE]
            line.do(V.tensor_tensor_scan(base, one, cnt, 0.0, ALU.mult, ALU.add))
            tt(base, base, cnt, ALU.subtract)
            tt(cnt3, last_dim(cnt, MAXBLK - 1), mid(C("thr"), NE), ALU.is_gt)
            line.do(V.reduce_sum(nblk, cnt3, AX))
            ts(nblk, nblk, 1.0, None, ALU.add)
            first_ = rs[:, 96:128]
            line.do(V.tensor_tensor_scan(first_, one, nblk, 0.0, ALU.mult, ALU.add))
            cp(tab_i[:, TOTAL:TOTAL + 1], first_[:, NE - 1:NE])
            tt(first_, first_, nblk, ALU.subtract)
            cp(tab_i[:, FIRST:FIRST + NE], first_)
            cp(tab_i[:, COUNT:COUNT + NE], nblk)
            tt(row3, mid(first_, NTAB), last_dim(C("count"), NE), ALU.is_gt)
            stt(nblk, first_, -float(BLK), base, ALU.mult, ALU.add)
            stt(row3, row3, 1e6, mid(nblk, NTAB), ALU.mult, ALU.add)
            line.do(V.tensor_reduce(rs[:, 128:128 + NTAB], row3, AX, ALU.min))
            stt(rs[:, 128:128 + NTAB], C("count"), float(BLK), rs[:, 128:128 + NTAB], ALU.mult, ALU.add)
            ts(tab_i[:, ROW:ROW + NTAB], rs[:, 128:128 + NTAB], float(ROWS), None, ALU.min)
            tell(N["tab_ready"])
            for i, (t0, n) in enumerate(TILES):
                z = slice(0, n)
                bank = vm.take(dve)
                tt(rs[z, 128:160], bank[z, 0:NE], base[z], ALU.add)
                tt(rs[z, 128:160], rs[z, 128:160], bank[z, NE:2 * NE], ALU.add, vm.freed)
                for k in range(2):
                    tt(rs[z, 160:192], rs[z, 128:160], hot[z, i, NE * k:NE * k + NE], ALU.mult)
                    line.do(V.reduce_sum(slot_f[z, 2 * i + k:2 * i + k + 1], rs[z, 160:192], AX))
                cp(slot_i[z, 2 * i:2 * i + 2], slot_f[z, 2 * i:2 * i + 2])
                tell(N["route_done"])
            def take_block():
                for half in range(2):
                    k = slice(4 * half, 4 * half + 4)
                    last = V.tensor_tensor(x_e[:, k, :], x_ps[half].rearrange("p (a b) -> p a b", b=BLK), last_dim(gains[:, 3, k], BLK), ALU.mult)
                last.then_inc(N["xe_ready"], 1)

            dve.wait_ge(N["scattered"], 16 * 2 * len(TILES))
            dve.wait_ge(N["xb_used"], 1)
            take_block()
            total = dve.value_load(tab_i[0:1, TOTAL:TOTAL + 1], min_val=NE, max_val=ALLBLK)
            with dve.Fori(0, total) as n:
                dve.wait_ge(N["silu_done"], n + 1)
                dve.wait_ge(N["u_full"], n + 1)
                V.tensor_tensor(h_b, h_sg, u_ps, ALU.mult).then_inc(N["h_done"], 1)
                dve.wait_ge(N["xb_used"], n + 2)
                take_block()
                dve.wait_ge(N["yb_out"], 16 * n + 16)
                dve.wait_ge(N["y_ready"], 2 * n + 2)
                V.tensor_copy(y_b[:, 512:1024], d_ps[1]).then_inc(N["y_taken_v"], 1)
            def final_norm(i):
                n = TILES[i][1]
                dve.wait_ge(N["rms"], 5 + i)
                rstd(n, i)
                stt(x_res[0:n, i, :], x_res[0:n, i, :], stat[0:n, i:i + 1], gfin[0:n], ALU.mult, ALU.mult)
                tell(N["y_final"])

            dve.wait_ge(N["gfin_in"], 16)
            for i, (t0, n) in enumerate(TILES):
                dve.wait_ge(yg_in[i], 32)
                for k in range(2):
                    stt(x_res[0:n, i, :], yg[2 * i + k][0:n], gate[0:n, i, k:k + 1], x_res[0:n, i, :], ALU.mult, ALU.add)
                tell(N["x3_done"])
                if i >= 1:
                    final_norm(i - 1)
            final_norm(len(TILES) - 1)

        @block.gpsimd
        def _(pool):
            line = Line(pool, N["pool_step"])
            G = nc.gpsimd

            def tt(out, x, y, op):
                line.do(G.tensor_tensor(out, x, y, op))

            pool.wait_ge(N["ring_used"], NA - 1)
            copied = 0

            def carry_rows(g, b):
                nonlocal copied
                window = GROUPS[g][0]
                src = caches[g][b, :, NS:window].rearrange("k (r q) h d -> k r (q h d)", q=NS)
                dst = o[f"s_cache{g}"][b, :, 0:window - NS].rearrange("k (r q) h d -> k r (q h d)", q=NS)
                if copied:
                    pool.wait_ge(N["copies"], 16 * copied)
                pool.dma_start(dst, src).then_inc(N["copies"], 16)
                copied += 1

            for b in range(NB // 2):
                for g in range(NG):
                    carry_rows(g, b)
            pool.wait_ge(N["ring_used"], NA)
            line.do(G.memset(q_own, 0.0))
            pool.sem_inc(N["q_own_clear"], 1)
            pool.wait_ge(N["shift_ready"], 1)
            pool.dma_start(o["s_shift"][:, :], last_s[0:NB, :]).then_inc(N["shift_out"], 16)
            pool.dma_start(o["p_shift"][0].rearrange("(j p) -> j p", p=P), last_p).then_inc(N["shift_out"], 16)
            pool.wait_ge(N["srec_in"], 16 * 2 * (6 * NB + 1))
            line.do(G.memset(rec_sa[:, 0, :], 0.0))
            for t in range(NS):
                def vec(n):
                    return rec[:, n, t * 64:(t + 1) * 64].unsqueeze(1).to_broadcast([P, 32, 64])

                def val(x):
                    return x.unsqueeze(2).to_broadcast([P, 32, 64])

                def row_sums(dst, src):
                    w = 32
                    while w >= 1:
                        last = dst.unsqueeze(2) if w == 1 else src[:, :, 0:w]
                        tt(last, src[:, :, 0:w], src[:, :, w:2 * w], ALU.add)
                        w //= 2

                tt(rec_t, rec_s, vec(2), ALU.mult)
                row_sums(rec_sa[:, 0, :], rec_t)
                tt(rec_s, rec_s, vec(4), ALU.mult)
                tt(rec_t, val(rec_sa[:, 0, :]), vec(3), ALU.mult)
                tt(rec_s, rec_s, rec_t, ALU.subtract)
                tt(rec_t, val(rec_v[:, t, :]), vec(1), ALU.mult)
                tt(rec_s, rec_s, rec_t, ALU.add)
                tt(rec_t, rec_s, vec(0), ALU.mult)
                row_sums(rec_y[:, t, :], rec_t)
            for hf in range(2):
                rows = slice(hf * 64, (hf + 1) * 64)
                dst = o["s_rwkv"].rearrange("b h (f v) k -> (b h) f (v k)", f=2)[:, hf]
                pool.dma_start(dst, rec_s[rows].rearrange("p v k -> p (v k)")).then_inc(N["state_out"], 16)
                for b in range(NB):
                    r8 = slice(hf * 64 + b * AH, hf * 64 + (b + 1) * AH)
                    dst = yrec_d[b * NS:(b + 1) * NS, :].rearrange("t (h f k) -> h f t k", h=AH, f=2)[:, hf]
                    pool.dma_start(dst, rec_y[r8]).then_inc(N["yrec_out"], 16)
            pool.wait_ge(N["yrec_out"], 16 * 2 * NB)
            pool.dma_start(y_tok[0:TS, :], yrec_d[:, :]).then_inc(N["yrec_in"], 16)
            for b in range(NB // 2, NB):
                for g in range(NG):
                    carry_rows(g, b)
            pool.wait_ge(N["state_out"], 32)
            pool.wait_ge(N["fin_ready"], 1)
            pool.dma_start(o["p_rwkv"][0].rearrange("h v k -> v h k"), fin_s[0:64].rearrange("p (h k) -> p h k", k=64))\
                .then_inc(N["state_out"], 16)
            pool.wait_ge(N["mkv_done"], 1)
            for i in range(2):
                pool.dma_start(o["p_mem"][0, :, i * P:(i + 1) * P].rearrange("k p h d -> p k (h d)"),
                               mkv[:, i, :].rearrange("p (k c) -> p k c", k=2)).then_inc(N["mkv_out"], 16)
            pool.wait_ge(N["x2_done"], 1)
            line.do(G.memset(xb, 0.0))
            pool.dma_start(xs_d[ROWS:ROWS + BLK, :], xb).then_inc(N["pad_out"], 16)
            pool.dma_start(ys_d[ROWS:ROWS + BLK, :], xb).then_inc(N["yb_out"], 16)
            pool.dma_start(rbias[:, 0:4], a["b_router_group"].partition_broadcast(P)).then_inc(N["rb_in"], 16)
            pool.dma_start(rbias[:, 4:36], a["b_router_expert"].partition_broadcast(P)).then_inc(N["rb_in"], 16)
            for i, (t0, n) in enumerate(TILES):
                pool.wait_ge(N["route_done"], i + 1)
                for k in range(2):
                    pool.indirect_dma_start(out=xs_d[0:ROWS, :], out_offset=bass.IndirectOffsetOnAxis(ap=slot_i[0:n, 2 * i + k:2 * i + k + 1], axis=0),
                                            in_=xs3[0:n, i, :], in_offset=None, bounds_check=ROWS - 1).then_inc(N["scattered"], 16)
            pool.wait_ge(N["scattered"], 16 * 2 * len(TILES))
            pool.wait_ge(N["pad_out"], 16)
            pool.wait_ge(N["yb_out"], 16)
            row0 = pool.value_load(tab_of(ROW, 0), min_val=0, max_val=ROWS)
            pool.dma_start(xb, xs_d[bass.ds(row0, BLK), :]).then_inc(N["xb_in"], 16)
            total = pool.value_load(tab_i[0:1, TOTAL:TOTAL + 1], min_val=NE, max_val=ALLBLK)
            with pool.Fori(0, total) as n:
                row = pool.value_load(tab_of(ROW, n), min_val=0, max_val=ROWS)
                ahead = pool.value_load(tab_of(ROW, n + 1), min_val=0, max_val=ROWS)
                pool.wait_ge(N["xb_used"], n + 1)
                pool.sem_inc(N["seen"], 1)
                pool.dma_start(xb, xs_d[bass.ds(ahead, BLK), :]).then_inc(N["xb_in"], 16)
                pool.wait_ge(N["y_taken_a"], n + 1)
                pool.wait_ge(N["y_taken_v"], n + 1)
                pool.wait_ge(N["yb_out"], 16 * n + 16)
                pool.sem_inc(N["seen"], 1)
                pool.dma_start(ys_d[bass.ds(row, BLK), :], y_b).then_inc(N["yb_out"], 16)
            pool.wait_ge(N["yb_out"], 16 * total + 16)
            pool.sem_inc(N["seen"], 1)
            pool.dma_start(gfin, a["norm_final_g"].partition_broadcast(P)).then_inc(N["gfin_in"], 16)
            for i, (t0, n) in enumerate(TILES):
                for k in range(2):
                    pool.indirect_dma_start(out=yg[2 * i + k][0:n], out_offset=None, in_=ys_d[0:ROWS, :],
                                            in_offset=bass.IndirectOffsetOnAxis(ap=slot_i[0:n, 2 * i + k:2 * i + k + 1], axis=0),
                                            bounds_check=ROWS - 1).then_inc(yg_in[i], 16)
            pool.wait_ge(N["copies"], 16 * NG * NB)
            pool.wait_ge(N["shift_out"], 32)
            pool.wait_ge(N["state_out"], 48)
            pool.wait_ge(N["mkv_out"], 32)


_INS = ['x_prompt', 'x_sample', 'state_rwkv', 'state_shift', 'cache_swa_w128', 'cache_swa_w512', 'cache_swa_w2048',
        'cache_mem_kv', 'mem_prompt', 'norm_mix_g', 'w_in', 'b_gate', 'rwkv_mu', 'rwkv_w0', 'rwkv_w2', 'rwkv_a0', 'rwkv_a2',
        'rwkv_g2', 'rwkv_k_k', 'rwkv_k_a', 'rwkv_r_k', 'rwkv_lnx_g', 'rwkv_lnx_b', 'w_branch_a', 'w_branch_b', 'w_out',
        'norm_mem_g', 'norm_memkv_g', 'w_mem_q', 'w_mem_kv', 'w_mem_out', 'norm_ffn_g', 'w_router_group', 'b_router_group',
        'w_router_expert', 'b_router_expert', 'w_exp_gate', 'w_exp_up', 'w_exp_down', 'norm_final_g']
_OUTS = [('y_prompt', (1, SEQ, D)), ('y_sample', (NB, NS, D)), ('p_rwkv', (1, AH, AD, AD)), ('p_shift', (1, APROJ)),
         ('p_cache0', (1, 2, 128, 4, 64)), ('p_cache1', (1, 2, 512, 4, 64)), ('p_cache2', (1, 2, 512, 4, 64)),
         ('p_mem', (1, 2, MEM, MH, MD)), ('s_rwkv', (NB, AH, AD, AD)), ('s_shift', (NB, APROJ)),
         ('s_cache0', (NB, 2, 128, 4, 64)), ('s_cache1', (NB, 2, 512, 4, 64)), ('s_cache2', (NB, 2, 2048, 4, 64))]


def kernel(**inputs):
    import concourse.bacc as _bacc
    from concourse.bass_utils import run_bass_kernel_spmd as _run

    nc = _bacc.Bacc("TRN2", target_bir_lowering=False, num_devices=1)
    arrays, ins, outs = {}, {}, {}
    for name in _INS:
        x = np.ascontiguousarray(inputs[name])
        arrays[f"in_{name}"] = x
        ins[name] = nc.dram_tensor(f"in_{name}", x.shape, mybir.dt.from_np(x.dtype), kind="ExternalInput").ap()
    table = np.concatenate(list(constants().values()), axis=1)
    arrays["constants"] = table
    cst = nc.dram_tensor("constants", table.shape, F32, kind="ExternalInput").ap()
    for name, shape in _OUTS:
        outs[name] = nc.dram_tensor(f"out_{name}", shape, F32, kind="ExternalOutput").ap()
    build(nc, ins, outs, cst)
    r = _run(nc, [arrays], core_ids=[0])
    return tuple(r.results[0][f"out_{name}"] for name, _ in _OUTS)
```
